# Optimizing a Trainium2 kernel written in Bass

```python
import jax, jax.numpy as jnp
from jax import lax
import numpy as np

D_MODEL = 1024
BATCH = 1
SEQ = 512
DEPTH = 1

MIX_WIDTH = D_MODEL
HGRN_WIDTH = MIX_WIDTH // 2
HGRN_HEADS = 4
HGRN_HEAD_DIM = HGRN_WIDTH // HGRN_HEADS
CONV_WIDTH = MIX_WIDTH - HGRN_WIDTH
CONV_GROUPS = 8
CONV_K = 3
FFN_CONV_K = 3
D_FF = 2816
CHUNK = 64
EPS = 1e-6
IN_COLS = 4 * HGRN_WIDTH + 3 * CONV_WIDTH


def rmsnorm(x, g):
    xf = x.astype(jnp.float32)
    y = xf * lax.rsqrt(jnp.mean(xf * xf, axis=-1, keepdims=True) + EPS)
    return (y * g.astype(jnp.float32)).astype(x.dtype)

def causal_dwconv(x, w):
    k = w.shape[0]
    c = x.shape[-1]
    return lax.conv_general_dilated(
        x, w[:, None, :].astype(x.dtype), window_strides=(1,), padding=[(k - 1, 0)],
        dimension_numbers=("NWC", "WIO", "NWC"), feature_group_count=c)

def to_chunks(t):
    b, t_len, _ = t.shape
    t = t.reshape(b, t_len // CHUNK, CHUNK, HGRN_HEADS, HGRN_HEAD_DIM)
    return t.transpose(1, 0, 3, 2, 4)

def from_chunks(t):
    n, b, h, c, d = t.shape
    return t.transpose(1, 0, 3, 2, 4).reshape(b, n * c, h * d)

def hgrn2_chunkwise(q, k, v, log_f):
    bsz = q.shape[0]
    causal = jnp.tril(jnp.ones((CHUNK, CHUNK), dtype=bool))

    def step(state, inp):
        qc, kc, vc, gc = inp
        b = jnp.cumsum(gc, axis=-2)
        diff = b[..., :, None, :] - b[..., None, :, :]
        decay = jnp.exp(jnp.where(causal[:, :, None], diff, -jnp.inf))
        scores = jnp.einsum('bhtk,bhsk,bhtsk->bhts', qc, kc, decay)
        o = (jnp.einsum('bhts,bhsv->bhtv', scores, vc)
             + jnp.einsum('bhtk,bhkv->bhtv', qc * jnp.exp(b), state))
        b_last = b[..., -1:, :]
        state = (jnp.exp(b_last[..., 0, :])[..., None] * state
                 + jnp.einsum('bhsk,bhsv->bhkv', kc * jnp.exp(b_last - b), vc))
        return state, o

    s0 = jnp.zeros((bsz, HGRN_HEADS, HGRN_HEAD_DIM, HGRN_HEAD_DIM), jnp.float32)
    _, o = lax.scan(step, s0, (to_chunks(q), to_chunks(k), to_chunks(v), to_chunks(log_f)))
    return from_chunks(o)

def hgrn2_mixer(q_pre, f_pre, i_pre, g_pre, lb, norm_g):
    dt = q_pre.dtype
    fp = f_pre.astype(jnp.float32)
    lbf = lb.astype(jnp.float32)
    q = jax.nn.silu(q_pre.astype(jnp.float32)) * (HGRN_HEAD_DIM ** -0.5)
    log_f = jnp.logaddexp(jnp.log(lbf), jnp.log1p(-lbf) + jax.nn.log_sigmoid(fp))
    k = (1.0 - lbf) * jax.nn.sigmoid(-fp)
    v = i_pre.astype(jnp.float32)
    o = hgrn2_chunkwise(q, k, v, log_f)
    bsz, t_len, _ = o.shape
    oh = o.reshape(bsz, t_len, HGRN_HEADS, HGRN_HEAD_DIM)
    oh = oh * lax.rsqrt(jnp.mean(oh * oh, axis=-1, keepdims=True) + EPS)
    o = oh.reshape(bsz, t_len, HGRN_WIDTH) * norm_g.astype(jnp.float32)
    return (o * jax.nn.silu(g_pre.astype(jnp.float32))).astype(dt)

def first_inputs(seed: int = 0) -> dict:
    key = jax.random.key(seed)
    ks = jax.random.split(key, 14)
    f32 = jnp.float32

    def gain(k, shape):
        return 1.0 + 0.05 * jax.random.normal(k, shape, f32)

    return {
        "x": jax.random.normal(ks[0], (BATCH, SEQ, D_MODEL), f32),
        "lb_param": jax.random.normal(ks[1], (DEPTH, HGRN_WIDTH), f32),
        "w_in": jax.random.normal(ks[2], (DEPTH, D_MODEL, IN_COLS), f32) * D_MODEL ** -0.5,
        "w_out": jax.random.normal(ks[3], (DEPTH, MIX_WIDTH, D_MODEL), f32) * MIX_WIDTH ** -0.5,
        "conv_w": jax.random.normal(ks[4], (DEPTH, CONV_K, CONV_WIDTH), f32) * CONV_K ** -0.5,
        "ffn_w_up": jax.random.normal(ks[5], (DEPTH, D_MODEL, 2 * D_FF), f32) * D_MODEL ** -0.5,
        "ffn_conv_w": jax.random.normal(ks[6], (DEPTH, FFN_CONV_K, 2 * D_FF), f32) * FFN_CONV_K ** -0.5,
        "ffn_w_down": jax.random.normal(ks[7], (DEPTH, D_FF, D_MODEL), f32) * D_FF ** -0.5,
        "hgrn_norm_g": gain(ks[8], (DEPTH, HGRN_WIDTH)),
        "pre_mix_g": gain(ks[9], (DEPTH, D_MODEL)),
        "post_mix_g": gain(ks[10], (DEPTH, D_MODEL)),
        "pre_ffn_g": gain(ks[11], (DEPTH, D_MODEL)),
        "post_ffn_g": gain(ks[12], (DEPTH, D_MODEL)),
    }

def first_block(x, lb_param, w_in, w_out, conv_w, ffn_w_up, ffn_conv_w, ffn_w_down,
              hgrn_norm_g, pre_mix_g, post_mix_g, pre_ffn_g, post_ffn_g):
    lb_all = jnp.cumsum(jax.nn.softmax(lb_param.astype(jnp.float32), axis=0), axis=0)
    lb_all = lb_all - lb_all[0:1]
    split_pts = [HGRN_WIDTH * j for j in range(1, 5)] + [4 * HGRN_WIDTH + CONV_WIDTH * j for j in range(1, 3)]

    for l in range(DEPTH):
        h = rmsnorm(x, pre_mix_g[l])
        z = jnp.einsum('btd,dc->btc', h, w_in[l])
        q_p, f_p, i_p, g_p, gate_b, gate_c, conv_h = jnp.split(z, split_pts, axis=-1)
        mix_a = hgrn2_mixer(q_p, f_p, i_p, g_p, lb_all[l], hgrn_norm_g[l])
        mix_b = gate_b * causal_dwconv(gate_c * conv_h, conv_w[l])
        mix = jnp.einsum('btc,cd->btd', jnp.concatenate([mix_a, mix_b], axis=-1), w_out[l])
        x = x + rmsnorm(mix, post_mix_g[l])
        h = rmsnorm(x, pre_ffn_g[l])
        u = causal_dwconv(jnp.einsum('btd,df->btf', h, ffn_w_up[l]), ffn_conv_w[l])
        gate, val = jnp.split(u, 2, axis=-1)
        y = jnp.einsum('btf,fd->btd', jax.nn.silu(gate) * val, ffn_w_down[l])
        x = x + rmsnorm(y, post_ffn_g[l])
    return x


DEPTH_2 = 2

N_A_LAYERS = DEPTH_2 // 2
N_B_LAYERS = DEPTH_2 - N_A_LAYERS

POOL_WINDOWS = (2, 4, 8, 16)
N_POOL_GROUPS = len(POOL_WINDOWS)
POOL_GROUP = D_MODEL // N_POOL_GROUPS

N_HEADS = 16
QK_NOPE_DIM = 128
QK_ROPE_DIM = 64
QK_DIM = QK_NOPE_DIM + QK_ROPE_DIM
V_DIM = 128
Q_LORA_RANK = 256
KV_LORA_RANK = 128
ROPE_THETA = 10000.0
Q_BLOCK = 128

RMS_EPS = 1e-6


def rmsnorm_2(x, g):
    xf = x.astype(jnp.float32)
    y = xf * lax.rsqrt(jnp.mean(xf * xf, axis=-1, keepdims=True) + RMS_EPS)
    return (y * g.astype(jnp.float32)).astype(x.dtype)

def swiglu(u, wg, wu, wd):
    return (jax.nn.silu(u @ wg) * (u @ wu)) @ wd

def rope_tables(seq):
    pos = jnp.arange(seq, dtype=jnp.float32)
    inv_freq = ROPE_THETA ** (-jnp.arange(0, QK_ROPE_DIM, 2, dtype=jnp.float32) / QK_ROPE_DIM)
    ang = pos[:, None] * inv_freq[None, :]
    return jnp.cos(ang), jnp.sin(ang)

def apply_rope(x, cos, sin):
    half = x.shape[-1] // 2
    x1, x2 = x[..., :half], x[..., half:]
    c, s = cos.astype(x.dtype), sin.astype(x.dtype)
    return jnp.concatenate([x1 * c - x2 * s, x1 * s + x2 * c], axis=-1)

def pool_mixer(u, w_groups, scale):
    B, S, D = u.shape
    uf = u.astype(jnp.float32)
    c = jnp.cumsum(uf, axis=1)
    count = jnp.arange(1, S + 1, dtype=jnp.float32)[None, :, None]
    outs = []
    for g, w in enumerate(POOL_WINDOWS):
        sl = slice(g * POOL_GROUP, (g + 1) * POOL_GROUP)
        cg = c[..., sl]
        lag = jnp.pad(cg, ((0, 0), (w, 0), (0, 0)))[:, :S]
        mean = (cg - lag) / jnp.minimum(count, float(w))
        outs.append(mean - uf[..., sl])
    y = jnp.stack(outs, axis=2).astype(u.dtype)
    z = jnp.einsum('bsgc,gcd->bsgd', y, w_groups).reshape(B, S, D)
    return z * scale

def mla_shared_kv(h, kv_in_norm, w_dkv, ckv_norm, w_uk, w_uv, cos, sin):
    u = rmsnorm_2(h, kv_in_norm)
    kv_a = u @ w_dkv
    c_kv = rmsnorm_2(kv_a[..., :KV_LORA_RANK], ckv_norm)
    k_rope = apply_rope(kv_a[..., KV_LORA_RANK:], cos[None], sin[None])
    k_nope = jnp.einsum('bsr,rhd->bshd', c_kv, w_uk)
    v = jnp.einsum('bsr,rhd->bshd', c_kv, w_uv)
    return k_nope, k_rope, v

def mla_attention(u, q_lora_norm, w_dq, w_uq, w_o, k_nope, k_rope, v, cos, sin):
    B, S, _ = u.shape
    cq = rmsnorm_2(u @ w_dq, q_lora_norm)
    q = jnp.einsum('bsr,rhd->bshd', cq, w_uq)
    q_nope = q[..., :QK_NOPE_DIM]
    q_rope = apply_rope(q[..., QK_NOPE_DIM:], cos[None, :, None], sin[None, :, None])
    nblk = S // Q_BLOCK
    qn = q_nope.reshape(B, nblk, Q_BLOCK, N_HEADS, QK_NOPE_DIM).transpose(1, 0, 2, 3, 4)
    qr = q_rope.reshape(B, nblk, Q_BLOCK, N_HEADS, QK_ROPE_DIM).transpose(1, 0, 2, 3, 4)
    scale = QK_DIM ** -0.5
    key_pos = jnp.arange(S)

    def block(args):
        i, qn_b, qr_b = args
        s = (jnp.einsum('bqhd,bkhd->bhqk', qn_b, k_nope)
             + jnp.einsum('bqhr,bkr->bhqk', qr_b, k_rope))
        s = s.astype(jnp.float32) * scale
        q_pos = i * Q_BLOCK + jnp.arange(Q_BLOCK)
        mask = key_pos[None, :] <= q_pos[:, None]
        s = jnp.where(mask[None, None], s, -jnp.inf)
        p = jax.nn.softmax(s, axis=-1).astype(v.dtype)
        return jnp.einsum('bhqk,bkhd->bqhd', p, v)

    o = lax.map(block, (jnp.arange(nblk), qn, qr))
    o = o.transpose(1, 0, 2, 3, 4).reshape(B, S, N_HEADS * V_DIM)
    return o @ w_o

def second_inputs(seed: int = 0) -> dict:
    key = jax.random.key(seed)
    ks = jax.random.split(key, 32)
    f32 = jnp.float32

    def w(k, shape, fan_in):
        return jax.random.normal(k, shape, f32) * (fan_in ** -0.5)

    def gain(k, shape):
        return 1.0 + 0.02 * jax.random.normal(k, shape, f32)

    D, F, G, Dg = D_MODEL, D_FF, N_POOL_GROUPS, POOL_GROUP
    return {
        "x": jax.random.normal(ks[0], (BATCH, SEQ, D), f32),
        "ffn_pre_norm": gain(ks[1], (DEPTH_2, D)),
        "ffn_pre_wg": w(ks[2], (DEPTH_2, D, F), D),
        "ffn_pre_wu": w(ks[3], (DEPTH_2, D, F), D),
        "ffn_pre_wd": w(ks[4], (DEPTH_2, F, D), F),
        "mix_norm": gain(ks[5], (DEPTH_2, D)),
        "ffn_post_norm": gain(ks[6], (DEPTH_2, D)),
        "ffn_post_wg": w(ks[7], (DEPTH_2, D, F), D),
        "ffn_post_wu": w(ks[8], (DEPTH_2, D, F), D),
        "ffn_post_wd": w(ks[9], (DEPTH_2, F, D), F),
        "pool_w": w(ks[10], (N_A_LAYERS, G, Dg, Dg), Dg),
        "pool_scale": gain(ks[11], (N_A_LAYERS, D)),
        "kv_in_norm": gain(ks[12], (D,)),
        "w_dkv": w(ks[13], (D, KV_LORA_RANK + QK_ROPE_DIM), D),
        "ckv_norm": gain(ks[14], (KV_LORA_RANK,)),
        "w_uk": w(ks[15], (KV_LORA_RANK, N_HEADS, QK_NOPE_DIM), KV_LORA_RANK),
        "w_uv": w(ks[16], (KV_LORA_RANK, N_HEADS, V_DIM), KV_LORA_RANK),
        "q_lora_norm": gain(ks[17], (N_B_LAYERS, Q_LORA_RANK)),
        "w_dq": w(ks[18], (N_B_LAYERS, D, Q_LORA_RANK), D),
        "w_uq": w(ks[19], (N_B_LAYERS, Q_LORA_RANK, N_HEADS, QK_DIM), Q_LORA_RANK),
        "w_o": w(ks[20], (N_B_LAYERS, N_HEADS * V_DIM, D), N_HEADS * V_DIM),
        "final_norm": gain(ks[21], (D,)),
    }

def second_block(x, ffn_pre_norm, ffn_pre_wg, ffn_pre_wu, ffn_pre_wd, mix_norm,
              ffn_post_norm, ffn_post_wg, ffn_post_wu, ffn_post_wd,
              pool_w, pool_scale, kv_in_norm, w_dkv, ckv_norm, w_uk, w_uv,
              q_lora_norm, w_dq, w_uq, w_o, final_norm):
    S = x.shape[1]
    cos, sin = rope_tables(S)
    h = x
    k_nope = k_rope = v = None
    for l in range(DEPTH_2):
        h = h + 0.5 * swiglu(rmsnorm_2(h, ffn_pre_norm[l]), ffn_pre_wg[l], ffn_pre_wu[l], ffn_pre_wd[l])
        u = rmsnorm_2(h, mix_norm[l])
        if l < N_A_LAYERS:
            h = h + pool_mixer(u, pool_w[l], pool_scale[l])
        else:
            j = l - N_A_LAYERS
            h = h + mla_attention(u, q_lora_norm[j], w_dq[j], w_uq[j], w_o[j],
                                  k_nope, k_rope, v, cos, sin)
        h = h + 0.5 * swiglu(rmsnorm_2(h, ffn_post_norm[l]), ffn_post_wg[l], ffn_post_wu[l], ffn_post_wd[l])
        if l == N_A_LAYERS - 1:
            k_nope, k_rope, v = mla_shared_kv(h, kv_in_norm, w_dkv, ckv_norm, w_uk, w_uv, cos, sin)
    return rmsnorm_2(h, final_norm)


def setup_inputs(seed=0):
    out = dict(first_inputs(seed))
    for name, value in second_inputs(seed + 1).items():
        if name != "x":
            out[name + "_2"] = value
    return out


def reference(
    x, lb_param, w_in, w_out, conv_w, ffn_w_up, ffn_conv_w, ffn_w_down, hgrn_norm_g, pre_mix_g,
    post_mix_g, pre_ffn_g, post_ffn_g, ffn_pre_norm_2, ffn_pre_wg_2, ffn_pre_wu_2, ffn_pre_wd_2,
    mix_norm_2, ffn_post_norm_2, ffn_post_wg_2, ffn_post_wu_2, ffn_post_wd_2, pool_w_2,
    pool_scale_2, kv_in_norm_2, w_dkv_2, ckv_norm_2, w_uk_2, w_uv_2, q_lora_norm_2, w_dq_2,
    w_uq_2, w_o_2, final_norm_2,
):
    x = first_block(
        x, lb_param, w_in, w_out, conv_w, ffn_w_up, ffn_conv_w, ffn_w_down, hgrn_norm_g,
        pre_mix_g, post_mix_g, pre_ffn_g, post_ffn_g,
    )
    return second_block(
        x, ffn_pre_norm_2, ffn_pre_wg_2, ffn_pre_wu_2, ffn_pre_wd_2, mix_norm_2,
        ffn_post_norm_2, ffn_post_wg_2, ffn_post_wu_2, ffn_post_wd_2, pool_w_2, pool_scale_2,
        kv_in_norm_2, w_dkv_2, ckv_norm_2, w_uk_2, w_uv_2, q_lora_norm_2, w_dq_2, w_uq_2, w_o_2,
        final_norm_2,
    )


_drawn_inputs = setup_inputs


def setup_inputs(seed=0):
    import zlib

    import numpy as np

    out = dict(_drawn_inputs(seed))
    spreads = {}
    factors = {'ffn_pre_norm_2': 8.0,
     'mix_norm_2': 6.092,
     'ffn_post_norm_2': 8.0,
     'pool_scale_2': 5.784,
     'kv_in_norm_2': 8.0,
     'ckv_norm_2': 22.654,
     'q_lora_norm_2': 8.0,
     'final_norm_2': 8.042}
    for name, (base, spread) in spreads.items():
        noise = np.random.default_rng([zlib.crc32(name.encode()), seed]).standard_normal(out[name].shape)
        drawn = base * np.exp(spread * noise) if base else spread * noise
        out[name] = __import__('jax').numpy.asarray(drawn.astype(out[name].dtype))
    for name, factor in factors.items():
        out[name] = (out[name] * factor).astype(out[name].dtype)
    return out
```

```python
from contextlib import ExitStack

import concourse.bass as bass
from concourse import mybir

F32 = mybir.dt.float32
F32R = mybir.dt.float32r
BF16 = mybir.dt.bfloat16
U8 = mybir.dt.uint8
ACT = mybir.ActivationFunctionType
ALU = mybir.AluOpType
AX_X = mybir.AxisListType.X

P = 128
T = 512
D = 1024
DT = D // P
FF = 2816
FT = FF // P
TC = T // P
UC = 256
UNIT = DT * UC
HH = 4
NH = 16
NOPE = 128
ROPE = 64
QR = 2
EPS = 1e-6
RING = 4
LEVELS = [1, 2, 4, 8, 16, 32, 64]
QUARTERS = 4
DOWN = [8, 8, 6]

VECTORS = [("pre_mix_g", 8), ("post_mix_g", 8), ("pre_ffn_g", 8), ("post_ffn_g", 8),
           ("ffn_pre_norm_2", 16), ("mix_norm_2", 16), ("ffn_post_norm_2", 16), ("pool_scale_2", 8),
           ("kv_in_norm_2", 8), ("ckv_norm_2", 1), ("q_lora_norm_2", 2), ("final_norm_2", 8),
           ("hgrn_norm_g", 4), ("conv_w", 12)]
COL = {}
_at = 0
for _name, _n in VECTORS:
    COL[_name] = _at
    _at += _n
NVEC = _at

PHASES = [("x_in", 0, 8), ("w_in", 14, 32), ("levels", 0, 4 * (len(LEVELS) + 1)), ("cross", 0, 8),
          ("state_out", 0, 4), ("head_sums", 0, 4), ("w_out", 4, 8), ("up0", 22, 44), ("down0", 12, 8),
          ("up1", 22, 44), ("down1", 12, 8), ("pool", 2, 8), ("up2", 22, 44), ("down2", 12, 8),
          ("kv", 2, 4), ("up3", 22, 44), ("down3", 12, 8), ("dq", 2, 4), ("attn", 8, 64),
          ("w_o", 8, 8), ("up4", 22, 44), ("down4", 12, 8), ("x_out", 0, 8)]
UB, GB = {}, {}
_u = _g = 0
for _name, _nu, _ng in PHASES:
    UB[_name], GB[_name] = _u, _g
    _u += _nu
    _g += _ng
UNITS = _u
MB, _m = {}, 0
for _name, _nk in [("w_out", 1), ("down0", 3), ("down1", 3), ("down2", 3), ("down3", 3), ("w_o", 2), ("down4", 3)]:
    MB[_name] = _m
    _m += 4 * (_nk - 1)

XG = {n: 8 * j for j, n in enumerate(["w_in", "w_out", "up0", "up1", "pool", "up2", "kv", "up3", "dq", "up4"])}
NORM = {n: j for j, n in enumerate(["pre_mix", "post_mix", "pre_ffn", "post_ffn", "pre0", "mix0", "post0",
                                    "kv_pre1", "mix1", "post1", "final"])}


def steps(eng, n, unroll=False):
    if unroll:
        for i in range(n):
            yield i
    else:
        with eng.Fori(0, n) as i:
            yield i


def build(nc, A, out):
    ctx = ExitStack()
    with ctx:
        def sb(name, shape, dt=F32, where=ctx):
            return where.enter_context(nc.sbuf_tensor(name, shape, dt))

        def sem(name):
            return ctx.enter_context(nc.semaphore(name))

        xT = sb("xT", [P, DT * T])
        raw = sb("raw", [P, 2 * UNIT])
        whi = sb("whi", [P, 2 * UNIT], F32R)
        wlo = sb("wlo", [P, 2 * UNIT], F32R)
        R = sb("R", [P, T])
        acc = sb("acc", [P, T])
        sq = sb("sq", [P, T])
        work = sb("work", [P, 6 * T])
        Tt, At, Ut = (work[:, 2 * j * T:2 * (j + 1) * T] for j in range(3))
        cols = sb("cols", [P, NVEC])
        cw = sb("cw", [P, 3 * 2 * FT])
        ident = sb("ident", [P, P])
        ones = sb("ones", [P, P])
        perm = sb("perm", [P, P])
        identb = sb("identb", [P, P], BF16)
        causal = sb("causal", [P, P], BF16)
        masks = sb("masks", [P, 8 * P], U8)
        rcol = sb("rcol", [P, TC])
        ends = sb("ends", [P, HH * TC])
        rowmax = sb("rowmax", [P, 8])
        negmax = sb("negmax", [P, 8])
        rowinv = sb("rowinv", [P, 8])
        rowsum = sb("rowsum", [P, 8])
        flex = ExitStack()
        xghi = sb("xghi", [P, DT * T], F32R, flex)
        xglo = sb("xglo", [P, DT * T], F32R, flex)
        act = ExitStack()
        ahi = sb("ahi", [P, FT * T], F32R, act)
        alo = sb("alo", [P, FT * T], F32R, act)
        act.close()
        hg = ExitStack()
        fkb = sb("fkb", [P, 2 * 2048], F32, hg)
        Q = sb("Q", [P, 2048], F32, hg)
        V = sb("V", [P, TC * 512], F32, hg)
        G = sb("G", [P, 2048], F32, hg)
        GBt = sb("GBt", [P, 2048], F32, hg)
        GC = sb("GC", [P, 2048], F32, hg)
        CH = sb("CH", [P, 2048], F32, hg)
        SD = sb("SD", [P, HH * TC * P], F32, hg)
        SC = sb("SC", [P, HH * 6 * P], F32, hg)
        hg.close()
        yb = ExitStack()
        Y0 = sb("Y0", [P, DT * T], F32, yb)
        rows = sb("rows", [P, 3 * P], F32, yb)
        wide_causal = sb("wide_causal", [P, P], F32, yb)
        wide_masks = sb("wide_masks", [P, 8 * P], mybir.dt.int32, yb)
        yb.close()
        pl = ExitStack()
        PW = 16 + T
        PU = sb("PU", [P, DT * PW], F32, pl)
        PA = sb("PA", [P, 2 * PW], F32, pl)
        PB = sb("PB", [P, 2 * PW], F32, pl)
        inv = sb("inv", [P, 4 * T], F32, pl)
        pl.close()
        kv = ExitStack()
        rope_kv = sb("rope_kv", [P, 2 * T], F32, kv)
        kvt = sb("kvt", [P, 2 * T], F32, kv)
        kv.close()
        fin = ExitStack()
        Z = sb("Z", [P, DT * T], F32, fin)
        ob = sb("ob", [P, TC * D], F32, fin)
        fin.close()
        flex.close()
        f2 = ExitStack()
        Y1 = sb("Y1", [P, DT * T], F32, f2)
        f2.close()
        at = ExitStack()
        KN = sb("KN", [P, 4 * T], F32, at)
        QN = sb("QN", [P, 4 * T], F32, at)
        VV = sb("VV", [P, TC * 512], F32, at)
        QRt = sb("QRt", [P, 2 * T], F32, at)
        Prb = sb("Prb", [P, 10 * P], F32, at)
        oThi = sb("oThi", [P, NH * T], F32R, at)
        oTlo = sb("oTlo", [P, NH * T], F32R, at)
        rope_q = sb("rope_q", [P, 2 * T], F32, at)
        ckhi = sb("ckhi", [P, T], F32R, at)
        cklo = sb("cklo", [P, T], F32R, at)
        cqhi = sb("cqhi", [P, QR * T], F32R, at)
        cqlo = sb("cqlo", [P, QR * T], F32R, at)
        PT = sb("PT", [P, 10 * P], F32, at)
        at.close()
        QRr = Prb[:, 0:2 * T]

        def probs(h):
            return work[:, 2 * T:2 * T + 10 * P] if h % 2 == 0 else Prb[:, :]

        banks = [ctx.enter_context(nc.psum_tensor(f"bank{b}", [P, 512], F32)) for b in range(8)]
        ring, stat, misc = banks[:RING], banks[4], banks[5]

        x_loaded = sem("x_loaded")
        rows_loaded = sem("rows_loaded")
        consts_loaded = sem("consts_loaded")
        ones_ready = sem("ones_ready")
        cols_turned = sem("cols_turned")
        cols_ready = sem("cols_ready")
        part_loaded = sem("part_loaded")
        raw_ready = [sem("raw_ready0"), sem("raw_ready1")]
        whi_ready = sem("whi_ready")
        wlo_ready = sem("wlo_ready")
        parts_used = sem("parts_used")
        groups_done = sem("groups_done")
        evacuated = sem("evacuated")
        resid_part = sem("resid_part")
        resid_ready = sem("resid_ready")
        square_ready = sem("square_ready")
        acc_step = sem("acc_step")
        acc_ready = sem("acc_ready")
        sums_ready = sem("sums_ready")
        rstd_part = sem("rstd_part")
        rstd_ready = sem("rstd_ready")
        root_ready = sem("root_ready")
        small_root = sem("small_root")
        rcol_sums = sem("rcol_sums")
        rcol_part = sem("rcol_part")
        rcol_ready = sem("rcol_ready")
        xghi_ready = sem("xghi_ready")
        xg_ready = sem("xg_ready")
        tap_ready = sem("tap_ready")
        conv_part = sem("conv_part")
        conv_ready = sem("conv_ready")
        silu_ready = sem("silu_ready")
        gated_ready = sem("gated_ready")
        ahi_ready = sem("ahi_ready")
        act_ready = sem("act_ready")
        decay_vec = sem("decay_vec")
        decay_act = sem("decay_act")
        q_silu = sem("q_silu")
        mixb_part = sem("mixb_part")
        mixb_ready = sem("mixb_ready")
        level_arg = sem("level_arg")
        scores_cleared = sem("scores_cleared")
        masks_ready = sem("masks_ready")
        level_exp = sem("level_exp")
        level_ready = sem("level_ready")
        cross_arg = sem("cross_arg")
        cross_exp = sem("cross_exp")
        cross_ready = sem("cross_ready")
        osq_ready = sem("osq_ready")
        head_part = sem("head_part")
        mixa_ready = sem("mixa_ready")
        pool_step = sem("pool_step")
        pool_ready = sem("pool_ready")
        inv_loaded = sem("inv_loaded")
        small_step = sem("small_step")
        ck_ready = sem("ck_ready")
        rope_kv_loaded = sem("rope_kv_loaded")
        rope_q_loaded = sem("rope_q_loaded")
        latent_ready = sem("latent_ready")
        latent_hi = sem("latent_hi")
        latent_split = sem("latent_split")
        qrope_part = sem("qrope_part")
        qrope_ready = sem("qrope_ready")
        scores_ready = sem("scores_ready")
        max_part = sem("max_part")
        negmax_ready = sem("negmax_ready")
        exp_ready = sem("exp_ready")
        recip_ready = sem("recip_ready")
        probs_ready = sem("probs_ready")
        turned_ready = sem("turned_ready")
        turned_act = sem("turned_act")
        turned_vec = sem("turned_vec")
        out_ready = sem("out_ready")
        outhi_ready = sem("outhi_ready")
        outlo_ready = sem("outlo_ready")
        normed_out = sem("normed_out")
        stored = sem("stored")

        block = ctx.enter_context(nc.Block())

        def tile(t, k, n=T):
            return t[:, k * n:(k + 1) * n] if isinstance(k, int) else t[:, bass.ds(k * n, n)]

        def col(name, k):
            c = COL[name] + k
            return cols[:, c:c + 1] if isinstance(c, int) else cols[:, bass.ds(c, 1)]

        def slot(t, n, kt=DT, width=UC):
            return t[:, n * UNIT:n * UNIT + kt * width].rearrange("p (k c) -> p k c", k=kt)

        fk, lb_ = fkb[:, 0:2048], fkb[:, 2048:4096]

        @block.sync
        def _(sp):
            xtok = fkb[:, :].rearrange("p (c d) -> p c d", c=TC)
            for c in range(TC):
                sp.dma_start(xtok[:, c, :], A["x"][0, c * P:(c + 1) * P, :]).then_inc(x_loaded, 16)

            def load(n, s, pieces):
                if not (isinstance(n, int) and n < 2):
                    sp.wait_ge(wlo_ready, n - 1)
                for dst, src in pieces[:-1]:
                    sp.dma_start(dst, src).then_inc(part_loaded, 16)
                    parts[0] += 16
                if len(pieces) > 1:
                    sp.wait_ge(part_loaded, parts[0])
                sp.dma_start(*pieces[-1]).then_inc(raw_ready[s], 16)

            parts = [0]
            win = A["w_in"][0].rearrange("(k p) c -> p k c", p=P)
            for j, part in enumerate([1, 0, 5, 6, 4, 2, 3]):
                for u in range(2):
                    c0 = part * 512 + u * UC
                    load(2 * j + u, u, [(slot(raw, u), win[:, :, c0:c0 + UC])])

            def column_blocks(name, w, ksplit, unroll=False):
                nk = len(ksplit)
                for i in steps(sp, 2, unroll):
                    for b in range(2):
                        k0 = 0
                        for j, kt in enumerate(ksplit):
                            s = (b * nk + j) % 2
                            c0 = i * (2 * UC) + b * UC
                            src = w[:, k0:k0 + kt, c0:c0 + UC] if isinstance(c0, int) else \
                                w[:, k0:k0 + kt, bass.ds(c0, UC)]
                            load(i * (2 * nk) + (UB[name] + b * nk + j), s, [(slot(raw, s, kt), src)])
                            k0 += kt

            def up(name, wg, wu):
                with sp.Fori(0, FF // UC) as i:
                    for s, w in enumerate((wg, wu)):
                        load(i * 2 + (UB[name] + s), s, [(slot(raw, s), w[:, :, bass.ds(i * UC, UC)])])

            def kp(w):
                return w.rearrange("(k p) c -> p k c", p=P)

            column_blocks("w_out", kp(A["w_out"][0]), [8])
            up0 = kp(A["ffn_w_up"][0])
            up("up0", up0[:, :, 0:FF], up0[:, :, FF:2 * FF])
            column_blocks("down0", kp(A["ffn_w_down"][0]), DOWN)

            def ffn(n, which, l, unroll=False):
                up(f"up{n}", kp(A[f"ffn_{which}_wg_2"][l]), kp(A[f"ffn_{which}_wu_2"][l]))
                column_blocks(f"down{n}", kp(A[f"ffn_{which}_wd_2"][l]), DOWN, unroll)

            ffn(1, "pre", 0)
            for u in range(2):
                load(UB["pool"] + u, u, [(slot(raw, u, 4), A["pool_w_2"][0, 2 * u:2 * u + 2].rearrange(
                    "g (t p) c -> p (g t) c", p=P))])
            sp.wait_ge(groups_done, GB["pool"])
            sp.dma_start(inv[:, :], A["inv_count"].to_broadcast([P, 4 * T])).then_inc(inv_loaded, 16)
            ffn(2, "post", 0)
            dkv = kp(A["w_dkv_2"])
            load(UB["kv"], 0, [(slot(raw, 0, DT, P), dkv[:, :, 0:P])])
            kr = slot(raw, 1, DT, P)
            load(UB["kv"] + 1, 1, [(kr[:, :, 0:ROPE], dkv[:, :, P:P + ROPE]),
                                   (kr[:, :, ROPE:P], dkv[:, :, P:P + ROPE])])
            sp.wait_ge(groups_done, GB["kv"])
            sp.dma_start(rope_kv[:, :], A["rope"]).then_inc(rope_kv_loaded, 16)
            ffn(3, "pre", 1)
            dq = kp(A["w_dq_2"][0])
            for u in range(2):
                load(UB["dq"] + u, u, [(slot(raw, u, DT, P), dq[:, :, u * P:(u + 1) * P])])
            sp.wait_ge(groups_done, GB["dq"])
            sp.dma_start(rope_q[:, :], A["rope"]).then_inc(rope_q_loaded, 16)
            uk = A["w_uk_2"].rearrange("r h d -> r (h d)")
            uv = A["w_uv_2"].rearrange("r h d -> r (h d)")
            uq = A["w_uq_2"][0].rearrange("(t p) h e -> p t h e", p=P)
            r0, r1 = raw[:, 0:UNIT], raw[:, UNIT:UNIT + 512]
            with sp.Fori(0, QUARTERS) as q:
                sp.wait_ge(wlo_ready, q * 2 + (UB["attn"] - 1))
                base = parts[0]
                sp.dma_start(r0[:, 0:512], uk[:, bass.ds(q * 512, 512)]).then_inc(part_loaded, 16)
                sp.dma_start(r0[:, 512:1024], uv[:, bass.ds(q * 512, 512)]).then_inc(part_loaded, 16)
                sp.dma_start(r0[:, 1024:1536].rearrange("p (h e) -> p h e", h=4),
                             uq[:, 0, bass.ds(q * 4, 4), 0:NOPE]).then_inc(part_loaded, 16)
                sp.wait_ge(part_loaded, q * 64 + (base + 48))
                sp.dma_start(r0[:, 1536:2048].rearrange("p (h e) -> p h e", h=4),
                             uq[:, 1, bass.ds(q * 4, 4), 0:NOPE]).then_inc(raw_ready[0], 16)
                sp.wait_ge(wlo_ready, q * 2 + UB["attn"])
                sp.dma_start(r1[:, 0:256].rearrange("p (h e) -> p h e", h=4),
                             uq[:, 0, bass.ds(q * 4, 4), NOPE:NOPE + ROPE]).then_inc(part_loaded, 16)
                sp.wait_ge(part_loaded, q * 64 + (base + 64))
                sp.dma_start(r1[:, 256:512].rearrange("p (h e) -> p h e", h=4),
                             uq[:, 1, bass.ds(q * 4, 4), NOPE:NOPE + ROPE]).then_inc(raw_ready[1], 16)
            column_blocks("w_o", kp(A["w_o_2"][0]), [8, 8])
            ffn(4, "post", 1)
            for c in range(TC):
                sp.wait_ge(evacuated, GB["x_out"] + 2 * (c + 1))
                sp.dma_start(out[0, c * P:(c + 1) * P, :], ob[:, c * D:(c + 1) * D]).then_inc(stored, 16)
            sp.wait_ge(stored, 16 * TC)

        @block.gpsimd
        def _(pool):
            nc.gpsimd.memset(ones[:, :], 1.0).then_inc(ones_ready, 1)
            acc_steps = [0]
            squares = [0]

            def sum_squares(name, t, signal, base):
                j = NORM[name]
                if j:
                    pool.wait_ge(sums_ready, j)
                for k in range(DT):
                    pool.wait_ge(signal, base + k + 1)
                    x = tile(t, k)
                    if k == 0:
                        nc.gpsimd.tensor_tensor(acc[:, :], x, x, ALU.mult).then_inc(acc_step, 1)
                    else:
                        pool.wait_ge(acc_step, acc_steps[0])
                        nc.gpsimd.tensor_tensor(sq[:, :], x, x, ALU.mult).then_inc(square_ready, 1)
                        squares[0] += 1
                        pool.wait_ge(square_ready, squares[0])
                        nc.gpsimd.tensor_tensor(acc[:, :], acc[:, :], sq[:, :], ALU.add).then_inc(
                            acc_step if k < DT - 1 else acc_ready, 1)
                    if k < DT - 1:
                        acc_steps[0] += 1

            sum_squares("pre_mix", xT, evacuated, GB["x_in"])
            sum_squares("post_mix", Y0, evacuated, GB["w_out"])
            sum_squares("pre_ffn", xT, resid_ready, 0)
            sum_squares("post_ffn", Y1, evacuated, GB["down0"])
            sum_squares("pre0", xT, resid_ready, DT)
            sum_squares("mix0", xT, evacuated, GB["down1"])
            sum_squares("post0", xT, evacuated, GB["pool"])
            sum_squares("kv_pre1", xT, evacuated, GB["down2"])
            sum_squares("mix1", xT, evacuated, GB["down3"])
            sum_squares("post1", xT, evacuated, GB["w_o"])
            sum_squares("final", xT, evacuated, GB["down4"])

        @block.scalar
        def _(a):
            for name, n in VECTORS:
                v = A[name]
                v = v.rearrange("a (k p) -> (a k) p", p=P) if len(v.shape) == 2 else (
                    v.rearrange("a b (k p) -> (a b k) p", p=P) if len(v.shape) == 3 else
                    v.rearrange("(k p) -> k p", p=P))
                a.dma_start(rows[COL[name]:COL[name] + n, 0:P], v).then_inc(rows_loaded, 16)
            taps = A["ffn_conv_w"].rearrange("a b (k p) -> (a b k) p", p=P)
            a.dma_start(rows[0:88, P:2 * P], taps[0:88]).then_inc(rows_loaded, 16)
            a.dma_start(rows[0:44, 2 * P:3 * P], taps[88:132]).then_inc(rows_loaded, 16)
            for dst, name in ((ident, "ident"), (perm, "perm"), (wide_causal, "causal"), (wide_masks, "masks")):
                a.dma_start(dst[:, :], A[name]).then_inc(consts_loaded, 16)

            def split_hi(n, s, signal=None, value=None):
                a.wait_ge(raw_ready[s], (n - s) * 8 + 16)
                if signal is not None:
                    a.wait_ge(signal, value)
                nc.scalar.activation(whi[:, s * UNIT:(s + 1) * UNIT], raw[:, s * UNIT:(s + 1) * UNIT],
                                     ACT.Copy).then_inc(whi_ready, 1)

            def xg_hi(signal, value, t, gain, k, w=None):
                a.wait_ge(signal, value)
                nc.scalar.activation(tile(xghi, k), tile(t, k), ACT.Copy,
                                     scale=1.0 if gain is None else col(gain, k if w is None else w)
                                     ).then_inc(xghi_ready, 1)

            split_hi(0, 0)
            split_hi(1, 1)
            a.wait_ge(cols_ready, 3)
            for k in range(DT):
                xg_hi(evacuated, k + 1, xT, "pre_mix_g", k)
            def root(name):
                a.wait_ge(rstd_part, NORM[name] + 1)
                nc.scalar.activation(R[:, :], R[:, :], ACT.Sqrt).then_inc(root_ready, 1)

            def root_of(t, signal, value):
                a.wait_ge(signal, value)
                nc.scalar.activation(t, t, ACT.Sqrt).then_inc(small_root, 1)

            root_of(rcol[:, :], rcol_part, 1)
            root("pre_mix")
            g0 = GB["w_in"]
            for n in range(14):
                read = 2 * (n + 1) if n < 10 else 20 + 4 * (n - 9) if n < 12 else 28 + 2 * (n - 11)
                split_hi(n + 2, n % 2, groups_done, g0 + read)
                if n == 3:
                    a.wait_ge(evacuated, g0 + 4)
                    nc.scalar.activation(lb_, fk, ACT.Abs).then_inc(decay_act, 1)
                    a.wait_ge(decay_act, 1)
                    nc.scalar.activation(lb_, lb_, ACT.Exp, scale=-1.0).then_inc(decay_act, 1)
                    a.wait_ge(decay_act, 2)
                    nc.scalar.activation(lb_, lb_, ACT.Ln, bias=1.0).then_inc(decay_act, 1)
                if n == 4:
                    a.wait_ge(decay_vec, 2)
                    nc.scalar.activation(fk, fk, ACT.Exp).then_inc(decay_act, 1)
                    a.wait_ge(evacuated, g0 + 8)
                    nc.scalar.activation(Q[:, :], Q[:, :], ACT.Silu).then_inc(q_silu, 1)
            a.wait_ge(evacuated, g0 + 32)
            nc.scalar.activation(G[:, :], G[:, :], ACT.Silu).then_inc(q_silu, 1)
            for k in range(4):
                a.wait_ge(mixb_ready, k + 1)
                nc.scalar.activation(tile(xghi, 4 + k), tile(GBt, k), ACT.Copy).then_inc(xghi_ready, 1)
            for l in range(len(LEVELS)):
                a.wait_ge(level_arg, 2 * (l + 1))
                nc.scalar.activation(CH[:, :], CH[:, :], ACT.Exp).then_inc(level_exp, 1)
            bends = lb_.rearrange("p (c t) -> p c t", t=P)[:, :, P - 1]
            a.wait_ge(cross_arg, 1)
            nc.scalar.activation(CH[:, :], CH[:, :], ACT.Exp).then_inc(cross_exp, 1)
            nc.scalar.activation(ends[:, :], bends, ACT.Exp).then_inc(cross_exp, 1)
            a.wait_ge(cross_exp, 2)
            nc.scalar.activation(lb_, lb_, ACT.Exp).then_inc(cross_exp, 1)
            for h in range(HH):
                root_of(tile(GC, h), evacuated, GB["head_sums"] + h + 1)
            for h in range(HH):
                a.wait_ge(mixa_ready, h + 1)
                nc.scalar.activation(tile(xghi, h), tile(CH, h), ACT.Copy).then_inc(xghi_ready, 1)
            def project(name, ksplit, gain=None, goff=0, unroll=False):
                nk = len(ksplit)
                for i in steps(a, 2, unroll):
                    for b in range(2):
                        for j in range(nk):
                            s = (b * nk + j) % 2
                            n = i * (2 * nk) + (UB[name] + b * nk + j + 2)
                            if unroll and n >= UNITS:
                                continue
                            if j < nk - 1:
                                split_hi(n, s, parts_used, i * (2 * nk - 2) + (MB[name] + b * (nk - 1) + j + 1))
                            else:
                                split_hi(n, s, groups_done, i * 4 + (GB[name] + 2 * b + 2))
                        if gain:
                            for f in range(2):
                                k = i * 4 + (2 * b + f)
                                xg_hi(evacuated, k + (GB[name] + 1), xT, gain, k, k + goff)

            project("w_out", [8])
            root("post_mix")
            for k in range(DT):
                xg_hi(resid_ready, k + 1, xT, "pre_ffn_g", k)

            def up(m, conv=False):
                name = f"up{m}"
                gb, hb = GB[name], FT * m
                with a.Fori(0, FT // 2) as i:
                    for f in range(2):
                        if conv:
                            a.wait_ge(evacuated, i * 4 + (gb + f + 1))
                            nc.scalar.activation(tile(Tt, f), tile(Ut, f), ACT.Copy,
                                                 scale=cw[:, bass.ds(i * 2 + (2 * 2 * FT + f), 1)]
                                                 ).then_inc(tap_ready, 1)
                    for f in range(2):
                        if conv:
                            a.wait_ge(conv_ready, i * 4 + (f + 1))
                        else:
                            a.wait_ge(evacuated, i * 4 + (gb + f + 1))
                        nc.scalar.activation(tile(Tt, f), tile(Tt, f), ACT.Silu).then_inc(silu_ready, 1)
                    split_hi(i * 2 + (UB[name] + 2), 0, groups_done, i * 4 + (gb + 2))
                    for f in range(2):
                        if conv:
                            a.wait_ge(evacuated, i * 4 + (gb + f + 3))
                            nc.scalar.activation(tile(At, f), tile(Ut, f), ACT.Copy,
                                                 scale=cw[:, bass.ds(i * 2 + (2 * 2 * FT + FT + f), 1)]
                                                 ).then_inc(tap_ready, 1)
                    for f in range(2):
                        a.wait_ge(gated_ready, i * 2 + (hb + f + 1))
                        nc.scalar.activation(tile(ahi, i * 2 + f), tile(At, f), ACT.Copy).then_inc(ahi_ready, 1)
                    split_hi(i * 2 + (UB[name] + 3), 1, groups_done, i * 4 + (gb + 4))

            root("pre_ffn")
            up(0, conv=True)
            project("down0", DOWN)
            root("post_ffn")
            for k in range(DT):
                xg_hi(resid_ready, DT + k + 1, xT, "ffn_pre_norm_2", k)
            root("pre0")
            up(1)
            project("down1", DOWN)
            root("mix0")
            for k in range(DT):
                a.wait_ge(pool_ready, k // 2 + 1)
                src = PB if (k // 2) % 2 else PA
                nc.scalar.activation(tile(xghi, k), src[:, (k % 2) * PW + 16:(k % 2 + 1) * PW], ACT.Copy
                                     ).then_inc(xghi_ready, 1)
            for u in range(2):
                split_hi(UB["pool"] + u + 2, u, groups_done, GB["pool"] + 4 * (u + 1))
            for k in range(DT):
                a.wait_ge(groups_done, GB["pool"] + DT)
                xg_hi(evacuated, GB["pool"] + k + 1, xT, "ffn_post_norm_2", k)
            root("post0")
            up(2)
            project("down2", DOWN, "kv_in_norm_2")
            root("kv_pre1")
            for u in range(2):
                split_hi(UB["kv"] + u + 2, u, groups_done, GB["kv"] + u + 1)
            root_of(kvt[:, T:2 * T], evacuated, GB["kv"] + 3)
            a.wait_ge(groups_done, GB["kv"] + 2)
            for k in range(DT):
                xg_hi(evacuated, GB["down2"] + k + 1, xT, "ffn_pre_norm_2", k, 8 + k)
            up(3)
            project("down3", DOWN, "mix_norm_2", 8)
            root("mix1")
            for u in range(2):
                split_hi(UB["dq"] + u + 2, u, groups_done, GB["dq"] + u + 1)
            root_of(PT[:, 0:T], evacuated, GB["dq"] + 4)
            for j in range(1 + QR):
                a.wait_ge(latent_ready, j + 1 if j else 1)
                dst = ckhi[:, :] if j == 0 else tile(cqhi, j - 1)
                src = Ut[:, 0:T] if j == 0 else tile(At, j - 1)
                nc.scalar.activation(dst, src, ACT.Copy).then_inc(latent_hi, 1)
            with a.Fori(0, QUARTERS) as q:
                split_hi(q * 2 + (UB["attn"] + 2), 0, groups_done, q * 16 + (GB["attn"] + 12))
                split_hi(q * 2 + (UB["attn"] + 3), 1, groups_done, q * 16 + (GB["attn"] + 14))

                def exps(h):
                    for i in range(TC):
                        e = 4 * h + i
                        a.wait_ge(negmax_ready, q * 16 + (e + 1))
                        c = 4 * (h % 2) + i
                        off = i * (i + 1) // 2 * P
                        nc.scalar.activation(probs(h)[:, off:off + (i + 1) * P], ring[i][:, 0:(i + 1) * P],
                                             ACT.Exp, bias=negmax[:, c:c + 1], scale=float((NOPE + ROPE) ** -0.5),
                                             accum_out=rowsum[:, c:c + 1]).then_inc(exp_ready, 1)

                exps(0)
                for h in range(4):
                    if h < 3:
                        exps(h + 1)
                    a.wait_ge(turned_ready, q * 12 + (3 * h + 1))
                    nc.scalar.activation(PT[:, 0:4 * P], banks[4][:, 0:4 * P], ACT.Copy).then_inc(turned_act, 1)
                    a.wait_ge(turned_ready, q * 12 + (3 * h + 3))
                    nc.scalar.activation(PT[:, 7 * P:10 * P], banks[6][:, 0:3 * P], ACT.Copy).then_inc(turned_act, 1)
                    a.wait_ge(out_ready, q * 4 + (h + 1))
                    nc.scalar.activation(tile(oThi, q * 4 + h), banks[7][:, :], ACT.Copy).then_inc(outhi_ready, 1)
            project("w_o", [8, 8], "ffn_post_norm_2", 8)
            root("post1")
            up(4)
            project("down4", DOWN, unroll=True)
            root("final")


        @block.tensor
        def _(pe):
            def unit_ready(n):
                pe.wait_ge(wlo_ready, n + 1)

            def three(bank, whi_, wlo_, xhi, xlo, first, last):
                nc.tensor.matmul(bank, wlo_, xhi, start=first, stop=False)
                nc.tensor.matmul(bank, whi_, xlo, start=False, stop=False)
                return nc.tensor.matmul(bank, whi_, xhi, start=False, stop=last)

            def bank_free(g):
                pe.wait_ge(evacuated, g - RING + 1)

            def sum_norm(name):
                j = NORM[name]
                pe.wait_ge(acc_ready, j + 1)
                if j:
                    pe.wait_ge(rstd_part, j)
                if j == 0:
                    for c in range(TC):
                        m = nc.tensor.matmul(misc[:, c:c + 1], acc[:, c * P:(c + 1) * P], ones[:, 0:1],
                                             start=True, stop=True)
                    m.then_inc(rcol_sums, 1)
                nc.tensor.matmul(stat[:, :], ones[:, :], acc[:, :], start=True, stop=True).then_inc(sums_ready, 1)

            pe.wait_ge(rows_loaded, 16 * (len(VECTORS) + 2))
            pe.wait_ge(consts_loaded, 16 * 4)
            nc.tensor.transpose(misc[:, 0:NVEC], rows[0:NVEC, 0:P], ident[0:NVEC, 0:NVEC])
            nc.tensor.transpose(misc[:, P:P + 88], rows[0:88, P:2 * P], ident[0:88, 0:88])
            nc.tensor.transpose(misc[:, P + 88:P + 132], rows[0:44, 2 * P:3 * P], ident[0:44, 0:44]
                                ).then_inc(cols_turned, 1)
            pe.wait_ge(x_loaded, 16 * TC)
            for k in range(DT):
                if k >= RING:
                    bank_free(k)
                for c in range(TC):
                    m = nc.tensor.transpose(ring[k % RING][:, c * P:(c + 1) * P],
                                            fkb[:, c * D + k * P:c * D + (k + 1) * P], ident[:, :])
                m.then_inc(groups_done, 1)

            pe.wait_ge(ones_ready, 1)
            pe.wait_ge(cols_ready, 3)
            sum_norm("pre_mix")

            def up_unit(n, s, g, xg, order=range(DT)):
                unit_ready(n)
                w, wl = slot(whi, s), slot(wlo, s)
                for f in range(2):
                    bank_free(g + f)
                    bank = ring[(2 * s + f) % RING][:, :]
                    for pos, k in enumerate(order):
                        if f == 0 and s == 0:
                            pe.wait_ge(xg_ready, XG[xg] + pos + 1)
                        m = three(bank, w[:, k, f * P:(f + 1) * P], wl[:, k, f * P:(f + 1) * P],
                                  tile(xghi, k), tile(xglo, k), pos == 0, pos == DT - 1)
                    m.then_inc(groups_done, 1)

            with pe.Fori(0, 5) as i:
                for s in range(2):
                    up_unit(i * 2 + s, s, i * 4 + (GB["w_in"] + 2 * s), "w_in")
            for s in range(2):
                unit_ready(10 + s)
                for c in range(TC):
                    g = GB["w_in"] + 20 + 4 * s + c
                    bank_free(g)
                    for k in range(DT):
                        xh = xghi[:, k * T + c * P:k * T + (c + 1) * P]
                        xl = xglo[:, k * T + c * P:k * T + (c + 1) * P]
                        w, wl = slot(whi, s)[:, k, :], slot(wlo, s)[:, k, :]
                        m = three(ring[g % RING][:, 0:UC], xh, xl, w, wl, k == 0, k == DT - 1)
                    m.then_inc(groups_done, 1)
            for s in range(2):
                up_unit(12 + s, s, GB["w_in"] + 28 + 2 * s, "w_in")

            g = GB["levels"]
            for l in range(len(LEVELS) + 1):
                if l == 0:
                    pe.wait_ge(q_silu, 1)
                    pe.wait_ge(decay_act, 4)
                    pe.wait_ge(evacuated, GB["levels"])
                else:
                    pe.wait_ge(level_ready, 2 * l)
                for h in range(HH):
                    bank_free(g)
                    for c in range(TC):
                        at_ = slice((TC * h + c) * P, (TC * h + c + 1) * P)
                        left, right = (fk[:, at_], Q[:, at_]) if l == 0 else (GC[:, at_], GC[:, at_])
                        m = nc.tensor.matmul(ring[g % RING][:, c * P:(c + 1) * P], left, right,
                                             start=True, stop=True)
                    m.then_inc(groups_done, 1)
                    g += 1
            pe.wait_ge(cross_ready, 5)
            for h in range(HH):
                def c_(t, c):
                    return t[:, (TC * h + c) * P:(TC * h + c + 1) * P]
                for pairs in (((GC, 0, 1), (fkb, 0, 2), (fkb, 2, 3)), ((GC, 1, 2), (fkb, 1, 3), (GC, 2, 3))):
                    bank_free(g)
                    for n, (t, i, j) in enumerate(pairs):
                        m = nc.tensor.matmul(ring[g % RING][:, n * P:(n + 1) * P], c_(t, i), c_(lb_, j),
                                             start=True, stop=True)
                    m.then_inc(groups_done, 1)
                    g += 1
            for h in range(HH):
                bank_free(g)
                pe.wait_ge(evacuated, GB["cross"] + 2 * h + 2)
                off = 0
                for i in range(TC):
                    v = V[:, i * 512 + h * P:i * 512 + (h + 1) * P]
                    m = nc.tensor.matmul(ring[h][:, i * P:(i + 1) * P], v,
                                         SD[:, (TC * h + i) * P:(TC * h + i + 1) * P],
                                         start=(i == 0), stop=(i == TC - 1))
                    if i < TC - 1:
                        n = TC - 1 - i
                        nc.tensor.matmul(ring[h][:, (i + 1) * P:T], v,
                                         SC[:, (6 * h + off) * P:(6 * h + off + n) * P], start=False, stop=False)
                        off += n
                m.then_inc(groups_done, 1)
                g += 1
            for h in range(HH):
                pe.wait_ge(osq_ready, h + 1)
                bank_free(g)
                nc.tensor.matmul(ring[h][:, :], ones[:, :], tile(GC, h), start=True, stop=True
                                 ).then_inc(groups_done, 1)
                g += 1

            def project(name, ksplit, hi, lo, ready, base, order=None, unroll=False):
                nk, total = len(ksplit), sum(ksplit)
                order = order or list(range(total))
                for i in steps(pe, 2, unroll):
                    for b in range(2):
                        pos0 = 0
                        for j, kt in enumerate(ksplit):
                            s = (b * nk + j) % 2
                            unit_ready(i * (2 * nk) + (UB[name] + b * nk + j))
                            w, wl = slot(whi, s, kt), slot(wlo, s, kt)
                            for f in range(2):
                                if j == 0:
                                    bank_free(i * 4 + (GB[name] + 2 * b + f))
                                for pos in range(pos0, pos0 + kt):
                                    k = order[pos]
                                    if b == 0 and f == 0:
                                        pe.wait_ge(ready, base + pos + 1)
                                    m = three(ring[2 * b + f][:, :], w[:, k - pos0, f * P:(f + 1) * P],
                                              wl[:, k - pos0, f * P:(f + 1) * P], tile(hi, k), tile(lo, k),
                                              pos == 0, pos == total - 1)
                                if j == nk - 1:
                                    m.then_inc(groups_done, 1)
                            if j < nk - 1:
                                m.then_inc(parts_used, 1)
                            pos0 += kt

            project("w_out", [8], xghi, xglo, xg_ready, XG["w_out"], [4, 5, 6, 7, 0, 1, 2, 3])
            sum_norm("post_mix")

            def ffn(m, norm):
                sum_norm(norm)
                name = f"up{m}"
                with pe.Fori(0, FT // 2) as i:
                    for s in range(2):
                        up_unit(i * 2 + (UB[name] + s), s, i * 4 + (GB[name] + 2 * s), name)
                project(f"down{m}", DOWN, ahi, alo, act_ready, FT * m, unroll=(m == 4))

            ffn(0, "pre_ffn")
            sum_norm("post_ffn")
            ffn(1, "pre0")
            sum_norm("mix0")
            for u in range(2):
                unit_ready(UB["pool"] + u)
                w, wl = slot(whi, u, 4), slot(wlo, u, 4)
                for gg in range(2):
                    for f in range(2):
                        g = GB["pool"] + 4 * u + 2 * gg + f
                        bank_free(g)
                        for kt in range(2):
                            k = 2 * (2 * u + gg) + kt
                            pe.wait_ge(xg_ready, XG["pool"] + k + 1)
                            c = slice(f * P, (f + 1) * P)
                            m = three(ring[g % RING][:, :], w[:, 2 * gg + kt, c], wl[:, 2 * gg + kt, c],
                                      tile(xghi, k), tile(xglo, k), kt == 0, kt == 1)
                        m.then_inc(groups_done, 1)
            ffn(2, "post0")

            def narrow(name, norm):
                sum_norm(norm)
                for u in range(2):
                    unit_ready(UB[name] + u)
                    bank_free(GB[name] + u)
                    w, wl = slot(whi, u, DT, P), slot(wlo, u, DT, P)
                    for k in range(DT):
                        pe.wait_ge(xg_ready, XG[name] + k + 1)
                        m = three(ring[u][:, :], w[:, k, :], wl[:, k, :], tile(xghi, k), tile(xglo, k),
                                  k == 0, k == DT - 1)
                    m.then_inc(groups_done, 1)

            narrow("kv", "kv_pre1")
            pe.wait_ge(small_step, 1)
            nc.tensor.matmul(ring[2][:, :], ones[:, :], kvt[:, 0:T], start=True, stop=True).then_inc(groups_done, 1)
            pe.wait_ge(evacuated, GB["kv"] + 2)
            nc.tensor.matmul(ring[3][:, :], perm[:, :], Ut[:, T:2 * T], start=True, stop=True
                             ).then_inc(groups_done, 1)

            def ffn_again(m):
                name = f"up{m}"
                with pe.Fori(0, FT // 2) as i:
                    for s in range(2):
                        up_unit(i * 2 + (UB[name] + s), s, i * 4 + (GB[name] + 2 * s), name)
                project(f"down{m}", DOWN, ahi, alo, act_ready, FT * m)

            ffn_again(3)
            narrow("dq", "mix1")
            pe.wait_ge(small_step, 3)
            nc.tensor.matmul(ring[2][:, :], ones[:, :], PT[:, 0:T], start=True, stop=False)
            nc.tensor.matmul(ring[2][:, :], ones[:, :], PT[:, T:2 * T], start=False, stop=True
                             ).then_inc(groups_done, 2)
            pe.wait_ge(latent_split, 1 + QR)

            scale_w0 = whi[:, 0:UNIT], wlo[:, 0:UNIT]
            w1 = whi[:, UNIT:2 * UNIT], wlo[:, UNIT:2 * UNIT]
            with pe.Fori(0, QUARTERS) as q:
                gb = GB["attn"]
                unit_ready(q * 2 + UB["attn"])
                for n in range(12):
                    bank_free(q * 16 + (gb + n))
                    bank = ring[n % RING][:, :]
                    x = n % 4
                    c = slice(x * P, (x + 1) * P)
                    if n < 4:
                        m = three(bank, scale_w0[0][:, c], scale_w0[1][:, c], ckhi[:, :], cklo[:, :], True, True)
                    elif n < 8:
                        m = three(bank, ckhi[:, c], cklo[:, c], scale_w0[0][:, 512:1024],
                                  scale_w0[1][:, 512:1024], True, True)
                    else:
                        for kt in range(QR):
                            o = 1024 + kt * 512 + x * P
                            m = three(bank, scale_w0[0][:, o:o + P], scale_w0[1][:, o:o + P],
                                      tile(cqhi, kt), tile(cqlo, kt), kt == 0, kt == QR - 1)
                    m.then_inc(groups_done, 1)
                unit_ready(q * 2 + (UB["attn"] + 1))
                for j in range(2):
                    bank_free(q * 16 + (gb + 12 + j))
                    for kt in range(QR):
                        o = kt * 256 + j * P
                        m = three(ring[j][:, :], w1[0][:, o:o + P], w1[1][:, o:o + P],
                                  tile(cqhi, kt), tile(cqlo, kt), kt == 0, kt == QR - 1)
                    m.then_inc(groups_done, 1)
                for j in range(2):
                    bank_free(q * 16 + (gb + 14 + j))
                    pe.wait_ge(evacuated, q * 16 + (gb + 13 + j))
                    nc.tensor.matmul(ring[2 + j][:, :], perm[:, :], tile(QRr, j), start=True, stop=True
                                     ).then_inc(groups_done, 1)

                def scores(h):
                    if h == 0:
                        pe.wait_ge(evacuated, q * 16 + (gb + 16))
                        pe.wait_ge(qrope_ready, q * 2 + 2)
                    for i in range(TC):
                        if h:
                            pe.wait_ge(exp_ready, q * 16 + (4 * (h - 1) + i + 1))
                        n = (i + 1) * P
                        nc.tensor.matmul(ring[i][:, 0:n], QN[:, h * T + i * P:h * T + (i + 1) * P],
                                         KN[:, h * T:h * T + n], start=True, stop=False)
                        r = (h // 2) * T + i * P
                        nc.tensor.matmul(ring[i][:, 0:n], QRt[:, r:r + P], Tt[:, (h % 2) * T:(h % 2) * T + n],
                                         start=False, stop=False)
                        nc.tensor.matmul(ring[i][:, i * P:n], identb[:, :], causal[:, :],
                                         start=False, stop=True).then_inc(scores_ready, 1)

                scores(0)
                for h in range(4):
                    if h < 3:
                        scores(h + 1)
                    for i in range(TC):
                        pe.wait_ge(probs_ready, q * 16 + (4 * h + i + 1))
                        off = i * (i + 1) // 2
                        for j in range(i + 1):
                            bank, at_ = [(banks[4], i), (banks[5], i - 1), (banks[6], i - 2), (banks[6], 2)][j]
                            m = nc.tensor.transpose(bank[:, at_ * P:(at_ + 1) * P],
                                                    probs(h)[:, (off + j) * P:(off + j + 1) * P], ident[:, :])
                            if i == TC - 1 and j != 2:
                                m.then_inc(turned_ready, 1)
                    if h:
                        pe.wait_ge(outlo_ready, q * 4 + h)
                    seg = 0
                    for j in range(TC):
                        if j == 0:
                            pe.wait_ge(turned_act, q * 8 + (2 * h + 1))
                        elif j == 1:
                            pe.wait_ge(turned_vec, q * 4 + (h + 1))
                        elif j == 2:
                            pe.wait_ge(turned_act, q * 8 + (2 * h + 2))
                        n = (TC - j) * P
                        m = nc.tensor.matmul(banks[7][:, j * P:T], VV[:, j * 512 + h * P:j * 512 + (h + 1) * P],
                                             PT[:, seg:seg + n], start=(j == 0), stop=(j == TC - 1))
                        seg += n
                    m.then_inc(out_ready, 1)
                pe.wait_ge(outlo_ready, q * 4 + 4)
            project("w_o", [8, 8], oThi, oTlo, outlo_ready, 0)
            ffn(4, "post1")
            sum_norm("final")
            g = GB["x_out"]
            for c in range(TC):
                for half in range(2):
                    bank_free(g)
                    for kk in range(4):
                        k = 4 * half + kk
                        if c == 0:
                            pe.wait_ge(normed_out, k + 1)
                        m = nc.tensor.transpose(ring[g % RING][:, kk * P:(kk + 1) * P],
                                                Z[:, k * T + c * P:k * T + (c + 1) * P], ident[:, :])
                    m.then_inc(groups_done, 1)
                    g += 1

        @block.vector
        def _(v):
            def split_lo(n, s):
                v.wait_ge(whi_ready, n + 1)
                c = slice(s * UNIT, (s + 1) * UNIT)
                nc.vector.tensor_tensor(wlo[:, c], raw[:, c], whi[:, c].bitcast(F32), ALU.subtract
                                        ).then_inc(wlo_ready, 1)

            def xg_lo(xg, pos, k, t, gain, w=None):
                v.wait_ge(xghi_ready, XG[xg] + pos + 1)
                hi = tile(xghi, k).bitcast(F32)
                if gain is None:
                    ins = nc.vector.tensor_tensor(tile(xglo, k), t, hi, ALU.subtract)
                else:
                    ins = nc.vector.scalar_tensor_tensor(tile(xglo, k), t, col(gain, k if w is None else w), hi,
                                                         ALU.mult, ALU.subtract)
                ins.then_inc(xg_ready, 1)

            def rstd(name):
                j = NORM[name]
                v.wait_ge(sums_ready, j + 1)
                nc.vector.tensor_scalar(R[:, :], stat[:, :], 1.0 / D, EPS, ALU.mult, ALU.add).then_inc(rstd_part, 1)
                v.wait_ge(root_ready, j + 1)
                nc.vector.reciprocal(R[:, :], R[:, :]).then_inc(rstd_ready, 1)
                v.wait_ge(rstd_ready, j + 1)

            v.wait_ge(cols_turned, 1)
            nc.vector.tensor_copy(cols[:, :], misc[:, 0:NVEC]).then_inc(cols_ready, 1)
            nc.vector.tensor_copy(cw[:, 0:88], misc[:, P:P + 88]).then_inc(cols_ready, 1)
            nc.vector.tensor_copy(cw[:, 88:132], misc[:, P + 88:P + 132]).then_inc(cols_ready, 1)
            v.wait_ge(consts_loaded, 16 * 4)
            nc.vector.tensor_copy(identb[:, :], ident[:, :])
            nc.vector.tensor_copy(causal[:, :], wide_causal[:, :])
            nc.vector.tensor_copy(masks[:, :], wide_masks[:, :]).then_inc(masks_ready, 1)
            for k in range(DT):
                v.wait_ge(groups_done, k + 1)
                nc.vector.tensor_copy(tile(xT, k), ring[k % RING][:, :]).then_inc(evacuated, 1)
            split_lo(0, 0)
            split_lo(1, 1)
            v.wait_ge(cols_ready, 3)
            for k in range(DT):
                xg_lo("w_in", k, k, tile(xT, k), "pre_mix_g")
            v.wait_ge(rcol_sums, 1)
            nc.vector.tensor_scalar(rcol[:, :], misc[:, 0:TC], 1.0 / D, EPS, ALU.mult, ALU.add).then_inc(rcol_part, 1)
            v.wait_ge(small_root, 1)
            nc.vector.reciprocal(rcol[:, :], rcol[:, :]).then_inc(rcol_ready, 1)
            rstd("pre_mix")

            g = GB["w_in"]
            dests = [fk, Q[:, :], GC[:, :], CH[:, :], GBt[:, :], None, G[:, :]]
            mixb_steps = [0]

            def after_mixb():
                v.wait_ge(mixb_part, mixb_steps[0])

            def mixb_step(ins):
                ins.then_inc(mixb_part, 1)
                mixb_steps[0] += 1

            def conv_tile(k):
                m, c, b = tile(GC, k), tile(CH, k), tile(GBt, k)
                mixb_step(nc.vector.tensor_tensor(m, m, c, ALU.mult))
                after_mixb()
                mixb_step(nc.vector.tensor_scalar(c, m, col("conv_w", 8 + k), None, ALU.mult))
                after_mixb()
                mixb_step(nc.vector.scalar_tensor_tensor(c[:, 1:T], m[:, 0:T - 1], col("conv_w", 4 + k), c[:, 1:T],
                                                         ALU.mult, ALU.add))
                after_mixb()
                mixb_step(nc.vector.scalar_tensor_tensor(c[:, 2:T], m[:, 0:T - 2], col("conv_w", k), c[:, 2:T],
                                                         ALU.mult, ALU.add))
                after_mixb()
                nc.vector.tensor_tensor(b, b, c, ALU.mult).then_inc(mixb_ready, 1)

            for n in range(14):
                s = n % 2
                if n in (10, 11):
                    if n == 10:
                        v.wait_ge(rcol_ready, 1)
                    for c in range(TC):
                        v.wait_ge(groups_done, g + 1)
                        nc.vector.tensor_scalar(V[:, c * 512 + s * UC:c * 512 + (s + 1) * UC],
                                                ring[g % RING][:, 0:UC], rcol[:, c:c + 1], float(P) ** -0.5,
                                                ALU.mult, ALU.mult).then_inc(evacuated, 1)
                        g += 1
                else:
                    for f in range(2):
                        v.wait_ge(groups_done, g + 1)
                        nc.vector.tensor_tensor(tile(dests[n // 2], 2 * s + f), ring[g % RING][:, :], R[:, :],
                                                ALU.mult).then_inc(evacuated, 1)
                        g += 1
                split_lo(n + 2, s)
                if n == 4:
                    v.wait_ge(decay_act, 3)
                    nc.vector.scalar_tensor_tensor(lb_, fk, 0.0, lb_, ALU.min, ALU.subtract).then_inc(decay_vec, 1)
                    v.wait_ge(decay_vec, 1)
                    nc.vector.tensor_tensor(fk, lb_, fk, ALU.subtract).then_inc(decay_vec, 1)
                    v.wait_ge(decay_vec, 2)
                    v.wait_ge(ones_ready, 1)
                    for c in range(HH * TC):
                        b = lb_[:, c * P:(c + 1) * P]
                        nc.vector.tensor_tensor_scan(b, ones[:, :], b, 0.0, ALU.mult, ALU.add
                                                     ).then_inc(decay_vec, 1)
                if n in (10, 11, 12, 13):
                    v.wait_ge(evacuated, GB["w_in"] + 20)
                    conv_tile(n - 10)

            for k in range(4):
                xg_lo("w_out", k, 4 + k, tile(GBt, k), None)
            v.wait_ge(decay_vec, 2 + HH * TC)
            nc.vector.memset(SD[:, :], 0.0).then_inc(scores_cleared, 1)
            v.wait_ge(scores_cleared, 1)
            v.wait_ge(masks_ready, 1)
            g = GB["levels"]
            mask = masks[:, :].rearrange("p (l t) -> p l t", l=8)

            def take(l, g):
                v.wait_ge(evacuated, g)
                for h in range(HH):
                    v.wait_ge(groups_done, g + 1)
                    nc.vector.copy_predicated(
                        SD[:, h * TC * P:(h + 1) * TC * P].rearrange("p (c t) -> p c t", c=TC),
                        mask[:, l:l + 1, :].to_broadcast([P, TC, P]),
                        ring[h][:, :].rearrange("p (c t) -> p c t", c=TC)).then_inc(evacuated, 1)
                    g += 1
                return g

            for l, hs in enumerate(LEVELS):
                def halves(t):
                    x = t.rearrange("p (n two h) -> p n two h", two=2, h=hs)
                    return x[:, :, 0, :], x[:, :, 1, :]
                bl, br = halves(lb_)
                ref = bl[:, :, hs - 1:hs].to_broadcast([P, 2048 // (2 * hs), hs])
                el, er = halves(CH[:, :])
                kl, _ = halves(fk)
                _, qr = halves(Q[:, :])
                gl, gr = halves(GC[:, :])
                if l == 0:
                    v.wait_ge(mixb_ready, 4)
                else:
                    v.wait_ge(level_ready, 2 * l)
                nc.vector.tensor_tensor(el, ref, bl, ALU.subtract).then_inc(level_arg, 1)
                nc.vector.tensor_tensor(er, br, ref, ALU.subtract).then_inc(level_arg, 1)
                g = take(l, g)
                v.wait_ge(level_exp, l + 1)
                nc.vector.tensor_tensor(gl, el, kl, ALU.mult).then_inc(level_ready, 1)
                nc.vector.tensor_tensor(gr, er, qr, ALU.mult).then_inc(level_ready, 1)
            b3 = lb_.rearrange("p (c t) -> p c t", t=P)
            e3 = CH[:, :].rearrange("p (c t) -> p c t", t=P)
            v.wait_ge(level_ready, 2 * len(LEVELS))
            nc.vector.tensor_tensor(e3, b3[:, :, P - 1:P].to_broadcast([P, HH * TC, P]), b3, ALU.subtract
                                    ).then_inc(cross_arg, 1)
            g = take(len(LEVELS), g)
            v.wait_ge(cross_exp, 1)
            nc.vector.tensor_tensor(GC[:, :], CH[:, :], fk, ALU.mult).then_inc(cross_ready, 1)
            v.wait_ge(cross_exp, 3)
            nc.vector.tensor_tensor(lb_, lb_, Q[:, :], ALU.mult).then_inc(cross_ready, 1)
            v.wait_ge(cross_ready, 1)
            ge = GC[:, :].rearrange("p (h c t) -> p h c t", h=HH, c=TC)
            fe = fk.rearrange("p (h c t) -> p h c t", h=HH, c=TC)
            en = ends[:, :].rearrange("p (h c) -> p h c", h=HH)
            for dst, src, c, e, after in ((0, ge, 0, 1, 1), (1, ge, 1, 2, 1), (2, fe, 0, 2, 3)):
                v.wait_ge(cross_ready, after)
                nc.vector.tensor_tensor(fe[:, :, dst, :], src[:, :, c, :],
                                        en[:, :, e:e + 1].to_broadcast([P, HH, P]), ALU.mult
                                        ).then_inc(cross_ready, 1)
            for h in range(HH):
                for part in range(2):
                    v.wait_ge(groups_done, g + 1)
                    o = (6 * h + 3 * part) * P
                    nc.vector.tensor_copy(SC[:, o:o + 3 * P], ring[g % RING][:, 0:3 * P]).then_inc(evacuated, 1)
                    g += 1
            for h in range(HH):
                v.wait_ge(groups_done, g + 1)
                nc.vector.tensor_copy(tile(CH, h), ring[h][:, :]).then_inc(evacuated, 1)
                g += 1
                v.wait_ge(evacuated, g)
                nc.vector.tensor_tensor(tile(GC, h), tile(CH, h), tile(CH, h), ALU.mult).then_inc(osq_ready, 1)
            for h in range(HH):
                v.wait_ge(groups_done, g + 1)
                nc.vector.tensor_scalar(tile(GC, h), ring[h][:, :], 1.0 / P, EPS, ALU.mult, ALU.add
                                        ).then_inc(evacuated, 1)
                g += 1
            v.wait_ge(q_silu, 2)
            for h in range(HH):
                o, r = tile(CH, h), tile(GC, h)
                v.wait_ge(small_root, 2 + h)
                nc.vector.reciprocal(r, r).then_inc(head_part, 1)
                v.wait_ge(head_part, 2 * h + 1)
                nc.vector.tensor_tensor(o, o, r, ALU.mult).then_inc(head_part, 1)
                v.wait_ge(head_part, 2 * h + 2)
                nc.vector.scalar_tensor_tensor(o, o, col("hgrn_norm_g", h), tile(G, h), ALU.mult, ALU.mult
                                               ).then_inc(mixa_ready, 1)
                xg_lo("w_out", 4 + h, h, o, None)

            def project(name, ksplit, dst, factor=None, xg=None, gain=None, goff=0, unroll=False):
                nk = len(ksplit)
                for i in steps(v, 2, unroll):
                    for b in range(2):
                        def ahead(j):
                            n = i * (2 * nk) + (UB[name] + b * nk + j + 2)
                            if not (unroll and n >= UNITS):
                                split_lo(n, (b * nk + j) % 2)
                        for j in range(nk - 1):
                            ahead(j)
                        for f in range(2):
                            gr = 2 * b + f
                            t = tile(dst, i * 4 + gr)
                            v.wait_ge(groups_done, i * 4 + (GB[name] + gr + 1))
                            if factor is None:
                                ins = nc.vector.tensor_copy(t, ring[gr][:, :])
                            else:
                                ins = nc.vector.scalar_tensor_tensor(t, ring[gr][:, :], factor, t,
                                                                     ALU.mult, ALU.add)
                            ins.then_inc(evacuated, 1)
                        ahead(nk - 1)
                        if xg:
                            for f in range(2):
                                k = i * 4 + (2 * b + f)
                                xg_lo(xg, k, k, tile(dst, k), gain, k + goff)

            def add_normed(y, gain, first, xg, next_gain):
                for k in range(DT + 2):
                    if k < DT:
                        nc.vector.scalar_tensor_tensor(tile(y, k), tile(y, k), col(gain, k), R[:, :],
                                                       ALU.mult, ALU.mult).then_inc(resid_part, 1)
                    if 1 <= k <= DT:
                        v.wait_ge(resid_part, first + k)
                        nc.vector.tensor_tensor(tile(xT, k - 1), tile(xT, k - 1), tile(y, k - 1), ALU.add
                                                ).then_inc(resid_ready, 1)
                    if k >= 2:
                        xg_lo(xg, k - 2, k - 2, tile(xT, k - 2), next_gain)

            project("w_out", [8], Y0)
            rstd("post_mix")
            add_normed(Y0, "post_mix_g", 0, "up0", "pre_ffn_g")

            def up(m, conv=False):
                name = f"up{m}"
                gb, hb = GB[name], FT * m
                with v.Fori(0, FT // 2) as i:
                    def conv_rest(f, half, dst):
                        n = 2 * half + f
                        u = tile(Ut, f)
                        v.wait_ge(tap_ready, i * 4 + (n + 1))
                        for tap, sh, signal in ((1, 1, conv_part), (0, 2, conv_ready)):
                            c = i * 2 + (tap * 2 * FT + half * FT + f)
                            if sh == 2:
                                v.wait_ge(conv_part, i * 4 + (n + 1))
                            nc.vector.scalar_tensor_tensor(dst[:, sh:T], u[:, 0:T - sh], cw[:, bass.ds(c, 1)],
                                                           dst[:, sh:T], ALU.mult, ALU.add).then_inc(signal, 1)
                    for f in range(2):
                        v.wait_ge(groups_done, i * 4 + (gb + f + 1))
                        nc.vector.tensor_tensor(tile(Ut if conv else Tt, f), ring[f][:, :], R[:, :], ALU.mult
                                                ).then_inc(evacuated, 1)
                    if conv:
                        for f in range(2):
                            conv_rest(f, 0, tile(Tt, f))
                    split_lo(i * 2 + (UB[name] + 2), 0)
                    if conv:
                        v.wait_ge(conv_ready, i * 4 + 2)
                    for f in range(2):
                        v.wait_ge(groups_done, i * 4 + (gb + f + 3))
                        nc.vector.tensor_tensor(tile(Ut if conv else At, f), ring[2 + f][:, :], R[:, :], ALU.mult
                                                ).then_inc(evacuated, 1)
                    for f in range(2):
                        if conv:
                            conv_rest(f, 1, tile(At, f))
                            v.wait_ge(conv_ready, i * 4 + (f + 3))
                        else:
                            v.wait_ge(evacuated, i * 4 + (gb + f + 3))
                        v.wait_ge(silu_ready, i * 2 + (hb + f + 1))
                        nc.vector.tensor_tensor(tile(At, f), tile(At, f), tile(Tt, f), ALU.mult
                                                ).then_inc(gated_ready, 1)
                    for f in range(2):
                        v.wait_ge(ahi_ready, i * 2 + (hb + f + 1))
                        nc.vector.tensor_tensor(tile(alo, i * 2 + f), tile(At, f),
                                                tile(ahi, i * 2 + f).bitcast(F32), ALU.subtract
                                                ).then_inc(act_ready, 1)
                    v.wait_ge(act_ready, i * 2 + (hb + 2))
                    split_lo(i * 2 + (UB[name] + 3), 1)

            rstd("pre_ffn")
            up(0, conv=True)
            project("down0", DOWN, Y1)
            rstd("post_ffn")
            add_normed(Y1, "post_ffn_g", DT, "up1", "ffn_pre_norm_2")
            rstd("pre0")
            up(1)
            project("down1", DOWN, xT, 0.5)
            nc.vector.memset(PU[:, :].rearrange("p (k t) -> p k t", t=PW)[:, :, 0:16], 0.0).then_inc(pool_step, 1)
            for t in (PA, PB):
                nc.vector.memset(t[:, :].rearrange("p (k t) -> p k t", t=PW)[:, :, 0:16], 0.0).then_inc(pool_step, 1)
            pool_steps = [3]

            def pool_do(ins):
                ins.then_inc(pool_step, 1)
                pool_steps[0] += 1

            rstd("mix0")
            v.wait_ge(inv_loaded, 16)
            for k in range(DT):
                pool_do(nc.vector.scalar_tensor_tensor(PU[:, k * PW + 16:(k + 1) * PW], tile(xT, k),
                                                       col("mix_norm_2", k), R[:, :], ALU.mult, ALU.mult))
            for w in range(4):
                u = PU[:, 2 * w * PW:2 * (w + 1) * PW].rearrange("p (k t) -> p k t", t=PW)
                cur = u
                v.wait_ge(xg_ready, XG["pool"] + 2 * w)
                for step in range(w + 1):
                    dst = (PA, PB)[step % 2][:, :].rearrange("p (k t) -> p k t", t=PW)
                    back = 1 << step
                    v.wait_ge(pool_step, pool_steps[0])
                    pool_do(nc.vector.tensor_tensor(dst[:, :, 16:PW], cur[:, :, 16:PW], cur[:, :, 16 - back:PW - back],
                                                    ALU.add))
                    cur = dst
                body = cur[:, :, 16:PW]
                v.wait_ge(pool_step, pool_steps[0])
                count = inv[:, w * T:(w + 1) * T].rearrange("p (k t) -> p k t", k=1).to_broadcast([P, 2, T])
                pool_do(nc.vector.tensor_tensor(body, body, count, ALU.mult))
                v.wait_ge(pool_step, pool_steps[0])
                nc.vector.tensor_tensor(body, body, u[:, :, 16:PW], ALU.subtract).then_inc(pool_ready, 1)
                for kt in range(2):
                    xg_lo("pool", 2 * w + kt, 2 * w + kt, cur[:, kt, 16:PW], None)
            for u in range(2):
                for n in range(4):
                    k = 4 * u + n
                    v.wait_ge(groups_done, GB["pool"] + k + 1)
                    nc.vector.scalar_tensor_tensor(tile(xT, k), ring[n][:, :], col("pool_scale_2", k), tile(xT, k),
                                                   ALU.mult, ALU.add).then_inc(evacuated, 1)
                split_lo(UB["pool"] + u + 2, u)
            for k in range(DT):
                xg_lo("up2", k, k, tile(xT, k), "ffn_post_norm_2")
            rstd("post0")
            up(2)
            project("down2", DOWN, xT, 0.5, "kv", "kv_in_norm_2")
            rstd("kv_pre1")
            g = GB["kv"]
            ck, krope = Ut[:, 0:T], Ut[:, T:2 * T]
            k0, k1 = kvt[:, 0:T], kvt[:, T:2 * T]
            v.wait_ge(groups_done, g + 1)
            nc.vector.tensor_tensor(ck, ring[0][:, :], R[:, :], ALU.mult).then_inc(evacuated, 1)
            split_lo(UB["kv"] + 2, 0)
            v.wait_ge(evacuated, g + 1)
            nc.vector.tensor_tensor(k0, ck, ck, ALU.mult).then_inc(small_step, 1)
            v.wait_ge(groups_done, g + 2)
            nc.vector.tensor_tensor(krope, ring[1][:, :], R[:, :], ALU.mult).then_inc(evacuated, 1)
            split_lo(UB["kv"] + 3, 1)
            v.wait_ge(groups_done, g + 3)
            nc.vector.tensor_scalar(k1, ring[2][:, :], 1.0 / P, EPS, ALU.mult, ALU.add).then_inc(evacuated, 1)
            v.wait_ge(small_root, 6)
            nc.vector.reciprocal(k1, k1).then_inc(ck_ready, 1)
            v.wait_ge(ck_ready, 1)
            nc.vector.scalar_tensor_tensor(ck, ck, col("ckv_norm_2", 0), k1, ALU.mult, ALU.mult).then_inc(ck_ready, 1)
            v.wait_ge(rope_kv_loaded, 16)
            v.wait_ge(groups_done, g + 4)
            nc.vector.tensor_tensor(k0, ring[3][:, :], rope_kv[:, T:2 * T], ALU.mult).then_inc(evacuated, 1)
            nc.vector.tensor_tensor(krope, krope, rope_kv[:, 0:T], ALU.mult).then_inc(ck_ready, 1)
            v.wait_ge(ck_ready, 3)
            v.wait_ge(evacuated, g + 4)
            nc.vector.tensor_tensor(krope, krope, k0, ALU.add).then_inc(ck_ready, 1)
            for k in range(DT):
                xg_lo("up3", k, k, tile(xT, k), "ffn_pre_norm_2", 8 + k)
            up(3)
            project("down3", DOWN, xT, 0.5, "dq", "mix_norm_2", 8)
            rstd("mix1")
            g = GB["dq"]
            for u in range(2):
                v.wait_ge(groups_done, g + u + 1)
                nc.vector.tensor_tensor(tile(At, u), ring[u][:, :], R[:, :], ALU.mult).then_inc(evacuated, 1)
                split_lo(UB["dq"] + u + 2, u)
                v.wait_ge(evacuated, g + u + 1)
                nc.vector.tensor_tensor(tile(PT, u), tile(At, u), tile(At, u), ALU.mult).then_inc(small_step, 1)
            nc.vector.memset(Tt[64:128, 0:T], 0.0)
            nc.vector.memset(Tt[0:64, T:2 * T], 0.0)
            v.wait_ge(ck_ready, 4)
            nc.vector.tensor_copy(Tt[0:64, 0:T], Ut[0:64, T:2 * T])
            nc.vector.tensor_copy(Tt[64:128, T:2 * T], Ut[64:128, T:2 * T]).then_inc(latent_ready, 1)
            v.wait_ge(groups_done, g + 4)
            r = tile(PT, 0)
            nc.vector.tensor_scalar(r, ring[2][:, :], 1.0 / (QR * P), EPS, ALU.mult, ALU.add).then_inc(evacuated, 2)
            v.wait_ge(small_root, 7)
            nc.vector.reciprocal(r, r).then_inc(ck_ready, 1)
            v.wait_ge(ck_ready, 5)
            for u in range(2):
                nc.vector.scalar_tensor_tensor(tile(At, u), tile(At, u), col("q_lora_norm_2", u), r,
                                               ALU.mult, ALU.mult).then_inc(latent_ready, 1)
            for j in range(1 + QR):
                v.wait_ge(latent_hi, j + 1)
                hi = ckhi[:, :] if j == 0 else tile(cqhi, j - 1)
                lo = cklo[:, :] if j == 0 else tile(cqlo, j - 1)
                src = Ut[:, 0:T] if j == 0 else tile(At, j - 1)
                nc.vector.tensor_tensor(lo, src, hi.bitcast(F32), ALU.subtract).then_inc(latent_split, 1)

            scale = float((NOPE + ROPE) ** -0.5)
            v.wait_ge(rope_q_loaded, 16)
            gb = GB["attn"]
            with v.Fori(0, QUARTERS) as q:
                for n in range(12):
                    v.wait_ge(groups_done, q * 16 + (gb + n + 1))
                    dst = (KN, VV, QN)[n // 4]
                    nc.vector.tensor_copy(tile(dst, n % 4), ring[n % RING][:, :]).then_inc(evacuated, 1)
                split_lo(q * 2 + (UB["attn"] + 2), 0)
                for j in range(2):
                    v.wait_ge(groups_done, q * 16 + (gb + 13 + j))
                    nc.vector.tensor_copy(tile(QRr, j), ring[j][:, :]).then_inc(evacuated, 1)
                split_lo(q * 2 + (UB["attn"] + 3), 1)
                for j in range(2):
                    v.wait_ge(groups_done, q * 16 + (gb + 15 + j))
                    nc.vector.tensor_tensor(tile(QRt, j), ring[2 + j][:, :], rope_q[:, T:2 * T], ALU.mult
                                            ).then_inc(evacuated, 1)
                    nc.vector.tensor_tensor(tile(QRr, j), tile(QRr, j), rope_q[:, 0:T], ALU.mult
                                            ).then_inc(qrope_part, 1)
                    v.wait_ge(qrope_part, q * 2 + (j + 1))
                    v.wait_ge(evacuated, q * 16 + (gb + 15 + j))
                    nc.vector.tensor_tensor(tile(QRt, j), tile(QRt, j), tile(QRr, j), ALU.add
                                            ).then_inc(qrope_ready, 1)

                def maxes(h):
                    for i in range(TC):
                        e, c = 4 * h + i, 4 * (h % 2) + i
                        v.wait_ge(scores_ready, q * 16 + (e + 1))
                        nc.vector.tensor_reduce(rowmax[:, c:c + 1], ring[i][:, 0:(i + 1) * P], AX_X, ALU.max
                                                ).then_inc(max_part, 1)
                        v.wait_ge(max_part, q * 16 + (e + 1))
                        nc.vector.tensor_scalar(negmax[:, c:c + 1], rowmax[:, c:c + 1], -scale, None, ALU.mult
                                                ).then_inc(negmax_ready, 1)

                def normalise(h):
                    c0 = 4 * (h % 2)
                    v.wait_ge(exp_ready, q * 16 + (4 * h + 4))
                    nc.vector.reciprocal(rowinv[:, c0:c0 + 4], rowsum[:, c0:c0 + 4]).then_inc(recip_ready, 1)
                    v.wait_ge(recip_ready, q * 4 + (h + 1))
                    for i in range(TC):
                        off = i * (i + 1) // 2 * P
                        pr = probs(h)[:, off:off + (i + 1) * P]
                        nc.vector.tensor_scalar(pr, pr, rowinv[:, c0 + i:c0 + i + 1], None, ALU.mult
                                                ).then_inc(probs_ready, 1)

                maxes(0)
                normalise(0)
                for h in range(4):
                    if h < 3:
                        maxes(h + 1)
                    v.wait_ge(turned_ready, q * 12 + (3 * h + 2))
                    nc.vector.tensor_copy(PT[:, 4 * P:7 * P], banks[5][:, 0:3 * P]).then_inc(turned_vec, 1)
                    if h < 3:
                        normalise(h + 1)
                    v.wait_ge(outhi_ready, q * 4 + (h + 1))
                    nc.vector.tensor_tensor(tile(oTlo, q * 4 + h), banks[7][:, :],
                                            tile(oThi, q * 4 + h).bitcast(F32), ALU.subtract
                                            ).then_inc(outlo_ready, 1)
            project("w_o", [8, 8], xT, 1.0, "up4", "ffn_post_norm_2", 8)
            rstd("post1")
            up(4)
            project("down4", DOWN, xT, 0.5, unroll=True)
            rstd("final")
            for k in range(DT):
                nc.vector.scalar_tensor_tensor(tile(Z, k), tile(xT, k), col("final_norm_2", k), R[:, :],
                                               ALU.mult, ALU.mult).then_inc(normed_out, 1)
            g = GB["x_out"]
            for n in range(2 * TC):
                v.wait_ge(groups_done, g + n + 1)
                nc.vector.tensor_copy(ob[:, n * T:(n + 1) * T], ring[n % RING][:, :]).then_inc(evacuated, 1)


def constants():
    import numpy as np

    s, t = np.arange(P)[:, None], np.arange(P)[None, :]
    masks = [s == t]
    for h in LEVELS:
        masks.append((s // (2 * h) == t // (2 * h)) & (s % (2 * h) < h) & (t % (2 * h) >= h))
    perm = np.zeros((P, P), np.float32)
    for m in range(P):
        if m % ROPE < ROPE // 2:
            perm[m + ROPE // 2, m] = -1.0
        else:
            perm[m - ROPE // 2, m] = 1.0
    freq = np.float32(10000.0) ** (-np.arange(0, ROPE, 2, dtype=np.float32) / np.float32(ROPE))
    ang = (np.arange(T, dtype=np.float32)[None, :] * freq[:, None]).astype(np.float32)
    rope = np.concatenate([np.tile(np.cos(ang), (4, 1)), np.tile(np.sin(ang), (4, 1))], 1).astype(np.float32)
    count = np.stack([1.0 / np.minimum(np.arange(1, T + 1), w) for w in (2, 4, 8, 16)])
    return {
        "ident": np.eye(P, dtype=np.float32), "perm": perm,
        "causal": np.where(t <= s, 0.0, -1e30).astype(np.float32),
        "masks": np.concatenate([m.astype(np.int32) for m in masks], 1),
        "rope": rope, "inv_count": count.astype(np.float32).reshape(1, 4 * T),
    }


_INS = ["x", "lb_param", "w_in", "w_out", "conv_w", "ffn_w_up", "ffn_conv_w", "ffn_w_down", "hgrn_norm_g",
        "pre_mix_g", "post_mix_g", "pre_ffn_g", "post_ffn_g", "ffn_pre_norm_2", "ffn_pre_wg_2", "ffn_pre_wu_2",
        "ffn_pre_wd_2", "mix_norm_2", "ffn_post_norm_2", "ffn_post_wg_2", "ffn_post_wu_2", "ffn_post_wd_2",
        "pool_w_2", "pool_scale_2", "kv_in_norm_2", "w_dkv_2", "ckv_norm_2", "w_uk_2", "w_uv_2",
        "q_lora_norm_2", "w_dq_2", "w_uq_2", "w_o_2", "final_norm_2"]


def kernel(**inputs):
    import numpy as _np
    import concourse.bacc as _bacc
    from concourse import mybir as _mybir
    from concourse.bass_utils import run_bass_kernel_spmd as _run

    nc = _bacc.Bacc("TRN2", target_bir_lowering=False, num_devices=1)
    arrays, args = {}, {}
    given = {name: inputs[name] for name in _INS}
    given.update(constants())
    for name, value in given.items():
        a = _np.ascontiguousarray(value)
        arrays[f"in_{name}_dram"] = a
        args[name] = nc.dram_tensor(f"in_{name}_dram", a.shape, _mybir.dt.from_np(a.dtype),
                                    kind="ExternalInput").ap()
    out = nc.dram_tensor("out_0_dram", (1, T, D), _mybir.dt.float32, kind="ExternalOutput").ap()
    build(nc, args, out)
    r = _run(nc, [arrays], core_ids=[0])
    return r.results[0]["out_0_dram"]
```

```python
from contextlib import ExitStack

import concourse.bass as bass
from concourse import mybir

F32 = mybir.dt.float32
F32R = mybir.dt.float32r
BF16 = mybir.dt.bfloat16
U8 = mybir.dt.uint8
ACT = mybir.ActivationFunctionType
ALU = mybir.AluOpType
AX_X = mybir.AxisListType.X

P = 128
T = 512
D = 1024
DT = D // P
FF = 2816
FT = FF // P
TC = T // P
UC = 256
UNIT = DT * UC
HH = 4
NH = 16
NOPE = 128
ROPE = 64
QR = 2
EPS = 1e-6
RING = 4
LEVELS = [1, 2, 4, 8, 16, 32, 64]
QUARTERS = 4
DOWN = [8, 8, 6]

VECTORS = [("pre_mix_g", 8), ("post_mix_g", 8), ("pre_ffn_g", 8), ("post_ffn_g", 8),
           ("ffn_pre_norm_2", 16), ("mix_norm_2", 16), ("ffn_post_norm_2", 16), ("pool_scale_2", 8),
           ("kv_in_norm_2", 8), ("ckv_norm_2", 1), ("q_lora_norm_2", 2), ("final_norm_2", 8),
           ("hgrn_norm_g", 4), ("conv_w", 12)]
COL = {}
_at = 0
for _name, _n in VECTORS:
    COL[_name] = _at
    _at += _n
NVEC = _at

PHASES = [("x_in", 0, 8), ("w_in", 14, 64), ("cross", 0, 8), ("state_out", 0, 4), ("w_out", 4, 8), ("up0", 22, 44), ("down0", 12, 8),
          ("up1", 22, 44), ("down1", 12, 8), ("pool", 2, 8), ("up2", 22, 44), ("down2", 12, 8),
          ("kv", 2, 4), ("up3", 22, 44), ("down3", 12, 8), ("dq", 2, 4), ("attn", 8, 64),
          ("w_o", 8, 8), ("up4", 22, 44), ("down4", 12, 8), ("x_out", 0, 8)]
UB, GB = {}, {}
_u = _g = 0
for _name, _nu, _ng in PHASES:
    UB[_name], GB[_name] = _u, _g
    _u += _nu
    _g += _ng
UNITS = _u
MB, _m = {}, 0
for _name, _nk in [("w_out", 1), ("down0", 3), ("down1", 3), ("down2", 3), ("down3", 3), ("w_o", 2), ("down4", 3)]:
    MB[_name] = _m
    _m += 4 * (_nk - 1)

XG = {n: 8 * j for j, n in enumerate(["w_in", "w_out", "up0", "up1", "pool", "up2", "kv", "up3", "dq", "up4"])}
NORM = {n: j for j, n in enumerate(["pre_mix", "post_mix", "pre_ffn", "post_ffn", "pre0", "mix0", "post0",
                                    "kv_pre1", "mix1", "post1", "final"])}


def steps(eng, n, unroll=False):
    if unroll:
        for i in range(n):
            yield i
    else:
        with eng.Fori(0, n) as i:
            yield i


def build(nc, A, out):
    ctx = ExitStack()
    with ctx:
        def sb(name, shape, dt=F32, where=ctx):
            return where.enter_context(nc.sbuf_tensor(name, shape, dt))

        def sem(name):
            return ctx.enter_context(nc.semaphore(name))

        xT = sb("xT", [P, DT * T])
        raw = sb("raw", [P, 2 * UNIT])
        whi = sb("whi", [P, 2 * UNIT], F32R)
        wlo = sb("wlo", [P, 2 * UNIT], F32R)
        R = sb("R", [P, T])
        acc = sb("acc", [P, T])
        sq = sb("sq", [P, 2 * T])
        work = sb("work", [P, 6 * T])
        Tt, At, Ut = (work[:, 2 * j * T:2 * (j + 1) * T] for j in range(3))
        cols = sb("cols", [P, NVEC])
        cw = sb("cw", [P, 3 * 2 * FT])
        ident = sb("ident", [P, P])
        ones = sb("ones", [P, P])
        eps = sb("eps", [P, 1])
        perm = sb("perm", [P, P])
        identb = sb("identb", [P, P], BF16)
        causal = sb("causal", [P, P], BF16)
        rcol = sb("rcol", [P, TC])
        ends = sb("ends", [P, HH * TC])
        rowmax = sb("rowmax", [P, 8])
        negmax = sb("negmax", [P, 8])
        rowinv = sb("rowinv", [P, 8])
        rowsum = sb("rowsum", [P, 8])
        flex = ExitStack()
        xghi = sb("xghi", [P, DT * T], F32R, flex)
        xglo = sb("xglo", [P, DT * T], F32R, flex)
        act = ExitStack()
        ahi = sb("ahi", [P, FT * T], F32R, act)
        alo = sb("alo", [P, FT * T], F32R, act)
        act.close()
        hg = ExitStack()
        fkb = sb("fkb", [P, 2 * 2048], F32, hg)
        Q = sb("Q", [P, 2048], F32, hg)
        V = sb("V", [P, TC * 512], F32, hg)
        G = sb("G", [P, 2048], F32, hg)
        GBt = sb("GBt", [P, 2048], F32, hg)
        GC = sb("GC", [P, 2048], F32, hg)
        CH = sb("CH", [P, 2048], F32, hg)
        SD = sb("SD", [P, HH * TC * P], F32, hg)
        SC = sb("SC", [P, HH * 6 * P], F32, hg)
        masks = sb("masks", [P, 8 * P], U8, hg)
        LG, EX = SC[:, 0:2048], V[:, :]
        hg.close()
        yb = ExitStack()
        Y0 = sb("Y0", [P, DT * T], F32, yb)
        rows = sb("rows", [P, 3 * P], F32, yb)
        wide_causal = sb("wide_causal", [P, P], F32, yb)
        wide_masks = sb("wide_masks", [P, 8 * P], mybir.dt.int32, yb)
        yb.close()
        pl = ExitStack()
        PW = 16 + T
        PU = sb("PU", [P, DT * PW], F32, pl)
        PA = sb("PA", [P, 2 * PW], F32, pl)
        PB = sb("PB", [P, 2 * PW], F32, pl)
        inv = sb("inv", [P, 4 * 16], F32, pl)
        PE16 = sb("PE16", [P, 2 * 16], F32, pl)
        pl.close()
        kv = ExitStack()
        rope_kv = sb("rope_kv", [P, 2 * T], F32, kv)
        kvt = sb("kvt", [P, 2 * T], F32, kv)
        kv.close()
        fin = ExitStack()
        Z = sb("Z", [P, DT * T], F32, fin)
        ob = sb("ob", [P, TC * D], F32, fin)
        fin.close()
        flex.close()
        f2 = ExitStack()
        Y1 = sb("Y1", [P, DT * T], F32, f2)
        f2.close()
        at = ExitStack()
        KN = sb("KN", [P, 4 * T], F32, at)
        QN = sb("QN", [P, 4 * T], F32, at)
        VV = sb("VV", [P, TC * 512], F32, at)
        QRt = sb("QRt", [P, 2 * T], F32, at)
        Prb = sb("Prb", [P, 10 * P], F32, at)
        oThi = sb("oThi", [P, NH * T], F32R, at)
        oTlo = sb("oTlo", [P, NH * T], F32R, at)
        rope_q = sb("rope_q", [P, 2 * T], F32, at)
        ckhi = sb("ckhi", [P, T], F32R, at)
        cklo = sb("cklo", [P, T], F32R, at)
        cqhi = sb("cqhi", [P, QR * T], F32R, at)
        cqlo = sb("cqlo", [P, QR * T], F32R, at)
        PT = sb("PT", [P, 10 * P], F32, at)
        at.close()
        QRr = Prb[:, 0:2 * T]

        def probs(h):
            return work[:, 2 * T:2 * T + 10 * P] if h % 2 == 0 else Prb[:, :]

        banks = [ctx.enter_context(nc.psum_tensor(f"bank{b}", [P, 512], F32)) for b in range(8)]
        ring, stat, misc = banks[:RING], banks[4], banks[5]

        x_loaded = sem("x_loaded")
        rows_loaded = sem("rows_loaded")
        ident_loaded = sem("ident_loaded")
        consts_loaded = sem("consts_loaded")
        ones_ready = sem("ones_ready")
        cols_turned = sem("cols_turned")
        cols_ready = sem("cols_ready")
        part_loaded = sem("part_loaded")
        raw_ready = [sem("raw_ready0"), sem("raw_ready1")]
        whi_ready = [sem("whi_ready0"), sem("whi_ready1")]
        wlo_ready = [sem("wlo_ready0"), sem("wlo_ready1")]
        parts_used = sem("parts_used")
        groups_done = sem("groups_done")
        evacuated = sem("evacuated")
        resid_part = sem("resid_part")
        resid_ready = sem("resid_ready")
        square_ready = sem("square_ready")
        acc_added = sem("acc_added")
        head_sums = sem("head_sums")
        edge_ready = sem("edge_ready")
        key_sums = sem("key_sums")
        query_sums = sem("query_sums")
        key_turned = sem("key_turned")
        sums_ready = sem("sums_ready")
        rstd_log = sem("rstd_log")
        rstd_ready = sem("rstd_ready")
        small_log = sem("small_log")
        small_root = sem("small_root")
        rcol_sums = sem("rcol_sums")
        xghi_ready = sem("xghi_ready")
        xg_ready = sem("xg_ready")
        tap_ready = sem("tap_ready")
        conv_part = sem("conv_part")
        conv_ready = sem("conv_ready")
        silu_ready = sem("silu_ready")
        gated_ready = sem("gated_ready")
        ahi_ready = sem("ahi_ready")
        act_ready = sem("act_ready")
        decay_vec = sem("decay_vec")
        decay_act = sem("decay_act")
        q_silu = sem("q_silu")
        mixb_part = sem("mixb_part")
        mixb_ready = sem("mixb_ready")
        level_arg = sem("level_arg")
        scores_cleared = sem("scores_cleared")
        masks_ready = sem("masks_ready")
        level_exp = sem("level_exp")
        level_ready = sem("level_ready")
        cross_arg = sem("cross_arg")
        cross_exp = sem("cross_exp")
        cross_ready = sem("cross_ready")
        osq_ready = sem("osq_ready")
        head_part = sem("head_part")
        mixa_ready = sem("mixa_ready")
        pool_step = sem("pool_step")
        pool_ready = sem("pool_ready")
        inv_loaded = sem("inv_loaded")
        small_step = sem("small_step")
        ck_ready = sem("ck_ready")
        rope_kv_loaded = sem("rope_kv_loaded")
        rope_q_loaded = sem("rope_q_loaded")
        latent_ready = sem("latent_ready")
        latent_hi = sem("latent_hi")
        latent_split = sem("latent_split")
        qrope_part = sem("qrope_part")
        qrope_ready = sem("qrope_ready")
        scores_ready = sem("scores_ready")
        max_part = sem("max_part")
        negmax_ready = sem("negmax_ready")
        exp_ready = sem("exp_ready")
        recip_ready = sem("recip_ready")
        probs_ready = sem("probs_ready")
        turned_ready = sem("turned_ready")
        turned_act = sem("turned_act")
        turned_vec = sem("turned_vec")
        out_ready = sem("out_ready")
        outhi_ready = sem("outhi_ready")
        outlo_ready = sem("outlo_ready")
        normed_out = sem("normed_out")
        stored = sem("stored")

        block = ctx.enter_context(nc.Block())

        def tile(t, k, n=T):
            return t[:, k * n:(k + 1) * n] if isinstance(k, int) else t[:, bass.ds(k * n, n)]

        def col(name, k):
            c = COL[name] + k
            return cols[:, c:c + 1] if isinstance(c, int) else cols[:, bass.ds(c, 1)]

        def slot(t, n, kt=DT, width=UC):
            return t[:, n * UNIT:n * UNIT + kt * width].rearrange("p (k c) -> p k c", k=kt)

        def split_count(n, s):
            return n - s + 2

        fk, lb_ = fkb[:, 0:2048], fkb[:, 2048:4096]

        @block.sync
        def _(sp):
            xtok = fkb[:, :].rearrange("p (c d) -> p c d", c=TC)
            for c in range(TC):
                sp.dma_start(xtok[:, c, :], A["x"][0, c * P:(c + 1) * P, :]).then_inc(x_loaded, 16)

            def load(n, s, pieces):
                if not (isinstance(n, int) and n < 2):
                    sp.wait_ge(wlo_ready[s], split_count(n, s) - 2)
                for dst, src in pieces[:-1]:
                    sp.dma_start(dst, src).then_inc(part_loaded, 16)
                    parts[0] += 16
                if len(pieces) > 1:
                    sp.wait_ge(part_loaded, parts[0])
                sp.dma_start(*pieces[-1]).then_inc(raw_ready[s], 16)

            parts = [0]
            win = A["w_in"][0].rearrange("(k p) c -> p k c", p=P)
            for j, part in enumerate([1, 0, 5, 6, 4, 3, 2]):
                for u in range(2):
                    c0 = part * 512 + u * UC
                    load(2 * j + u, u, [(slot(raw, u), win[:, :, c0:c0 + UC])])
                if j == 0:
                    for dst, name in ((wide_masks, "masks"), (wide_causal, "causal"), (perm, "perm")):
                        sp.dma_start(dst[:, :], A[name]).then_inc(consts_loaded, 16)

            def column_blocks(name, w, ksplit, unroll=False):
                nk = len(ksplit)
                for i in steps(sp, 2, unroll):
                    for b in range(2):
                        k0 = 0
                        for j, kt in enumerate(ksplit):
                            s = (b * nk + j) % 2
                            c0 = i * (2 * UC) + b * UC
                            src = w[:, k0:k0 + kt, c0:c0 + UC] if isinstance(c0, int) else \
                                w[:, k0:k0 + kt, bass.ds(c0, UC)]
                            load(i * (2 * nk) + (UB[name] + b * nk + j), s, [(slot(raw, s, kt), src)])
                            k0 += kt

            def up(name, wg, wu):
                with sp.Fori(0, FF // UC) as i:
                    for s, w in enumerate((wg, wu)):
                        load(i * 2 + (UB[name] + s), s, [(slot(raw, s), w[:, :, bass.ds(i * UC, UC)])])

            def kp(w):
                return w.rearrange("(k p) c -> p k c", p=P)

            column_blocks("w_out", kp(A["w_out"][0]), [8])
            up0 = kp(A["ffn_w_up"][0])
            up("up0", up0[:, :, 0:FF], up0[:, :, FF:2 * FF])
            column_blocks("down0", kp(A["ffn_w_down"][0]), DOWN)

            def ffn(n, which, l, unroll=False):
                up(f"up{n}", kp(A[f"ffn_{which}_wg_2"][l]), kp(A[f"ffn_{which}_wu_2"][l]))
                column_blocks(f"down{n}", kp(A[f"ffn_{which}_wd_2"][l]), DOWN, unroll)

            ffn(1, "pre", 0)
            for u in range(2):
                load(UB["pool"] + u, u, [(slot(raw, u, 4), A["pool_w_2"][0, 2 * u:2 * u + 2].rearrange(
                    "g (t p) c -> p (g t) c", p=P))])
            sp.wait_ge(groups_done, GB["pool"])
            sp.dma_start(inv[:, :], A["inv_count"].to_broadcast([P, 4 * 16])).then_inc(inv_loaded, 16)
            ffn(2, "post", 0)
            dkv = kp(A["w_dkv_2"])
            load(UB["kv"], 0, [(slot(raw, 0, DT, P), dkv[:, :, 0:P])])
            kr = slot(raw, 1, DT, P)
            load(UB["kv"] + 1, 1, [(kr[:, :, 0:ROPE], dkv[:, :, P:P + ROPE]),
                                   (kr[:, :, ROPE:P], dkv[:, :, P:P + ROPE])])
            sp.wait_ge(groups_done, GB["kv"])
            sp.dma_start(rope_kv[:, :], A["rope"]).then_inc(rope_kv_loaded, 16)
            ffn(3, "pre", 1)
            dq = kp(A["w_dq_2"][0])
            for u in range(2):
                load(UB["dq"] + u, u, [(slot(raw, u, DT, P), dq[:, :, u * P:(u + 1) * P])])
            sp.wait_ge(groups_done, GB["dq"])
            sp.dma_start(rope_q[:, :], A["rope"]).then_inc(rope_q_loaded, 16)
            uk = A["w_uk_2"].rearrange("r h d -> r (h d)")
            uv = A["w_uv_2"].rearrange("r h d -> r (h d)")
            uq = A["w_uq_2"][0].rearrange("(t p) h e -> p t h e", p=P)
            r0, r1 = raw[:, 0:UNIT], raw[:, UNIT:UNIT + 512]
            with sp.Fori(0, QUARTERS) as q:
                sp.wait_ge(wlo_ready[0], split_count(q * 2 + UB["attn"], 0) - 2)
                base = parts[0]
                sp.dma_start(r0[:, 0:512], uk[:, bass.ds(q * 512, 512)]).then_inc(part_loaded, 16)
                sp.dma_start(r0[:, 512:1024], uv[:, bass.ds(q * 512, 512)]).then_inc(part_loaded, 16)
                sp.dma_start(r0[:, 1024:1536].rearrange("p (h e) -> p h e", h=4),
                             uq[:, 0, bass.ds(q * 4, 4), 0:NOPE]).then_inc(part_loaded, 16)
                sp.wait_ge(part_loaded, q * 64 + (base + 48))
                sp.dma_start(r0[:, 1536:2048].rearrange("p (h e) -> p h e", h=4),
                             uq[:, 1, bass.ds(q * 4, 4), 0:NOPE]).then_inc(raw_ready[0], 16)
                sp.wait_ge(wlo_ready[1], split_count(q * 2 + (UB["attn"] + 1), 1) - 2)
                sp.dma_start(r1[:, 0:256].rearrange("p (h e) -> p h e", h=4),
                             uq[:, 0, bass.ds(q * 4, 4), NOPE:NOPE + ROPE]).then_inc(part_loaded, 16)
                sp.wait_ge(part_loaded, q * 64 + (base + 64))
                sp.dma_start(r1[:, 256:512].rearrange("p (h e) -> p h e", h=4),
                             uq[:, 1, bass.ds(q * 4, 4), NOPE:NOPE + ROPE]).then_inc(raw_ready[1], 16)
            column_blocks("w_o", kp(A["w_o_2"][0]), [8, 8])
            ffn(4, "post", 1)
            for c in range(TC):
                sp.wait_ge(evacuated, GB["x_out"] + 2 * (c + 1))
                sp.dma_start(out[0, c * P:(c + 1) * P, :], ob[:, c * D:(c + 1) * D]).then_inc(stored, 16)
            sp.wait_ge(stored, 16 * TC)

        @block.gpsimd
        def _(pool):
            nc.gpsimd.memset(ones[:, :], 1.0).then_inc(ones_ready, 1)
            nc.gpsimd.memset(eps[:, :], EPS).then_inc(ones_ready, 1)

            def sum_squares(name):
                j = NORM[name]
                if j:
                    pool.wait_ge(sums_ready, j)
                for k in range(1, DT - 1):
                    pool.wait_ge(square_ready, DT * j + k + 1)
                    a0 = sq[:, 0:T] if k == 1 else acc[:, :]
                    if k > 1:
                        pool.wait_ge(acc_added, (DT - 2) * j + k - 1)
                    nc.gpsimd.tensor_tensor(acc[:, :], a0, tile(sq, k % 2), ALU.add).then_inc(acc_added, 1)

            sum_squares("pre_mix")
            pool.wait_ge(decay_vec, 2 + HH * TC)
            for l, hs in enumerate(LEVELS):
                b = lb_.rearrange("p (n two h) -> p n two h", two=2, h=hs)
                e = EX.rearrange("p (n two h) -> p n two h", two=2, h=hs)
                ref = b[:, :, 0, hs - 1:hs].to_broadcast([P, 2048 // (2 * hs), hs])
                if l:
                    pool.wait_ge(level_ready, 2 * l)
                nc.gpsimd.tensor_tensor(e[:, :, 0, :], ref, b[:, :, 0, :], ALU.subtract).then_inc(level_arg, 1)
                nc.gpsimd.tensor_tensor(e[:, :, 1, :], b[:, :, 1, :], ref, ALU.subtract).then_inc(level_arg, 1)
            pool.wait_ge(evacuated, GB["w_in"] + 56)
            b3 = lb_.rearrange("p (c t) -> p c t", t=P)
            nc.gpsimd.tensor_tensor(LG.rearrange("p (c t) -> p c t", t=P),
                                    b3[:, :, P - 1:P].to_broadcast([P, HH * TC, P]), b3, ALU.subtract
                                    ).then_inc(cross_arg, 1)
            sum_squares("post_mix")
            sum_squares("pre_ffn")
            with pool.Fori(0, FT // 2) as i:
                n = i * 2 + (UB["up0"] + 3)
                pool.wait_ge(whi_ready[1], split_count(n, 1))
                nc.gpsimd.tensor_tensor(wlo[:, UNIT:2 * UNIT], raw[:, UNIT:2 * UNIT],
                                        whi[:, UNIT:2 * UNIT].bitcast(F32), ALU.subtract).then_inc(wlo_ready[1], 2)
            for name in ("post_ffn", "pre0", "mix0", "post0", "kv_pre1", "mix1", "post1", "final"):
                sum_squares(name)

        @block.scalar
        def _(a):
            a.dma_start(ident[:, :], A["ident"]).then_inc(ident_loaded, 16)
            for name, n in VECTORS:
                v = A[name]
                v = v.rearrange("a (k p) -> (a k) p", p=P) if len(v.shape) == 2 else (
                    v.rearrange("a b (k p) -> (a b k) p", p=P) if len(v.shape) == 3 else
                    v.rearrange("(k p) -> k p", p=P))
                a.dma_start(rows[COL[name]:COL[name] + n, 0:P], v).then_inc(rows_loaded, 16)
            taps = A["ffn_conv_w"].rearrange("a b (k p) -> (a b k) p", p=P)
            a.dma_start(rows[0:88, P:2 * P], taps[0:88]).then_inc(rows_loaded, 16)
            a.dma_start(rows[0:44, 2 * P:3 * P], taps[88:132]).then_inc(rows_loaded, 16)

            def split_hi(n, s, signal=None, value=None):
                a.wait_ge(raw_ready[s], (n - s) * 8 + 16)
                if signal is not None:
                    a.wait_ge(signal, value)
                nc.scalar.activation(whi[:, s * UNIT:(s + 1) * UNIT], raw[:, s * UNIT:(s + 1) * UNIT],
                                     ACT.Copy).then_inc(whi_ready[s], 2)

            def square(name, k, t):
                j = NORM[name]
                after = (DT - 2) * j + (0 if k < 2 else max(1, k - 2))
                if after > 0:
                    a.wait_ge(acc_added, after)
                if j and k == 1:
                    a.wait_ge(sums_ready, j)
                nc.scalar.activation(tile(sq, k % 2), tile(t, k), ACT.Square).then_inc(square_ready, 1)

            def xg_hi(signal, value, t, gain, k, w=None):
                a.wait_ge(signal, value)
                nc.scalar.activation(tile(xghi, k), tile(t, k), ACT.Copy,
                                     scale=1.0 if gain is None else col(gain, k if w is None else w)
                                     ).then_inc(xghi_ready, 1)

            split_hi(0, 0)
            a.wait_ge(cols_ready, 1)
            for k in range(DT):
                xg_hi(evacuated, k + 1, xT, "pre_mix_g", k)
                square("pre_mix", k, xT)
                if k == 0:
                    split_hi(1, 1)

            def root(name):
                j = NORM[name]
                a.wait_ge(sums_ready, j + 1)
                nc.scalar.activation(R[:, :], stat[:, :], ACT.Ln, bias=eps[:, :], scale=1.0 / D).then_inc(rstd_log, 1)
                a.wait_ge(rstd_log, j + 1)
                nc.scalar.activation(R[:, :], R[:, :], ACT.Exp, scale=-0.5).then_inc(rstd_ready, 1)

            smalls = [0]

            def root_of(t, sums, n, signal, value):
                smalls[0] += 1
                a.wait_ge(signal, value)
                nc.scalar.activation(t, sums, ACT.Ln, bias=eps[:, :], scale=1.0 / n).then_inc(small_log, 1)
                a.wait_ge(small_log, smalls[0])
                nc.scalar.activation(t, t, ACT.Exp, scale=-0.5).then_inc(small_root, 1)

            a.wait_ge(ones_ready, 2)
            root("pre_mix")
            root_of(rcol[:, :], misc[:, 0:TC], D, rcol_sums, 1)
            g0 = GB["w_in"]
            for n in range(14):
                read = 2 * (n + 1) if n < 4 else 8 + 6 * (n - 4) + 2 if n < 12 else 56 + 4 * (n - 11)
                if n == 12:
                    bends = lb_.rearrange("p (c t) -> p c t", t=P)[:, :, P - 1]
                    a.wait_ge(cross_arg, 1)
                    nc.scalar.activation(LG, LG, ACT.Exp).then_inc(cross_exp, 1)
                    nc.scalar.activation(ends[:, :], bends, ACT.Exp).then_inc(cross_exp, 1)
                    a.wait_ge(cross_exp, 2)
                    nc.scalar.activation(lb_, lb_, ACT.Exp).then_inc(cross_exp, 1)
                split_hi(n + 2, n % 2, groups_done, g0 + read)
                if n == 1:
                    a.wait_ge(evacuated, g0 + 4)
                    nc.scalar.activation(lb_, fk, ACT.Abs).then_inc(decay_act, 1)
                    a.wait_ge(decay_act, 1)
                    nc.scalar.activation(lb_, lb_, ACT.Exp, scale=-1.0).then_inc(decay_act, 1)
                    a.wait_ge(decay_act, 2)
                    nc.scalar.activation(lb_, lb_, ACT.Ln, bias=1.0).then_inc(decay_act, 1)
                if n == 2:
                    a.wait_ge(decay_vec, 2)
                    nc.scalar.activation(fk, fk, ACT.Exp).then_inc(decay_act, 1)
                if n == 3:
                    a.wait_ge(evacuated, g0 + 8)
                    nc.scalar.activation(Q[:, :], Q[:, :], ACT.Silu).then_inc(q_silu, 1)
                if 4 <= n <= 10:
                    a.wait_ge(level_arg, 2 * (n - 3))
                    nc.scalar.activation(EX, EX, ACT.Exp).then_inc(level_exp, 1)
                if n == 11:
                    a.wait_ge(evacuated, g0 + 52)
                    nc.scalar.activation(G[:, :], G[:, :], ACT.Silu).then_inc(q_silu, 1)
            for k in range(4):
                a.wait_ge(mixb_ready, k + 1)
                nc.scalar.activation(tile(xghi, 4 + k), tile(GBt, k), ACT.Copy).then_inc(xghi_ready, 1)
            for h in range(HH):
                root_of(tile(GC, h), banks[4 + h][:, :], P, head_sums, h + 1)
            for h in range(HH):
                a.wait_ge(mixa_ready, h + 1)
                nc.scalar.activation(tile(xghi, h), tile(CH, h), ACT.Copy).then_inc(xghi_ready, 1)
            def project(name, ksplit, norm, gain=None, goff=0, unroll=False, t=xT):
                nk = len(ksplit)
                for i in steps(a, 2, unroll):
                    for b in range(2):
                        def ahead(j):
                            n = i * (2 * nk) + (UB[name] + b * nk + j + 2)
                            if unroll and n >= UNITS:
                                return
                            s = (b * nk + j) % 2
                            if j < nk - 1:
                                split_hi(n, s, parts_used, i * (2 * nk - 2) + (MB[name] + b * (nk - 1) + j + 1))
                            else:
                                split_hi(n, s, groups_done, i * 4 + (GB[name] + 2 * b + 2))
                        for j in range(nk - 1):
                            ahead(j)
                        for f in range(2):
                            gr = 2 * b + f
                            k = i * 4 + gr
                            if norm:
                                base = (DT - 2) * NORM[norm]
                                if gr == 1:
                                    a.wait_ge(sums_ready, NORM[norm])
                                a.wait_ge(acc_added,
                                          (i * 2 + base, i * 3 + base, i * 3 + (base + 1), i * 4 + (base + 1))[gr])
                            if gain:
                                xg_hi(evacuated, k + (GB[name] + 1), xT, gain, k, k + goff)
                            else:
                                a.wait_ge(evacuated, k + (GB[name] + 1))
                            if norm:
                                nc.scalar.activation(tile(sq, f), tile(t, k), ACT.Square).then_inc(square_ready, 1)
                        ahead(nk - 1)

            project("w_out", [8], "post_mix", t=Y0)
            root("post_mix")
            for k in range(DT):
                xg_hi(resid_ready, k + 1, xT, "pre_ffn_g", k)
                square("pre_ffn", k, xT)

            def up(m, conv=False):
                name = f"up{m}"
                gb, hb = GB[name], FT * m
                with a.Fori(0, FT // 2) as i:
                    for f in range(2):
                        if conv:
                            a.wait_ge(evacuated, i * 4 + (gb + f + 1))
                            nc.scalar.activation(tile(Tt, f), tile(Ut, f), ACT.Copy,
                                                 scale=cw[:, bass.ds(i * 2 + (2 * 2 * FT + f), 1)]
                                                 ).then_inc(tap_ready, 1)
                    for f in range(2):
                        if conv:
                            a.wait_ge(conv_ready, i * 4 + (f + 1))
                        else:
                            a.wait_ge(evacuated, i * 4 + (gb + f + 1))
                        nc.scalar.activation(tile(Tt, f), tile(Tt, f), ACT.Silu).then_inc(silu_ready, 1)
                    split_hi(i * 2 + (UB[name] + 2), 0, groups_done, i * 4 + (gb + 2))
                    for f in range(2):
                        if conv:
                            a.wait_ge(evacuated, i * 4 + (gb + f + 3))
                            nc.scalar.activation(tile(At, f), tile(Ut, f), ACT.Copy,
                                                 scale=cw[:, bass.ds(i * 2 + (2 * 2 * FT + FT + f), 1)]
                                                 ).then_inc(tap_ready, 1)
                    if conv:
                        split_hi(i * 2 + (UB[name] + 3), 1, groups_done, i * 4 + (gb + 4))
                    for f in range(2):
                        a.wait_ge(gated_ready, i * 2 + (hb + f + 1))
                        nc.scalar.activation(tile(ahi, i * 2 + f), tile(At, f), ACT.Copy).then_inc(ahi_ready, 1)
                    if not conv:
                        split_hi(i * 2 + (UB[name] + 3), 1, groups_done, i * 4 + (gb + 4))

            root("pre_ffn")
            up(0, conv=True)
            project("down0", DOWN, "post_ffn", t=Y1)
            root("post_ffn")
            for k in range(DT):
                xg_hi(resid_ready, DT + k + 1, xT, "ffn_pre_norm_2", k)
                square("pre0", k, xT)
            root("pre0")
            up(1)
            project("down1", DOWN, "mix0")
            root("mix0")
            for k in range(DT):
                a.wait_ge(pool_ready, k // 2 + 1)
                src = PB if (k // 2) % 2 else PA
                nc.scalar.activation(tile(xghi, k), src[:, (k % 2) * PW + 16:(k % 2 + 1) * PW], ACT.Copy
                                     ).then_inc(xghi_ready, 1)
            for u in range(2):
                split_hi(UB["pool"] + u + 2, u, groups_done, GB["pool"] + 4 * (u + 1))
            for k in range(DT):
                a.wait_ge(groups_done, GB["pool"] + DT)
                xg_hi(evacuated, GB["pool"] + k + 1, xT, "ffn_post_norm_2", k)
                square("post0", k, xT)
            root("post0")
            up(2)
            project("down2", DOWN, "kv_pre1", "kv_in_norm_2")
            root("kv_pre1")
            split_hi(UB["kv"] + 2, 0, groups_done, GB["kv"] + 2)
            a.wait_ge(groups_done, GB["kv"] + 4)
            for k in range(DT):
                xg_hi(evacuated, GB["down2"] + k + 1, xT, "ffn_pre_norm_2", k, 8 + k)
            split_hi(UB["kv"] + 3, 1, groups_done, GB["kv"] + 4)
            root_of(kvt[:, T:2 * T], banks[6][:, :], P, key_sums, 1)
            up(3)
            project("down3", DOWN, "mix1", "mix_norm_2", 8)
            root("mix1")
            for u in range(2):
                split_hi(UB["dq"] + u + 2, u, groups_done, GB["dq"] + (1, 4)[u])
                if u == 0:
                    a.wait_ge(latent_ready, 1)
                    nc.scalar.activation(ckhi[:, :], Ut[:, 0:T], ACT.Copy).then_inc(latent_hi, 1)
            for j in range(1, 1 + QR):
                if j == 1:
                    root_of(PT[:, 0:T], misc[:, :], QR * P, query_sums, 1)
                a.wait_ge(latent_ready, j + 1)
                nc.scalar.activation(tile(cqhi, j - 1), tile(At, j - 1), ACT.Copy).then_inc(latent_hi, 1)
            with a.Fori(0, QUARTERS) as q:
                split_hi(q * 2 + (UB["attn"] + 2), 0, groups_done, q * 16 + (GB["attn"] + 12))
                split_hi(q * 2 + (UB["attn"] + 3), 1, groups_done, q * 16 + (GB["attn"] + 14))

                def exps(h):
                    for i in range(TC):
                        e = 4 * h + i
                        a.wait_ge(negmax_ready, q * 16 + (e + 1))
                        c = 4 * (h % 2) + i
                        off = i * (i + 1) // 2 * P
                        nc.scalar.activation(probs(h)[:, off:off + (i + 1) * P], ring[i][:, 0:(i + 1) * P],
                                             ACT.Exp, bias=negmax[:, c:c + 1], scale=float((NOPE + ROPE) ** -0.5),
                                             accum_out=rowsum[:, c:c + 1]).then_inc(exp_ready, 1)

                exps(0)
                for h in range(4):
                    if h < 3:
                        exps(h + 1)
                    a.wait_ge(turned_ready, q * 12 + (3 * h + 1))
                    nc.scalar.activation(PT[:, 0:4 * P], banks[4][:, 0:4 * P], ACT.Copy).then_inc(turned_act, 1)
                    a.wait_ge(turned_ready, q * 12 + (3 * h + 3))
                    nc.scalar.activation(PT[:, 7 * P:10 * P], banks[6][:, 0:3 * P], ACT.Copy).then_inc(turned_act, 1)
                    a.wait_ge(out_ready, q * 4 + (h + 1))
                    nc.scalar.activation(tile(oThi, q * 4 + h), banks[7][:, :], ACT.Copy).then_inc(outhi_ready, 1)
            project("w_o", [8, 8], "post1", "ffn_post_norm_2", 8)
            root("post1")
            up(4)
            project("down4", DOWN, "final", unroll=True)
            root("final")


        @block.tensor
        def _(pe):
            def unit_ready(n, s):
                pe.wait_ge(wlo_ready[s], split_count(n, s))

            def three(bank, whi_, wlo_, xhi, xlo, first, last):
                nc.tensor.matmul(bank, wlo_, xhi, start=first, stop=False)
                nc.tensor.matmul(bank, whi_, xlo, start=False, stop=False)
                return nc.tensor.matmul(bank, whi_, xhi, start=False, stop=last)

            def bank_free(g):
                pe.wait_ge(evacuated, g - RING + 1)

            def sum_norm(name):
                j = NORM[name]
                pe.wait_ge(acc_added, (DT - 2) * (j + 1))
                if j:
                    pe.wait_ge(rstd_log, j)
                nc.tensor.matmul(stat[:, :], ones[:, :], acc[:, :], start=True, stop=False)
                pe.wait_ge(square_ready, DT * (j + 1))
                nc.tensor.matmul(stat[:, :], ones[:, :], sq[:, T:2 * T], start=False, stop=True
                                 ).then_inc(sums_ready, 1)
                if j == 0:
                    for c in range(TC):
                        nc.tensor.matmul(misc[:, c:c + 1], acc[:, c * P:(c + 1) * P], ones[:, 0:1],
                                         start=True, stop=False)
                        m = nc.tensor.matmul(misc[:, c:c + 1], sq[:, T + c * P:T + (c + 1) * P], ones[:, 0:1],
                                             start=False, stop=True)
                    m.then_inc(rcol_sums, 1)

            pe.wait_ge(ident_loaded, 16)
            pe.wait_ge(x_loaded, 16 * TC)
            for k in range(DT):
                if k >= RING:
                    bank_free(k)
                for c in range(TC):
                    m = nc.tensor.transpose(ring[k % RING][:, c * P:(c + 1) * P],
                                            fkb[:, c * D + k * P:c * D + (k + 1) * P], ident[:, :])
                m.then_inc(groups_done, 1)
            pe.wait_ge(rows_loaded, 16 * (len(VECTORS) + 2))
            nc.tensor.transpose(misc[:, 0:NVEC], rows[0:NVEC, 0:P], ident[0:NVEC, 0:NVEC])
            nc.tensor.transpose(misc[:, P:P + 88], rows[0:88, P:2 * P], ident[0:88, 0:88])
            nc.tensor.transpose(misc[:, P + 88:P + 132], rows[0:44, 2 * P:3 * P], ident[0:44, 0:44]
                                ).then_inc(cols_turned, 1)

            def up_unit(n, s, g, xg, order=range(DT)):
                unit_ready(n, s)
                w, wl = slot(whi, s), slot(wlo, s)
                for f in range(2):
                    bank_free(g + f)
                    bank = ring[(2 * s + f) % RING][:, :]
                    for pos, k in enumerate(order):
                        if f == 0 and s == 0:
                            pe.wait_ge(xg_ready, XG[xg] + pos + 1)
                        m = three(bank, w[:, k, f * P:(f + 1) * P], wl[:, k, f * P:(f + 1) * P],
                                  tile(xghi, k), tile(xglo, k), pos == 0, pos == DT - 1)
                    m.then_inc(groups_done, 1)

            def first_units(n, g, xg, between):
                for tiles, slots in ([((k,), (0, 1)) for k in range(4)]
                                     + [(range(4, DT), (0,)), (range(4, DT), (1,))]):
                    for k in tiles:
                        pe.wait_ge(xg_ready, XG[xg] + k + 1)
                        for s in slots:
                            if k == 0:
                                unit_ready(n + s, s)
                            for f in range(2):
                                if k == 0:
                                    bank_free(g + 2 * s + f)
                                m = three(ring[2 * s + f][:, :], slot(whi, s)[:, k, f * P:(f + 1) * P],
                                          slot(wlo, s)[:, k, f * P:(f + 1) * P], tile(xghi, k), tile(xglo, k),
                                          k == 0, k == DT - 1)
                                if k == DT - 1:
                                    m.then_inc(groups_done, 1)
                    if slots == (0,) and between:
                        between()

            def level(l, g):
                if l == 0:
                    pe.wait_ge(q_silu, 1)
                    pe.wait_ge(decay_act, 4)
                else:
                    pe.wait_ge(level_ready, 2 * l)
                for h in range(HH):
                    bank_free(g + h)
                    for c in range(TC):
                        at_ = slice((TC * h + c) * P, (TC * h + c + 1) * P)
                        left, right = (fk[:, at_], Q[:, at_]) if l == 0 else (LG[:, at_], LG[:, at_])
                        m = nc.tensor.matmul(ring[(g + h) % RING][:, c * P:(c + 1) * P], left, right,
                                             start=True, stop=True)
                    m.then_inc(groups_done, 1)

            g = GB["w_in"]
            pe.wait_ge(ones_ready, 2)
            pe.wait_ge(cols_ready, 3)
            first_units(0, g, "w_in", lambda: sum_norm("pre_mix"))
            g += 4
            for n in range(2, 12):
                up_unit(n, n % 2, g, "w_in")
                g += 2
                if n >= 4:
                    level(n - 4, g)
                    g += 4
            for s in range(2):
                unit_ready(12 + s, s)
                for c in range(TC):
                    bank_free(g)
                    for k in range(DT):
                        xh = xghi[:, k * T + c * P:k * T + (c + 1) * P]
                        xl = xglo[:, k * T + c * P:k * T + (c + 1) * P]
                        w, wl = slot(whi, s)[:, k, :], slot(wlo, s)[:, k, :]
                        m = three(ring[g % RING][:, 0:UC], xh, xl, w, wl, k == 0, k == DT - 1)
                    m.then_inc(groups_done, 1)
                    g += 1
            pe.wait_ge(cross_ready, 5)
            for h in range(HH):
                def c_(t, c):
                    return t[:, (TC * h + c) * P:(TC * h + c + 1) * P]
                for pairs in (((GC, 0, 1), (fkb, 0, 2), (fkb, 2, 3)), ((GC, 1, 2), (fkb, 1, 3), (GC, 2, 3))):
                    bank_free(g)
                    for n, (t, i, j) in enumerate(pairs):
                        m = nc.tensor.matmul(ring[g % RING][:, n * P:(n + 1) * P], c_(t, i), c_(lb_, j),
                                             start=True, stop=True)
                    m.then_inc(groups_done, 1)
                    g += 1
            for h in range(HH):
                bank_free(g)
                pe.wait_ge(evacuated, GB["cross"] + 2 * h + 2)
                off = 0
                for i in range(TC):
                    v = V[:, i * 512 + h * P:i * 512 + (h + 1) * P]
                    m = nc.tensor.matmul(ring[h][:, i * P:(i + 1) * P], v,
                                         SD[:, (TC * h + i) * P:(TC * h + i + 1) * P],
                                         start=(i == 0), stop=(i == TC - 1))
                    if i < TC - 1:
                        n = TC - 1 - i
                        nc.tensor.matmul(ring[h][:, (i + 1) * P:T], v,
                                         SC[:, (6 * h + off) * P:(6 * h + off + n) * P], start=False, stop=False)
                        off += n
                m.then_inc(groups_done, 1)
                g += 1
            order = [4, 5, 6, 7, 0, 1, 2, 3]
            for part in range(2):
                for b in range(2):
                    unit_ready(UB["w_out"] + b, b)
                    w, wl = slot(whi, b), slot(wlo, b)
                    for f in range(2):
                        if part == 0:
                            bank_free(g + 2 * b + f)
                        for pos in range(4 * part, 4 * part + 4):
                            k = order[pos]
                            if b == 0 and f == 0:
                                pe.wait_ge(xg_ready, XG["w_out"] + pos + 1)
                            m = three(ring[2 * b + f][:, :], w[:, k, f * P:(f + 1) * P], wl[:, k, f * P:(f + 1) * P],
                                      tile(xghi, k), tile(xglo, k), pos == 0, pos == DT - 1)
                        if part == 1:
                            m.then_inc(groups_done, 1)
                    if part == 0 and b == 0:
                        for h in range(HH):
                            pe.wait_ge(osq_ready, h + 1)
                            nc.tensor.matmul(banks[4 + h][:, :], ones[:, :], tile(GC, h), start=True, stop=True
                                             ).then_inc(head_sums, 1)

            def project(name, ksplit, hi, lo, ready, base, iterations=None):
                nk, total = len(ksplit), sum(ksplit)
                for i in (steps(pe, 2) if iterations is None else iterations):
                    for b in range(2):
                        pos0 = 0
                        for j, kt in enumerate(ksplit):
                            s = (b * nk + j) % 2
                            unit_ready(i * (2 * nk) + (UB[name] + b * nk + j), s)
                            w, wl = slot(whi, s, kt), slot(wlo, s, kt)
                            for f in range(2):
                                if j == 0:
                                    bank_free(i * 4 + (GB[name] + 2 * b + f))
                                for pos in range(pos0, pos0 + kt):
                                    k = pos
                                    if b == 0 and f == 0:
                                        pe.wait_ge(ready, base + pos + 1)
                                    m = three(ring[2 * b + f][:, :], w[:, k - pos0, f * P:(f + 1) * P],
                                              wl[:, k - pos0, f * P:(f + 1) * P], tile(hi, k), tile(lo, k),
                                              pos == 0, pos == total - 1)
                                if j == nk - 1:
                                    m.then_inc(groups_done, 1)
                            if j < nk - 1:
                                m.then_inc(parts_used, 1)
                            pos0 += kt

            project("w_out", [8], xghi, xglo, xg_ready, XG["w_out"], (1,))
            sum_norm("post_mix")

            def ffn(m, norm=None, between=None):
                name = f"up{m}"
                first_units(UB[name], GB[name], name, (lambda: sum_norm(norm)) if norm else between)
                with pe.Fori(1, FT // 2) as i:
                    for s in range(2):
                        up_unit(i * 2 + (UB[name] + s), s, i * 4 + (GB[name] + 2 * s), name)
                project(f"down{m}", DOWN, ahi, alo, act_ready, FT * m)

            ffn(0, "pre_ffn")
            sum_norm("post_ffn")
            ffn(1, "pre0")
            sum_norm("mix0")
            for u in range(2):
                unit_ready(UB["pool"] + u, u)
                w, wl = slot(whi, u, 4), slot(wlo, u, 4)
                for gg in range(2):
                    for f in range(2):
                        g = GB["pool"] + 4 * u + 2 * gg + f
                        bank_free(g)
                        for kt in range(2):
                            k = 2 * (2 * u + gg) + kt
                            pe.wait_ge(xg_ready, XG["pool"] + k + 1)
                            c = slice(f * P, (f + 1) * P)
                            m = three(ring[g % RING][:, :], w[:, 2 * gg + kt, c], wl[:, 2 * gg + kt, c],
                                      tile(xghi, k), tile(xglo, k), kt == 0, kt == 1)
                        m.then_inc(groups_done, 1)
            ffn(2, "post0")

            def narrow(name, norm, counts):
                for u in range(2):
                    unit_ready(UB[name] + u, u)
                    bank_free(GB[name] + u)
                    w, wl = slot(whi, u, DT, P), slot(wlo, u, DT, P)
                    for k in range(DT):
                        pe.wait_ge(xg_ready, XG[name] + k + 1)
                        m = three(ring[u][:, :], w[:, k, :], wl[:, k, :], tile(xghi, k), tile(xglo, k),
                                  k == 0, k == DT - 1)
                    m.then_inc(groups_done, counts[u])
                    if u == 0:
                        sum_norm(norm)

            narrow("kv", "kv_pre1", (2, 2))
            pe.wait_ge(evacuated, GB["kv"] + 4)

            def key_extras():
                pe.wait_ge(small_step, 1)
                pe.wait_ge(consts_loaded, 16 * 3)
                nc.tensor.matmul(banks[6][:, :], ones[:, :], kvt[:, 0:T], start=True, stop=True).then_inc(key_sums, 1)
                nc.tensor.matmul(banks[7][:, :], perm[:, :], Ut[:, T:2 * T], start=True, stop=True
                                 ).then_inc(key_turned, 1)

            ffn(3, between=key_extras)
            narrow("dq", "mix1", (1, 3))
            pe.wait_ge(small_step, 3)
            nc.tensor.matmul(misc[:, :], ones[:, :], PT[:, 0:T], start=True, stop=False)
            nc.tensor.matmul(misc[:, :], ones[:, :], PT[:, T:2 * T], start=False, stop=True
                             ).then_inc(query_sums, 1)
            scale_w0 = whi[:, 0:UNIT], wlo[:, 0:UNIT]
            w1 = whi[:, UNIT:2 * UNIT], wlo[:, UNIT:2 * UNIT]
            with pe.Fori(0, QUARTERS) as q:
                gb = GB["attn"]
                unit_ready(q * 2 + UB["attn"], 0)
                pe.wait_ge(latent_split, 1)
                for n in range(12):
                    if n == 8:
                        pe.wait_ge(latent_split, 1 + QR)
                    bank_free(q * 16 + (gb + n))
                    bank = ring[n % RING][:, :]
                    x = n % 4
                    c = slice(x * P, (x + 1) * P)
                    if n < 4:
                        m = three(bank, scale_w0[0][:, c], scale_w0[1][:, c], ckhi[:, :], cklo[:, :], True, True)
                    elif n < 8:
                        m = three(bank, ckhi[:, c], cklo[:, c], scale_w0[0][:, 512:1024],
                                  scale_w0[1][:, 512:1024], True, True)
                    else:
                        for kt in range(QR):
                            o = 1024 + kt * 512 + x * P
                            m = three(bank, scale_w0[0][:, o:o + P], scale_w0[1][:, o:o + P],
                                      tile(cqhi, kt), tile(cqlo, kt), kt == 0, kt == QR - 1)
                    m.then_inc(groups_done, 1)
                unit_ready(q * 2 + (UB["attn"] + 1), 1)
                for j in range(2):
                    bank_free(q * 16 + (gb + 12 + j))
                    for kt in range(QR):
                        o = kt * 256 + j * P
                        m = three(ring[j][:, :], w1[0][:, o:o + P], w1[1][:, o:o + P],
                                  tile(cqhi, kt), tile(cqlo, kt), kt == 0, kt == QR - 1)
                    m.then_inc(groups_done, 1)
                for j in range(2):
                    bank_free(q * 16 + (gb + 14 + j))
                    pe.wait_ge(evacuated, q * 16 + (gb + 13 + j))
                    nc.tensor.matmul(ring[2 + j][:, :], perm[:, :], tile(QRr, j), start=True, stop=True
                                     ).then_inc(groups_done, 1)

                def scores(h):
                    if h == 0:
                        pe.wait_ge(evacuated, q * 16 + (gb + 16))
                        pe.wait_ge(qrope_ready, q * 2 + 2)
                    for i in range(TC):
                        if h:
                            pe.wait_ge(exp_ready, q * 16 + (4 * (h - 1) + i + 1))
                        n = (i + 1) * P
                        nc.tensor.matmul(ring[i][:, 0:n], QN[:, h * T + i * P:h * T + (i + 1) * P],
                                         KN[:, h * T:h * T + n], start=True, stop=False)
                        r = (h // 2) * T + i * P
                        nc.tensor.matmul(ring[i][:, 0:n], QRt[:, r:r + P], Tt[:, (h % 2) * T:(h % 2) * T + n],
                                         start=False, stop=False)
                        nc.tensor.matmul(ring[i][:, i * P:n], identb[:, :], causal[:, :],
                                         start=False, stop=True).then_inc(scores_ready, 1)

                scores(0)
                for h in range(4):
                    if h < 3:
                        scores(h + 1)
                    for i in range(TC):
                        pe.wait_ge(probs_ready, q * 16 + (4 * h + i + 1))
                        off = i * (i + 1) // 2
                        for j in range(i + 1):
                            bank, at_ = [(banks[4], i), (banks[5], i - 1), (banks[6], i - 2), (banks[6], 2)][j]
                            m = nc.tensor.transpose(bank[:, at_ * P:(at_ + 1) * P],
                                                    probs(h)[:, (off + j) * P:(off + j + 1) * P], ident[:, :])
                            if i == TC - 1 and j != 2:
                                m.then_inc(turned_ready, 1)
                    if h:
                        pe.wait_ge(outlo_ready, q * 4 + h)
                    seg = 0
                    for j in range(TC):
                        if j == 0:
                            pe.wait_ge(turned_act, q * 8 + (2 * h + 1))
                        elif j == 1:
                            pe.wait_ge(turned_vec, q * 4 + (h + 1))
                        elif j == 2:
                            pe.wait_ge(turned_act, q * 8 + (2 * h + 2))
                        n = (TC - j) * P
                        m = nc.tensor.matmul(banks[7][:, j * P:T], VV[:, j * 512 + h * P:j * 512 + (h + 1) * P],
                                             PT[:, seg:seg + n], start=(j == 0), stop=(j == TC - 1))
                        seg += n
                    m.then_inc(out_ready, 1)
                pe.wait_ge(outlo_ready, q * 4 + 4)
            project("w_o", [8, 8], oThi, oTlo, outlo_ready, 0)
            ffn(4, "post1")
            sum_norm("final")
            g = GB["x_out"]
            for c in range(TC):
                for half in range(2):
                    bank_free(g)
                    for kk in range(4):
                        k = 4 * half + kk
                        if c == 0:
                            pe.wait_ge(normed_out, k + 1)
                        m = nc.tensor.transpose(ring[g % RING][:, kk * P:(kk + 1) * P],
                                                Z[:, k * T + c * P:k * T + (c + 1) * P], ident[:, :])
                    m.then_inc(groups_done, 1)
                    g += 1

        @block.vector
        def _(v):
            def split_lo(n, s):
                v.wait_ge(whi_ready[s], split_count(n, s))
                c = slice(s * UNIT, (s + 1) * UNIT)
                nc.vector.tensor_tensor(wlo[:, c], raw[:, c], whi[:, c].bitcast(F32), ALU.subtract
                                        ).then_inc(wlo_ready[s], 2)

            def xg_lo(xg, pos, k, t, gain, w=None):
                v.wait_ge(xghi_ready, XG[xg] + pos + 1)
                hi = tile(xghi, k).bitcast(F32)
                if gain is None:
                    ins = nc.vector.tensor_tensor(tile(xglo, k), t, hi, ALU.subtract)
                else:
                    ins = nc.vector.scalar_tensor_tensor(tile(xglo, k), t, col(gain, k if w is None else w), hi,
                                                         ALU.mult, ALU.subtract)
                ins.then_inc(xg_ready, 1)

            def rstd(name):
                v.wait_ge(rstd_ready, NORM[name] + 1)

            for k in range(DT):
                v.wait_ge(groups_done, k + 1)
                nc.vector.tensor_copy(tile(xT, k), ring[k % RING][:, :]).then_inc(evacuated, 1)
            v.wait_ge(cols_turned, 1)
            nc.vector.tensor_copy(cols[:, :], misc[:, 0:NVEC]).then_inc(cols_ready, 1)
            nc.vector.tensor_copy(cw[:, 0:88], misc[:, P:P + 88]).then_inc(cols_ready, 1)
            nc.vector.tensor_copy(cw[:, 88:132], misc[:, P + 88:P + 132]).then_inc(cols_ready, 1)
            split_lo(0, 0)
            v.wait_ge(cols_ready, 3)
            for k in range(DT):
                xg_lo("w_in", k, k, tile(xT, k), "pre_mix_g")
                if k == 0:
                    split_lo(1, 1)
            v.wait_ge(ident_loaded, 16)
            v.wait_ge(consts_loaded, 16 * 3)
            nc.vector.tensor_copy(identb[:, :], ident[:, :])
            nc.vector.tensor_copy(causal[:, :], wide_causal[:, :])
            nc.vector.tensor_copy(masks[:, :], wide_masks[:, :]).then_inc(masks_ready, 1)
            rstd("pre_mix")

            g = GB["w_in"]
            dests = [fk, Q[:, :], GC[:, :], CH[:, :], GBt[:, :], G[:, :]]
            mask = masks[:, :].rearrange("p (l t) -> p l t", l=8)

            def take(l, g):
                v.wait_ge(evacuated, g)
                for h in range(HH):
                    v.wait_ge(groups_done, g + 1)
                    nc.vector.copy_predicated(
                        SD[:, h * TC * P:(h + 1) * TC * P].rearrange("p (c t) -> p c t", c=TC),
                        mask[:, l:l + 1, :].to_broadcast([P, TC, P]),
                        ring[g % RING][:, :].rearrange("p (c t) -> p c t", c=TC)).then_inc(evacuated, 1)
                    g += 1
                return g

            def level_operand(l):
                hs = LEVELS[l - 1]
                e, k_, q_, o = (t.rearrange("p (n two h) -> p n two h", two=2, h=hs) for t in (EX, fk, Q[:, :], LG))
                v.wait_ge(level_exp, l)
                nc.vector.tensor_tensor(o[:, :, 0, :], e[:, :, 0, :], k_[:, :, 0, :], ALU.mult).then_inc(level_ready, 1)
                nc.vector.tensor_tensor(o[:, :, 1, :], e[:, :, 1, :], q_[:, :, 1, :], ALU.mult).then_inc(level_ready, 1)

            mixb_steps = [0]

            def after_mixb():
                v.wait_ge(mixb_part, mixb_steps[0])

            def mixb_step(ins):
                ins.then_inc(mixb_part, 1)
                mixb_steps[0] += 1

            def conv_tile(k):
                m, c, b = tile(GC, k), tile(CH, k), tile(GBt, k)
                mixb_step(nc.vector.tensor_tensor(m, m, c, ALU.mult))
                after_mixb()
                mixb_step(nc.vector.tensor_scalar(c, m, col("conv_w", 8 + k), None, ALU.mult))
                after_mixb()
                mixb_step(nc.vector.scalar_tensor_tensor(c[:, 1:T], m[:, 0:T - 1], col("conv_w", 4 + k), c[:, 1:T],
                                                         ALU.mult, ALU.add))
                after_mixb()
                mixb_step(nc.vector.scalar_tensor_tensor(c[:, 2:T], m[:, 0:T - 2], col("conv_w", k), c[:, 2:T],
                                                         ALU.mult, ALU.add))
                after_mixb()
                nc.vector.tensor_tensor(b, b, c, ALU.mult).then_inc(mixb_ready, 1)

            def cross_ends(scale_chunks):
                if not scale_chunks:
                    v.wait_ge(cross_exp, 1)
                    v.wait_ge(mixb_ready, 4)
                    nc.vector.tensor_tensor(GC[:, :], LG, fk, ALU.mult).then_inc(cross_ready, 1)
                    return
                v.wait_ge(cross_exp, 3)
                nc.vector.tensor_tensor(lb_, lb_, Q[:, :], ALU.mult).then_inc(cross_ready, 1)
                ge = GC[:, :].rearrange("p (h c t) -> p h c t", h=HH, c=TC)
                fe = fk.rearrange("p (h c t) -> p h c t", h=HH, c=TC)
                en = ends[:, :].rearrange("p (h c) -> p h c", h=HH)
                for dst, src, c, e, after in ((0, ge, 0, 1, 1), (1, ge, 1, 2, 1), (2, fe, 0, 2, 3)):
                    v.wait_ge(cross_ready, after)
                    nc.vector.tensor_tensor(fe[:, :, dst, :], src[:, :, c, :],
                                            en[:, :, e:e + 1].to_broadcast([P, HH, P]), ALU.mult
                                            ).then_inc(cross_ready, 1)

            for n in range(14):
                s = n % 2
                if n in (12, 13):
                    if n == 12:
                        v.wait_ge(small_root, 1)
                        v.wait_ge(level_ready, 2 * len(LEVELS))
                    for c in range(TC):
                        v.wait_ge(groups_done, g + 1)
                        nc.vector.tensor_scalar(V[:, c * 512 + s * UC:c * 512 + (s + 1) * UC],
                                                ring[g % RING][:, 0:UC], rcol[:, c:c + 1], float(P) ** -0.5,
                                                ALU.mult, ALU.mult).then_inc(evacuated, 1)
                        g += 1
                        if n == 12 and c in (1, 3):
                            cross_ends(c == 3)
                else:
                    for f in range(2):
                        v.wait_ge(groups_done, g + 1)
                        nc.vector.tensor_tensor(tile(dests[n // 2], 2 * s + f), ring[g % RING][:, :], R[:, :],
                                                ALU.mult).then_inc(evacuated, 1)
                        g += 1
                if n < 4 or n == 12:
                    split_lo(n + 2, s)
                if n == 1:
                    nc.vector.memset(SD[:, :], 0.0).then_inc(scores_cleared, 1)
                if n == 2:
                    v.wait_ge(decay_act, 3)
                    nc.vector.scalar_tensor_tensor(lb_, fk, 0.0, lb_, ALU.min, ALU.subtract).then_inc(decay_vec, 1)
                    v.wait_ge(decay_vec, 1)
                    nc.vector.tensor_tensor(fk, lb_, fk, ALU.subtract).then_inc(decay_vec, 1)
                    v.wait_ge(decay_vec, 2)
                    v.wait_ge(ones_ready, 2)
                    for c in range(HH * TC):
                        b = lb_[:, c * P:(c + 1) * P]
                        nc.vector.tensor_tensor_scan(b, ones[:, :], b, 0.0, ALU.mult, ALU.add
                                                     ).then_inc(decay_vec, 1)
                if 4 <= n <= 11:
                    if n == 4:
                        v.wait_ge(scores_cleared, 1)
                        v.wait_ge(masks_ready, 1)
                    g = take(n - 4, g)
                    split_lo(n + 2, s)
                    if n < 11:
                        level_operand(n - 3)
                if 8 <= n <= 11:
                    v.wait_ge(evacuated, GB["w_in"] + 8 + 6 * (min(n, 9) - 4) + 2)
                    conv_tile(n - 8)

            for h in range(HH):
                for part in range(2):
                    v.wait_ge(groups_done, g + 1)
                    o = (6 * h + 3 * part) * P
                    nc.vector.tensor_copy(SC[:, o:o + 3 * P], ring[g % RING][:, 0:3 * P]).then_inc(evacuated, 1)
                    g += 1
            split_lo(15, 1)
            for k in range(4):
                xg_lo("w_out", k, 4 + k, tile(GBt, k), None)
            v.wait_ge(q_silu, 2)
            for h in range(HH):
                o = tile(CH, h)
                v.wait_ge(groups_done, g + 1)
                nc.vector.tensor_copy(o, ring[h][:, :]).then_inc(evacuated, 1)
                g += 1
                v.wait_ge(evacuated, g)
                nc.vector.tensor_tensor(tile(GC, h), o, o, ALU.mult).then_inc(osq_ready, 1)
                v.wait_ge(osq_ready, h + 1)
                nc.vector.scalar_tensor_tensor(o, o, col("hgrn_norm_g", h), tile(G, h), ALU.mult, ALU.mult
                                               ).then_inc(head_part, 1)
            v.wait_ge(head_part, HH)
            for h in range(HH + 1):
                if h < HH:
                    v.wait_ge(small_root, 2 + h)
                    nc.vector.tensor_tensor(tile(CH, h), tile(CH, h), tile(GC, h), ALU.mult).then_inc(mixa_ready, 1)
                if h:
                    xg_lo("w_out", 3 + h, h - 1, tile(CH, h - 1), None)

            def project(name, ksplit, dst, factor=None, xg=None, gain=None, goff=0, unroll=False):
                nk = len(ksplit)
                for i in steps(v, 2, unroll):
                    for b in range(2):
                        def ahead(j):
                            n = i * (2 * nk) + (UB[name] + b * nk + j + 2)
                            if not (unroll and n >= UNITS):
                                split_lo(n, (b * nk + j) % 2)
                        for j in range(nk - 1):
                            ahead(j)
                        for f in range(2):
                            gr = 2 * b + f
                            t = tile(dst, i * 4 + gr)
                            v.wait_ge(groups_done, i * 4 + (GB[name] + gr + 1))
                            if factor is None:
                                ins = nc.vector.tensor_copy(t, ring[gr][:, :])
                            else:
                                ins = nc.vector.scalar_tensor_tensor(t, ring[gr][:, :], factor, t,
                                                                     ALU.mult, ALU.add)
                            ins.then_inc(evacuated, 1)
                        if xg:
                            for f in range(2):
                                k = i * 4 + (2 * b + f)
                                xg_lo(xg, k, k, tile(dst, k), gain, k + goff)
                        ahead(nk - 1)

            def add_normed(y, gain, first, xg, next_gain):
                for k in range(DT + 2):
                    if k < DT:
                        nc.vector.scalar_tensor_tensor(tile(y, k), tile(y, k), col(gain, k), R[:, :],
                                                       ALU.mult, ALU.mult).then_inc(resid_part, 1)
                    if 1 <= k <= DT:
                        v.wait_ge(resid_part, first + k)
                        nc.vector.tensor_tensor(tile(xT, k - 1), tile(xT, k - 1), tile(y, k - 1), ALU.add
                                                ).then_inc(resid_ready, 1)
                    if k >= 2:
                        xg_lo(xg, k - 2, k - 2, tile(xT, k - 2), next_gain)

            project("w_out", [8], Y0)
            rstd("post_mix")
            add_normed(Y0, "post_mix_g", 0, "up0", "pre_ffn_g")

            def up(m, conv=False):
                name = f"up{m}"
                gb, hb = GB[name], FT * m
                with v.Fori(0, FT // 2) as i:
                    def conv_rest(f, half, dst):
                        n = 2 * half + f
                        u = tile(Ut, f)
                        v.wait_ge(tap_ready, i * 4 + (n + 1))
                        for tap, sh, signal in ((1, 1, conv_part), (0, 2, conv_ready)):
                            c = i * 2 + (tap * 2 * FT + half * FT + f)
                            if sh == 2:
                                v.wait_ge(conv_part, i * 4 + (n + 1))
                            nc.vector.scalar_tensor_tensor(dst[:, sh:T], u[:, 0:T - sh], cw[:, bass.ds(c, 1)],
                                                           dst[:, sh:T], ALU.mult, ALU.add).then_inc(signal, 1)
                    for f in range(2):
                        v.wait_ge(groups_done, i * 4 + (gb + f + 1))
                        nc.vector.tensor_tensor(tile(Ut if conv else Tt, f), ring[f][:, :], R[:, :], ALU.mult
                                                ).then_inc(evacuated, 1)
                    if conv:
                        for f in range(2):
                            conv_rest(f, 0, tile(Tt, f))
                    split_lo(i * 2 + (UB[name] + 2), 0)
                    if conv:
                        v.wait_ge(conv_ready, i * 4 + 2)
                    for f in range(2):
                        v.wait_ge(groups_done, i * 4 + (gb + f + 3))
                        nc.vector.tensor_tensor(tile(Ut if conv else At, f), ring[2 + f][:, :], R[:, :], ALU.mult
                                                ).then_inc(evacuated, 1)
                    for f in range(2):
                        if conv:
                            conv_rest(f, 1, tile(At, f))
                            v.wait_ge(conv_ready, i * 4 + (f + 3))
                        else:
                            v.wait_ge(evacuated, i * 4 + (gb + f + 3))
                        v.wait_ge(silu_ready, i * 2 + (hb + f + 1))
                        nc.vector.tensor_tensor(tile(At, f), tile(At, f), tile(Tt, f), ALU.mult
                                                ).then_inc(gated_ready, 1)
                    for f in range(2):
                        v.wait_ge(ahi_ready, i * 2 + (hb + f + 1))
                        nc.vector.tensor_tensor(tile(alo, i * 2 + f), tile(At, f),
                                                tile(ahi, i * 2 + f).bitcast(F32), ALU.subtract
                                                ).then_inc(act_ready, 1)
                    v.wait_ge(act_ready, i * 2 + (hb + 2))
                    if not conv:
                        split_lo(i * 2 + (UB[name] + 3), 1)

            rstd("pre_ffn")
            up(0, conv=True)
            project("down0", DOWN, Y1)
            rstd("post_ffn")
            add_normed(Y1, "post_ffn_g", DT, "up1", "ffn_pre_norm_2")
            rstd("pre0")
            up(1)
            project("down1", DOWN, xT, 0.5)
            nc.vector.memset(PU[:, :].rearrange("p (k t) -> p k t", t=PW)[:, :, 0:16], 0.0).then_inc(pool_step, 1)
            for t in (PA, PB):
                nc.vector.memset(t[:, :].rearrange("p (k t) -> p k t", t=PW)[:, :, 0:16], 0.0).then_inc(pool_step, 1)
            pool_steps = [3]

            def pool_do(ins):
                ins.then_inc(pool_step, 1)
                pool_steps[0] += 1

            rstd("mix0")
            v.wait_ge(inv_loaded, 16)
            for k in range(DT):
                pool_do(nc.vector.scalar_tensor_tensor(PU[:, k * PW + 16:(k + 1) * PW], tile(xT, k),
                                                       col("mix_norm_2", k), R[:, :], ALU.mult, ALU.mult))
            for w in range(4):
                u = PU[:, 2 * w * PW:2 * (w + 1) * PW].rearrange("p (k t) -> p k t", t=PW)
                cur = u
                v.wait_ge(xg_ready, XG["pool"] + 2 * w)
                for step in range(w + 1):
                    dst = (PA, PB)[step % 2][:, :].rearrange("p (k t) -> p k t", t=PW)
                    back = 1 << step
                    v.wait_ge(pool_step, pool_steps[0])
                    pool_do(nc.vector.tensor_tensor(dst[:, :, 16:PW], cur[:, :, 16:PW], cur[:, :, 16 - back:PW - back],
                                                    ALU.add))
                    cur = dst
                v.wait_ge(pool_step, pool_steps[0])
                edge = PE16[:, :].rearrange("p (k t) -> p k t", k=2)
                count = inv[:, w * 16:(w + 1) * 16].rearrange("p (k t) -> p k t", k=1).to_broadcast([P, 2, 16])
                pool_do(nc.vector.tensor_tensor(edge, cur[:, :, 16:32], count, ALU.mult))
                v.wait_ge(pool_step, pool_steps[0])
                pool_do(nc.vector.scalar_tensor_tensor(cur[:, :, 16:PW], cur[:, :, 16:PW], 0.5 ** (w + 1),
                                                       u[:, :, 16:PW], ALU.mult, ALU.subtract))
                v.wait_ge(pool_step, pool_steps[0])
                nc.vector.tensor_tensor(cur[:, :, 16:32], edge, u[:, :, 16:32], ALU.subtract).then_inc(pool_ready, 1)
                v.wait_ge(pool_ready, w + 1)
                for kt in range(2):
                    xg_lo("pool", 2 * w + kt, 2 * w + kt, cur[:, kt, 16:PW], None)
            for u in range(2):
                for n in range(4):
                    k = 4 * u + n
                    v.wait_ge(groups_done, GB["pool"] + k + 1)
                    nc.vector.scalar_tensor_tensor(tile(xT, k), ring[n][:, :], col("pool_scale_2", k), tile(xT, k),
                                                   ALU.mult, ALU.add).then_inc(evacuated, 1)
                split_lo(UB["pool"] + u + 2, u)
            for k in range(DT):
                xg_lo("up2", k, k, tile(xT, k), "ffn_post_norm_2")
            rstd("post0")
            up(2)
            project("down2", DOWN, xT, 0.5, "kv", "kv_in_norm_2")
            rstd("kv_pre1")
            g = GB["kv"]
            ck, krope = Ut[:, 0:T], Ut[:, T:2 * T]
            k0, k1 = kvt[:, 0:T], kvt[:, T:2 * T]
            v.wait_ge(groups_done, g + 2)
            nc.vector.tensor_tensor(ck, ring[0][:, :], R[:, :], ALU.mult).then_inc(evacuated, 2)
            split_lo(UB["kv"] + 2, 0)
            v.wait_ge(evacuated, g + 2)
            v.wait_ge(groups_done, g + 4)
            nc.vector.tensor_tensor(krope, ring[1][:, :], R[:, :], ALU.mult).then_inc(evacuated, 2)
            nc.vector.tensor_tensor(k0, ck, ck, ALU.mult).then_inc(small_step, 1)
            for k in range(DT):
                xg_lo("up3", k, k, tile(xT, k), "ffn_pre_norm_2", 8 + k)
            split_lo(UB["kv"] + 3, 1)
            v.wait_ge(rope_kv_loaded, 16)
            v.wait_ge(key_turned, 1)
            nc.vector.tensor_tensor(k0, banks[7][:, :], rope_kv[:, T:2 * T], ALU.mult).then_inc(ck_ready, 1)
            nc.vector.tensor_tensor(krope, krope, rope_kv[:, 0:T], ALU.mult).then_inc(ck_ready, 1)
            v.wait_ge(ck_ready, 2)
            nc.vector.tensor_tensor(krope, krope, k0, ALU.add).then_inc(ck_ready, 1)
            v.wait_ge(small_root, 6)
            nc.vector.scalar_tensor_tensor(ck, ck, col("ckv_norm_2", 0), k1, ALU.mult, ALU.mult).then_inc(ck_ready, 1)
            up(3)
            project("down3", DOWN, xT, 0.5, "dq", "mix_norm_2", 8)
            v.wait_ge(groups_done, GB["dq"])
            nc.vector.memset(Tt[64:128, 0:T], 0.0)
            nc.vector.memset(Tt[0:64, T:2 * T], 0.0)
            v.wait_ge(ck_ready, 4)
            nc.vector.tensor_copy(Tt[0:64, 0:T], Ut[0:64, T:2 * T])
            nc.vector.tensor_copy(Tt[64:128, T:2 * T], Ut[64:128, T:2 * T]).then_inc(latent_ready, 1)

            def latent_lo(j):
                v.wait_ge(latent_hi, j + 1)
                hi = ckhi[:, :] if j == 0 else tile(cqhi, j - 1)
                lo = cklo[:, :] if j == 0 else tile(cqlo, j - 1)
                src = Ut[:, 0:T] if j == 0 else tile(At, j - 1)
                nc.vector.tensor_tensor(lo, src, hi.bitcast(F32), ALU.subtract).then_inc(latent_split, 1)

            rstd("mix1")
            g = GB["dq"]
            for u in range(2):
                v.wait_ge(groups_done, g + (1, 4)[u])
                nc.vector.tensor_tensor(tile(At, u), ring[u][:, :], R[:, :], ALU.mult).then_inc(evacuated, (1, 3)[u])
                v.wait_ge(evacuated, g + (1, 4)[u])
                nc.vector.tensor_tensor(tile(PT, u), tile(At, u), tile(At, u), ALU.mult).then_inc(small_step, 1)
                split_lo(UB["dq"] + u + 2, u)
                if u == 0:
                    latent_lo(0)
            r = tile(PT, 0)
            v.wait_ge(small_root, 7)
            for u in range(2):
                nc.vector.scalar_tensor_tensor(tile(At, u), tile(At, u), col("q_lora_norm_2", u), r,
                                               ALU.mult, ALU.mult).then_inc(latent_ready, 1)
            for j in range(1, 1 + QR):
                latent_lo(j)

            scale = float((NOPE + ROPE) ** -0.5)
            v.wait_ge(rope_q_loaded, 16)
            gb = GB["attn"]
            with v.Fori(0, QUARTERS) as q:
                for n in range(12):
                    v.wait_ge(groups_done, q * 16 + (gb + n + 1))
                    dst = (KN, VV, QN)[n // 4]
                    nc.vector.tensor_copy(tile(dst, n % 4), ring[n % RING][:, :]).then_inc(evacuated, 1)
                split_lo(q * 2 + (UB["attn"] + 2), 0)
                for j in range(2):
                    v.wait_ge(groups_done, q * 16 + (gb + 13 + j))
                    nc.vector.tensor_copy(tile(QRr, j), ring[j][:, :]).then_inc(evacuated, 1)
                split_lo(q * 2 + (UB["attn"] + 3), 1)
                for j in range(2):
                    v.wait_ge(groups_done, q * 16 + (gb + 15 + j))
                    nc.vector.tensor_tensor(tile(QRt, j), ring[2 + j][:, :], rope_q[:, T:2 * T], ALU.mult
                                            ).then_inc(evacuated, 1)
                    nc.vector.tensor_tensor(tile(QRr, j), tile(QRr, j), rope_q[:, 0:T], ALU.mult
                                            ).then_inc(qrope_part, 1)
                    v.wait_ge(qrope_part, q * 2 + (j + 1))
                    v.wait_ge(evacuated, q * 16 + (gb + 15 + j))
                    nc.vector.tensor_tensor(tile(QRt, j), tile(QRt, j), tile(QRr, j), ALU.add
                                            ).then_inc(qrope_ready, 1)

                def maxes(h):
                    for i in range(TC):
                        e, c = 4 * h + i, 4 * (h % 2) + i
                        v.wait_ge(scores_ready, q * 16 + (e + 1))
                        nc.vector.tensor_reduce(rowmax[:, c:c + 1], ring[i][:, 0:(i + 1) * P], AX_X, ALU.max
                                                ).then_inc(max_part, 1)
                        v.wait_ge(max_part, q * 16 + (e + 1))
                        nc.vector.tensor_scalar(negmax[:, c:c + 1], rowmax[:, c:c + 1], -scale, None, ALU.mult
                                                ).then_inc(negmax_ready, 1)

                def normalise(h):
                    c0 = 4 * (h % 2)
                    v.wait_ge(exp_ready, q * 16 + (4 * h + 4))
                    nc.vector.reciprocal(rowinv[:, c0:c0 + 4], rowsum[:, c0:c0 + 4]).then_inc(recip_ready, 1)
                    v.wait_ge(recip_ready, q * 4 + (h + 1))
                    for i in range(TC):
                        off = i * (i + 1) // 2 * P
                        pr = probs(h)[:, off:off + (i + 1) * P]
                        nc.vector.tensor_scalar(pr, pr, rowinv[:, c0 + i:c0 + i + 1], None, ALU.mult
                                                ).then_inc(probs_ready, 1)

                maxes(0)
                normalise(0)
                for h in range(4):
                    if h < 3:
                        maxes(h + 1)
                    v.wait_ge(turned_ready, q * 12 + (3 * h + 2))
                    nc.vector.tensor_copy(PT[:, 4 * P:7 * P], banks[5][:, 0:3 * P]).then_inc(turned_vec, 1)
                    if h < 3:
                        normalise(h + 1)
                    v.wait_ge(outhi_ready, q * 4 + (h + 1))
                    nc.vector.tensor_tensor(tile(oTlo, q * 4 + h), banks[7][:, :],
                                            tile(oThi, q * 4 + h).bitcast(F32), ALU.subtract
                                            ).then_inc(outlo_ready, 1)
            project("w_o", [8, 8], xT, 1.0, "up4", "ffn_post_norm_2", 8)
            rstd("post1")
            up(4)
            project("down4", DOWN, xT, 0.5, unroll=True)
            rstd("final")
            for k in range(DT):
                nc.vector.scalar_tensor_tensor(tile(Z, k), tile(xT, k), col("final_norm_2", k), R[:, :],
                                               ALU.mult, ALU.mult).then_inc(normed_out, 1)
            g = GB["x_out"]
            for n in range(2 * TC):
                v.wait_ge(groups_done, g + n + 1)
                nc.vector.tensor_copy(ob[:, n * T:(n + 1) * T], ring[n % RING][:, :]).then_inc(evacuated, 1)


def constants():
    import numpy as np

    s, t = np.arange(P)[:, None], np.arange(P)[None, :]
    masks = [s == t]
    for h in LEVELS:
        masks.append((s // (2 * h) == t // (2 * h)) & (s % (2 * h) < h) & (t % (2 * h) >= h))
    perm = np.zeros((P, P), np.float32)
    for m in range(P):
        if m % ROPE < ROPE // 2:
            perm[m + ROPE // 2, m] = -1.0
        else:
            perm[m - ROPE // 2, m] = 1.0
    freq = np.float32(10000.0) ** (-np.arange(0, ROPE, 2, dtype=np.float32) / np.float32(ROPE))
    ang = (np.arange(T, dtype=np.float32)[None, :] * freq[:, None]).astype(np.float32)
    rope = np.concatenate([np.tile(np.cos(ang), (4, 1)), np.tile(np.sin(ang), (4, 1))], 1).astype(np.float32)
    count = np.stack([1.0 / np.minimum(np.arange(1, 17), w) for w in (2, 4, 8, 16)])
    return {
        "ident": np.eye(P, dtype=np.float32), "perm": perm,
        "causal": np.where(t <= s, 0.0, -1e30).astype(np.float32),
        "masks": np.concatenate([m.astype(np.int32) for m in masks], 1),
        "rope": rope, "inv_count": count.astype(np.float32).reshape(1, 4 * 16),
    }


_INS = ["x", "lb_param", "w_in", "w_out", "conv_w", "ffn_w_up", "ffn_conv_w", "ffn_w_down", "hgrn_norm_g",
        "pre_mix_g", "post_mix_g", "pre_ffn_g", "post_ffn_g", "ffn_pre_norm_2", "ffn_pre_wg_2", "ffn_pre_wu_2",
        "ffn_pre_wd_2", "mix_norm_2", "ffn_post_norm_2", "ffn_post_wg_2", "ffn_post_wu_2", "ffn_post_wd_2",
        "pool_w_2", "pool_scale_2", "kv_in_norm_2", "w_dkv_2", "ckv_norm_2", "w_uk_2", "w_uv_2",
        "q_lora_norm_2", "w_dq_2", "w_uq_2", "w_o_2", "final_norm_2"]


def kernel(**inputs):
    import numpy as _np
    import concourse.bacc as _bacc
    from concourse import mybir as _mybir
    from concourse.bass_utils import run_bass_kernel_spmd as _run

    nc = _bacc.Bacc("TRN2", target_bir_lowering=False, num_devices=1)
    arrays, args = {}, {}
    given = {name: inputs[name] for name in _INS}
    given.update(constants())
    for name, value in given.items():
        a = _np.ascontiguousarray(value)
        arrays[f"in_{name}_dram"] = a
        args[name] = nc.dram_tensor(f"in_{name}_dram", a.shape, _mybir.dt.from_np(a.dtype),
                                    kind="ExternalInput").ap()
    out = nc.dram_tensor("out_0_dram", (1, T, D), _mybir.dt.float32, kind="ExternalOutput").ap()
    build(nc, args, out)
    r = _run(nc, [arrays], core_ids=[0])
    return r.results[0]["out_0_dram"]
```

```python
from contextlib import ExitStack

import concourse.bass as bass
from concourse import mybir

F32 = mybir.dt.float32
F32R = mybir.dt.float32r
BF16 = mybir.dt.bfloat16
U8 = mybir.dt.uint8
ACT = mybir.ActivationFunctionType
ALU = mybir.AluOpType
AX_X = mybir.AxisListType.X

P = 128
T = 512
D = 1024
DT = D // P
FF = 2816
FT = FF // P
TC = T // P
UC = 256
UNIT = DT * UC
HH = 4
NH = 16
NOPE = 128
ROPE = 64
QR = 2
EPS = 1e-6
RING = 4
LOG_EXP = "natural_log_exp_and_others"
LEVELS = [1, 2, 4, 8, 16, 32, 64]
QUARTERS = 4
DOWN = [8, 8, 6]

VECTORS = [("pre_mix_g", 8), ("post_mix_g", 8), ("pre_ffn_g", 8), ("post_ffn_g", 8),
           ("ffn_pre_norm_2", 16), ("mix_norm_2", 16), ("ffn_post_norm_2", 16), ("pool_scale_2", 8),
           ("kv_in_norm_2", 8), ("ckv_norm_2", 1), ("q_lora_norm_2", 2), ("final_norm_2", 8),
           ("hgrn_norm_g", 4), ("conv_w", 12)]
COL = {}
_at = 0
for _name, _n in VECTORS:
    COL[_name] = _at
    _at += _n
NVEC = _at

PHASES = [("x_in", 0, 8), ("w_in", 14, 64), ("cross", 0, 8), ("state_out", 0, 4), ("w_out", 4, 8),
          ("up0", 22, 44), ("down0", 12, 8),
          ("up1", 22, 44), ("down1", 12, 8), ("pool", 2, 8), ("up2", 22, 44), ("down2", 12, 8),
          ("kv", 2, 4), ("up3", 22, 44), ("down3", 12, 8), ("dq", 2, 4), ("attn", 8, 64),
          ("w_o", 8, 8), ("up4", 22, 44), ("down4", 12, 8), ("x_out", 0, 8)]
UB, GB = {}, {}
_u = _g = 0
for _name, _nu, _ng in PHASES:
    UB[_name], GB[_name] = _u, _g
    _u += _nu
    _g += _ng
UNITS = _u
MB, _m = {}, 0
for _name, _nk in [("w_out", 1), ("down0", 3), ("down1", 3), ("down2", 3), ("down3", 3), ("w_o", 2), ("down4", 3)]:
    MB[_name] = _m
    _m += 4 * (_nk - 1)

XG = {n: 8 * j for j, n in enumerate(["w_in", "w_out", "up0", "up1", "pool", "up2", "kv", "up3", "dq", "up4"])}
POOL_ORDER = [0, 3, 1, 2]
MIXED_ORDER = [0, 1, 2, 3, 6, 7, 4, 5]
NORM = {n: j for j, n in enumerate(["pre_mix", "post_mix", "pre_ffn", "post_ffn", "pre0", "mix0", "post0",
                                    "kv_pre1", "mix1", "post1", "final"])}
ADDS = {n: DT - 2 if n in ("pre_mix", "post_mix", "post_ffn", "final") else DT - 1 for n in NORM}
ADDED = {n: sum(ADDS[m] for m in NORM if NORM[m] < NORM[n]) for n in NORM}
BEFORE = {n: ([None] + list(NORM))[NORM[n]] for n in NORM}


def steps(eng, n, unroll=False):
    if unroll:
        for i in range(n):
            yield i
    else:
        with eng.Fori(0, n) as i:
            yield i


def build(nc, A, out):
    ctx = ExitStack()
    with ctx:
        def sb(name, shape, dt=F32, where=ctx):
            return where.enter_context(nc.sbuf_tensor(name, shape, dt))

        def sem(name):
            return ctx.enter_context(nc.semaphore(name))

        xT = sb("xT", [P, DT * T])
        raw = sb("raw", [P, 2 * UNIT])
        whi = sb("whi", [P, 2 * UNIT], F32R)
        wlo = sb("wlo", [P, 2 * UNIT], F32R)
        R = sb("R", [P, T])
        acc = sb("acc", [P, T])
        sq = sb("sq", [P, 2 * T])
        work = sb("work", [P, 6 * T])
        Tt, At, Ut = (work[:, 2 * j * T:2 * (j + 1) * T] for j in range(3))
        cols = sb("cols", [P, NVEC])
        cw = sb("cw", [P, 3 * 2 * FT])
        ident = sb("ident", [P, P])
        ones = sb("ones", [P, P])
        eps = sb("eps", [P, 1])
        perm = sb("perm", [P, P])
        identb = sb("identb", [P, P], BF16)
        causal = sb("causal", [P, P], BF16)
        rcol = sb("rcol", [P, TC])
        ends = sb("ends", [P, HH * TC])
        rowmax = sb("rowmax", [P, 8])
        negmax = sb("negmax", [P, 8])
        rowinv = sb("rowinv", [P, 8])
        rowsum = sb("rowsum", [P, 8])
        flex = ExitStack()
        xghi = sb("xghi", [P, DT * T], F32R, flex)
        xglo = sb("xglo", [P, DT * T], F32R, flex)
        act = ExitStack()
        ahi = sb("ahi", [P, FT * T], F32R, act)
        alo = sb("alo", [P, FT * T], F32R, act)
        act.close()
        hg = ExitStack()
        fkb = sb("fkb", [P, 2 * 2048], F32, hg)
        Q = sb("Q", [P, 2048], F32, hg)
        V = sb("V", [P, TC * 512], F32, hg)
        G = sb("G", [P, 2048], F32, hg)
        GBt = sb("GBt", [P, 2048], F32, hg)
        GC = sb("GC", [P, 2048], F32, hg)
        CH = sb("CH", [P, 2048], F32, hg)
        SD = sb("SD", [P, HH * TC * P], F32, hg)
        SC = sb("SC", [P, HH * 6 * P], F32, hg)
        masks = sb("masks", [P, 8 * P], U8, hg)
        LG, EX = SC[:, 0:2048], V[:, :]
        hg.close()
        yb = ExitStack()
        Y0 = sb("Y0", [P, DT * T], F32, yb)
        rows = sb("rows", [P, 3 * P], F32, yb)
        wide_causal = sb("wide_causal", [P, P], F32, yb)
        wide_masks = sb("wide_masks", [P, 8 * P], mybir.dt.int32, yb)
        yb.close()
        pl = ExitStack()
        PW = 16 + T
        PU = sb("PU", [P, DT * PW], F32, pl)
        PW2 = sb("PW2", [P, 4 * 2 * 2 * PW], F32, pl)
        inv = sb("inv", [P, 4 * 16], F32, pl)
        edges = sb("edges", [P, 4 * 2 * 16], F32, pl)
        pl.close()
        kv = ExitStack()
        rope_kv = sb("rope_kv", [P, 2 * T], F32, kv)
        kvt = sb("kvt", [P, 2 * T], F32, kv)
        kv.close()
        fin = ExitStack()
        Z = sb("Z", [P, DT * T], F32, fin)
        ob = sb("ob", [P, TC * D], F32, fin)
        fin.close()
        flex.close()
        f2 = ExitStack()
        Y1 = sb("Y1", [P, DT * T], F32, f2)
        f2.close()
        at = ExitStack()
        KN = sb("KN", [P, 4 * T], F32, at)
        QN = sb("QN", [P, 4 * T], F32, at)
        VV = sb("VV", [P, TC * 512], F32, at)
        QRt = sb("QRt", [P, 2 * T], F32, at)
        Prb = sb("Prb", [P, 10 * P], F32, at)
        oThi = sb("oThi", [P, NH * T], F32R, at)
        oTlo = sb("oTlo", [P, NH * T], F32R, at)
        rope_q = sb("rope_q", [P, 2 * T], F32, at)
        ckhi = sb("ckhi", [P, T], F32R, at)
        cklo = sb("cklo", [P, T], F32R, at)
        cqhi = sb("cqhi", [P, QR * T], F32R, at)
        cqlo = sb("cqlo", [P, QR * T], F32R, at)
        PT = sb("PT", [P, 10 * P], F32, at)
        at.close()
        QRr = Prb[:, 0:2 * T]

        def probs(h):
            return work[:, 2 * T:2 * T + 10 * P] if h % 2 == 0 else Prb[:, :]

        banks = [ctx.enter_context(nc.psum_tensor(f"bank{b}", [P, 512], F32)) for b in range(8)]
        ring, stat, misc = banks[:RING], banks[4], banks[5]

        x_loaded = [sem(f"x_loaded{c}") for c in range(TC)]
        first_row_loaded = sem("first_row_loaded")
        first_turned = sem("first_turned")
        first_gain = sem("first_gain")
        rows_loaded = sem("rows_loaded")
        ident_loaded = sem("ident_loaded")
        consts_loaded = sem("consts_loaded")
        ones_ready = sem("ones_ready")
        cols_turned = sem("cols_turned")
        cols_ready = sem("cols_ready")
        part_loaded = sem("part_loaded")
        raw_ready = [sem("raw_ready0"), sem("raw_ready1")]
        whi_ready = [sem("whi_ready0"), sem("whi_ready1")]
        wlo_ready = [sem("wlo_ready0"), sem("wlo_ready1")]
        parts_used = sem("parts_used")
        groups_done = sem("groups_done")
        evacuated = sem("evacuated")
        resid_part = sem("resid_part")
        resid_ready = sem("resid_ready")
        square_ready = sem("square_ready")
        acc_added = sem("acc_added")
        head_sums = sem("head_sums")
        key_sums = sem("key_sums")
        query_sums = sem("query_sums")
        key_turned = sem("key_turned")
        sums_ready = sem("sums_ready")
        rstd_log = sem("rstd_log")
        rstd_ready = sem("rstd_ready")
        small_log = sem("small_log")
        small_root = sem("small_root")
        rcol_sums = sem("rcol_sums")
        xghi_ready = sem("xghi_ready")
        xg_ready = sem("xg_ready")
        tap_ready = sem("tap_ready")
        conv_part = sem("conv_part")
        conv_ready = sem("conv_ready")
        silu_ready = sem("silu_ready")
        gated_ready = sem("gated_ready")
        ahi_ready = sem("ahi_ready")
        act_ready = sem("act_ready")
        decay_vec = sem("decay_vec")
        decay_act = sem("decay_act")
        q_silu = sem("q_silu")
        mixb_part = sem("mixb_part")
        mixb_ready = sem("mixb_ready")
        level_arg = sem("level_arg")
        scores_cleared = sem("scores_cleared")
        masks_ready = sem("masks_ready")
        level_exp = sem("level_exp")
        level_ready = sem("level_ready")
        cross_arg = sem("cross_arg")
        cross_exp = sem("cross_exp")
        cross_ready = sem("cross_ready")
        osq_ready = sem("osq_ready")
        head_part = sem("head_part")
        mixa_ready = sem("mixa_ready")
        pads_ready = sem("pads_ready")
        far_step = sem("far_step")
        pool_step = sem("pool_step")
        mixed_ready = sem("mixed_ready")
        inv_loaded = sem("inv_loaded")
        small_step = sem("small_step")
        ck_ready = sem("ck_ready")
        rope_kv_loaded = sem("rope_kv_loaded")
        rope_q_loaded = sem("rope_q_loaded")
        latent_ready = sem("latent_ready")
        latent_hi = sem("latent_hi")
        latent_split = sem("latent_split")
        qrope_part = sem("qrope_part")
        qrope_ready = sem("qrope_ready")
        scores_ready = sem("scores_ready")
        max_part = sem("max_part")
        negmax_ready = sem("negmax_ready")
        exp_ready = sem("exp_ready")
        recip_ready = sem("recip_ready")
        probs_ready = sem("probs_ready")
        turned_ready = sem("turned_ready")
        turned_act = sem("turned_act")
        turned_vec = sem("turned_vec")
        out_ready = sem("out_ready")
        outhi_ready = sem("outhi_ready")
        outlo_ready = sem("outlo_ready")
        normed_out = sem("normed_out")
        stored = sem("stored")

        block = ctx.enter_context(nc.Block())

        def tile(t, k, n=T):
            return t[:, k * n:(k + 1) * n] if isinstance(k, int) else t[:, bass.ds(k * n, n)]

        def col(name, k):
            c = COL[name] + k
            return cols[:, c:c + 1] if isinstance(c, int) else cols[:, bass.ds(c, 1)]

        def slot(t, n, kt=DT, width=UC):
            return t[:, n * UNIT:n * UNIT + kt * width].rearrange("p (k c) -> p k c", k=kt)

        def zeros_before(t):
            return t[:, :].rearrange("p (k t) -> p k t", t=PW)[:, :, 0:16]

        def window(w, step):
            if step < 0:
                t = PU[:, 2 * w * PW:2 * (w + 1) * PW]
            else:
                t = PW2[:, (4 * w + 2 * (step % 2)) * PW:(4 * w + 2 * (step % 2) + 2) * PW]
            return t.rearrange("p (k t) -> p k t", t=PW)

        def window_step(engine, w, step):
            t, back = window(w, step - 1), 1 << step
            return engine.tensor_tensor(window(w, step)[:, :, 16:PW], t[:, :, 16:PW], t[:, :, 16 - back:PW - back],
                                        ALU.add)

        def tap_col(i, tap, half, f):
            c = tap * 2 * FT + half * FT + f
            return cw[:, c + 2 * i:c + 2 * i + 1] if isinstance(i, int) else cw[:, bass.ds(i * 2 + c, 1)]

        def split_count(n, s):
            return n - s + 2

        fk, lb_ = fkb[:, 0:2048], fkb[:, 2048:4096]

        @block.sync
        def _(sp):
            xtok = fkb[:, :].rearrange("p (c d) -> p c d", c=TC)
            for c in range(TC):
                sp.dma_start(xtok[:, c, :], A["x"][0, c * P:(c + 1) * P, :]).then_inc(x_loaded[c], 16)

            def load(n, s, pieces):
                if not (isinstance(n, int) and n < 2):
                    sp.wait_ge(wlo_ready[s], split_count(n, s) - 2)
                for dst, src in pieces[:-1]:
                    sp.dma_start(dst, src).then_inc(part_loaded, 16)
                    parts[0] += 16
                if len(pieces) > 1:
                    sp.wait_ge(part_loaded, parts[0])
                sp.dma_start(*pieces[-1]).then_inc(raw_ready[s], 16)

            parts = [0]
            win = A["w_in"][0].rearrange("(k p) c -> p k c", p=P)
            for j, part in enumerate([1, 0, 5, 6, 4, 3, 2]):
                for u in range(2):
                    c0 = part * 512 + u * UC
                    load(2 * j + u, u, [(slot(raw, u), win[:, :, c0:c0 + UC])])
                if j == 0:
                    for dst, name in ((wide_masks, "masks"), (wide_causal, "causal"), (perm, "perm")):
                        sp.dma_start(dst[:, :], A[name]).then_inc(consts_loaded, 16)

            def column_blocks(name, w, ksplit, unroll=False):
                nk = len(ksplit)
                for i in steps(sp, 2, unroll):
                    for b in range(2):
                        k0 = 0
                        for j, kt in enumerate(ksplit):
                            s = (b * nk + j) % 2
                            c0 = i * (2 * UC) + b * UC
                            src = w[:, k0:k0 + kt, c0:c0 + UC] if isinstance(c0, int) else \
                                w[:, k0:k0 + kt, bass.ds(c0, UC)]
                            load(i * (2 * nk) + (UB[name] + b * nk + j), s, [(slot(raw, s, kt), src)])
                            k0 += kt

            def up(name, wg, wu):
                with sp.Fori(0, FF // UC) as i:
                    for s, w in enumerate((wg, wu)):
                        load(i * 2 + (UB[name] + s), s, [(slot(raw, s), w[:, :, bass.ds(i * UC, UC)])])

            def kp(w):
                return w.rearrange("(k p) c -> p k c", p=P)

            column_blocks("w_out", kp(A["w_out"][0]), [8])
            up0 = kp(A["ffn_w_up"][0])
            up("up0", up0[:, :, 0:FF], up0[:, :, FF:2 * FF])
            column_blocks("down0", kp(A["ffn_w_down"][0]), DOWN)

            def ffn(n, which, l, unroll=False):
                up(f"up{n}", kp(A[f"ffn_{which}_wg_2"][l]), kp(A[f"ffn_{which}_wu_2"][l]))
                column_blocks(f"down{n}", kp(A[f"ffn_{which}_wd_2"][l]), DOWN, unroll)

            ffn(1, "pre", 0)
            for u in range(2):
                load(UB["pool"] + u, u, [(slot(raw, u, 4)[:, 2 * j:2 * j + 2, :],
                                          A["pool_w_2"][0, POOL_ORDER[2 * u + j]].rearrange(
                                              "(t p) c -> p t c", p=P)) for j in range(2)])
            sp.wait_ge(groups_done, GB["pool"])
            sp.dma_start(inv[:, :], A["inv_count"].to_broadcast([P, 4 * 16])).then_inc(inv_loaded, 16)
            ffn(2, "post", 0)
            dkv = kp(A["w_dkv_2"])
            load(UB["kv"], 0, [(slot(raw, 0, DT, P), dkv[:, :, 0:P])])
            kr = slot(raw, 1, DT, P)
            load(UB["kv"] + 1, 1, [(kr[:, :, 0:ROPE], dkv[:, :, P:P + ROPE]),
                                   (kr[:, :, ROPE:P], dkv[:, :, P:P + ROPE])])
            sp.wait_ge(groups_done, GB["kv"])
            sp.dma_start(rope_kv[:, :], A["rope"]).then_inc(rope_kv_loaded, 16)
            ffn(3, "pre", 1)
            dq = kp(A["w_dq_2"][0])
            for u in range(2):
                load(UB["dq"] + u, u, [(slot(raw, u, DT, P), dq[:, :, u * P:(u + 1) * P])])
            sp.wait_ge(groups_done, GB["dq"])
            sp.dma_start(rope_q[:, :], A["rope"]).then_inc(rope_q_loaded, 16)
            uk = A["w_uk_2"].rearrange("r h d -> r (h d)")
            uv = A["w_uv_2"].rearrange("r h d -> r (h d)")
            uq = A["w_uq_2"][0].rearrange("(t p) h e -> p t h e", p=P)
            r0, r1 = raw[:, 0:UNIT], raw[:, UNIT:UNIT + 512]
            with sp.Fori(0, QUARTERS) as q:
                sp.wait_ge(wlo_ready[0], split_count(q * 2 + UB["attn"], 0) - 2)
                base = parts[0]
                sp.dma_start(r0[:, 0:512], uk[:, bass.ds(q * 512, 512)]).then_inc(part_loaded, 16)
                sp.dma_start(r0[:, 512:1024], uv[:, bass.ds(q * 512, 512)]).then_inc(part_loaded, 16)
                sp.dma_start(r0[:, 1024:1536].rearrange("p (h e) -> p h e", h=4),
                             uq[:, 0, bass.ds(q * 4, 4), 0:NOPE]).then_inc(part_loaded, 16)
                sp.wait_ge(part_loaded, q * 64 + (base + 48))
                sp.dma_start(r0[:, 1536:2048].rearrange("p (h e) -> p h e", h=4),
                             uq[:, 1, bass.ds(q * 4, 4), 0:NOPE]).then_inc(raw_ready[0], 16)
                sp.wait_ge(wlo_ready[1], split_count(q * 2 + (UB["attn"] + 1), 1) - 2)
                sp.dma_start(r1[:, 0:256].rearrange("p (h e) -> p h e", h=4),
                             uq[:, 0, bass.ds(q * 4, 4), NOPE:NOPE + ROPE]).then_inc(part_loaded, 16)
                sp.wait_ge(part_loaded, q * 64 + (base + 64))
                sp.dma_start(r1[:, 256:512].rearrange("p (h e) -> p h e", h=4),
                             uq[:, 1, bass.ds(q * 4, 4), NOPE:NOPE + ROPE]).then_inc(raw_ready[1], 16)
            column_blocks("w_o", kp(A["w_o_2"][0]), [8, 8])
            ffn(4, "post", 1)
            for c in range(TC):
                sp.wait_ge(evacuated, GB["x_out"] + 2 * (c + 1))
                sp.dma_start(out[0, c * P:(c + 1) * P, :], ob[:, c * D:(c + 1) * D]).then_inc(stored, 16)
            sp.wait_ge(stored, 16 * TC)

        @block.gpsimd
        def _(pool):
            nc.gpsimd.memset(ones[:, :], 1.0).then_inc(ones_ready, 1)
            nc.gpsimd.memset(eps[:, :], EPS).then_inc(ones_ready, 1)

            def split_lo(n, s):
                pool.wait_ge(whi_ready[s], split_count(n, s))
                c = slice(s * UNIT, (s + 1) * UNIT)
                nc.gpsimd.tensor_tensor(wlo[:, c], raw[:, c], whi[:, c].bitcast(F32), ALU.subtract
                                        ).then_inc(wlo_ready[s], 2)

            def sum_squares(name, splits=()):
                j = NORM[name]
                if j:
                    pool.wait_ge(sums_ready, j)
                for k in range(1, ADDS[name] + 1):
                    if k == 4 and splits:
                        split_lo(splits[0], 1)
                    pool.wait_ge(square_ready, DT * j + k + 1)
                    a0 = sq[:, 0:T] if k == 1 else acc[:, :]
                    if k > 1:
                        pool.wait_ge(acc_added, ADDED[name] + k - 1)
                    nc.gpsimd.tensor_tensor(acc[:, :], a0, tile(sq, k % 2), ALU.add).then_inc(acc_added, 1)
                if splits:
                    split_lo(splits[1], 1)

            def last_splits(name, nk):
                return [UB[name] + 2 * nk * (i + 1) + 1 for i in range(2)]

            sum_squares("pre_mix")
            pool.wait_ge(decay_vec, 2 + HH * TC)
            for l, hs in enumerate(LEVELS):
                b = lb_.rearrange("p (n two h) -> p n two h", two=2, h=hs)
                e = EX.rearrange("p (n two h) -> p n two h", two=2, h=hs)
                ref = b[:, :, 0, hs - 1:hs].to_broadcast([P, 2048 // (2 * hs), hs])
                if l:
                    pool.wait_ge(level_ready, 2 * l)
                nc.gpsimd.tensor_tensor(e[:, :, 0, :], ref, b[:, :, 0, :], ALU.subtract).then_inc(level_arg, 1)
                nc.gpsimd.tensor_tensor(e[:, :, 1, :], b[:, :, 1, :], ref, ALU.subtract).then_inc(level_arg, 1)
            pool.wait_ge(evacuated, GB["w_in"] + 56)
            b3 = lb_.rearrange("p (c t) -> p c t", t=P)
            nc.gpsimd.tensor_tensor(LG.rearrange("p (c t) -> p c t", t=P),
                                    b3[:, :, P - 1:P].to_broadcast([P, HH * TC, P]), b3, ALU.subtract
                                    ).then_inc(cross_arg, 1)
            sum_squares("post_mix", last_splits("w_out", 1))
            sum_squares("pre_ffn")

            with pool.Fori(0, FT // 2) as i:
                split_lo(i * 2 + (UB["up0"] + 3), 1)
            sum_squares("post_ffn", last_splits("down0", len(DOWN)))
            for name in ("pre0", "mix0"):
                sum_squares(name)
            pool.wait_ge(groups_done, GB["pool"])
            nc.gpsimd.memset(zeros_before(PU), 0.0).then_inc(pads_ready, 1)
            nc.gpsimd.memset(zeros_before(PW2), 0.0).then_inc(pads_ready, 1)
            pool.wait_ge(pads_ready, 2)
            done = 0
            for w, taken in ((3, 4), (2, 8)):
                if w == 2:
                    split_lo(UB["pool"] + 3, 1)
                pool.wait_ge(evacuated, GB["pool"] + taken)
                for step in range(w + 1):
                    if done:
                        pool.wait_ge(far_step, done)
                    window_step(nc.gpsimd, w, step).then_inc(far_step, 1)
                    done += 1
            for name in ("post0", "kv_pre1", "mix1"):
                sum_squares(name)
            split_lo(UB["dq"] + 3, 1)
            with pool.Fori(0, QUARTERS) as q:
                split_lo(q * 2 + (UB["attn"] + 3), 1)
                split_lo(q * 2 + (UB["attn"] + 2), 0)
            for name in ("post1", "final"):
                sum_squares(name)

        @block.scalar
        def _(a):
            nc.scalar.preload_act_table_set(LOG_EXP)
            a.dma_start(ident[:, :], A["ident"]).then_inc(ident_loaded, 16)
            for name, n in VECTORS:
                v = A[name]
                v = v.rearrange("a (k p) -> (a k) p", p=P) if len(v.shape) == 2 else (
                    v.rearrange("a b (k p) -> (a b k) p", p=P) if len(v.shape) == 3 else
                    v.rearrange("(k p) -> k p", p=P))
                a.dma_start(rows[COL[name]:COL[name] + n, 0:P], v).then_inc(
                    rows_loaded if COL[name] else first_row_loaded, 16)
            taps = A["ffn_conv_w"].rearrange("a b (k p) -> (a b k) p", p=P)
            a.dma_start(rows[0:88, P:2 * P], taps[0:88]).then_inc(rows_loaded, 16)
            a.dma_start(rows[0:44, 2 * P:3 * P], taps[88:132]).then_inc(rows_loaded, 16)

            def split_hi(n, s, signal=None, value=None):
                a.wait_ge(raw_ready[s], (n - s) * 8 + 16)
                if signal is not None:
                    a.wait_ge(signal, value)
                nc.scalar.activation(whi[:, s * UNIT:(s + 1) * UNIT], raw[:, s * UNIT:(s + 1) * UNIT],
                                     ACT.Copy).then_inc(whi_ready[s], 2)

            def last_square_read(name):
                if NORM[name] and ADDS[BEFORE[name]] < DT - 1:
                    a.wait_ge(sums_ready, NORM[name])

            def square(name, k, t, at=None):
                after = ADDED[name] + (0 if k < 2 else max(1, k - 2))
                if after > 0:
                    a.wait_ge(acc_added, after)
                if k == 1:
                    last_square_read(name)
                nc.scalar.activation(tile(sq, k % 2), tile(t, k if at is None else at), ACT.Square).then_inc(square_ready, 1)

            def xg_hi(signal, value, t, gain, k, w=None):
                a.wait_ge(signal, value)
                nc.scalar.activation(tile(xghi, k), tile(t, k), ACT.Copy,
                                     scale=1.0 if gain is None else col(gain, k if w is None else w)
                                     ).then_inc(xghi_ready, 1)

            split_hi(0, 0)
            a.wait_ge(first_gain, 1)
            for k in range(DT):
                xg_hi(evacuated, k + 1, xT, "pre_mix_g", k)
                square("pre_mix", k, xT)
            split_hi(1, 1)

            def root(name):
                j = NORM[name]
                a.wait_ge(sums_ready, j + 1)
                nc.scalar.activation(R[:, :], stat[:, :], ACT.Ln, bias=eps[:, :], scale=1.0 / D).then_inc(rstd_log, 1)
                a.wait_ge(rstd_log, j + 1)
                nc.scalar.activation(R[:, :], R[:, :], ACT.Exp, scale=-0.5).then_inc(rstd_ready, 1)

            smalls = [0]

            def root_of(t, sums, n, signal, value):
                smalls[0] += 1
                a.wait_ge(signal, value)
                nc.scalar.activation(t, sums, ACT.Ln, bias=eps[:, :], scale=1.0 / n).then_inc(small_log, 1)
                a.wait_ge(small_log, smalls[0])
                nc.scalar.activation(t, t, ACT.Exp, scale=-0.5).then_inc(small_root, 1)

            a.wait_ge(ones_ready, 2)
            nc.scalar.preload_act_table_set(LOG_EXP)
            root("pre_mix")
            root_of(rcol[:, :], misc[:, 0:TC], D, rcol_sums, 1)
            g0 = GB["w_in"]
            for n in range(14):
                read = 2 * (n + 1) if n < 4 else 8 + 6 * (n - 4) + 2 if n < 12 else 56 + 4 * (n - 11)
                if n == 12:
                    bends = lb_.rearrange("p (c t) -> p c t", t=P)[:, :, P - 1]
                    a.wait_ge(cross_arg, 1)
                    nc.scalar.activation(LG, LG, ACT.Exp).then_inc(cross_exp, 1)
                    nc.scalar.activation(ends[:, :], bends, ACT.Exp).then_inc(cross_exp, 1)
                    a.wait_ge(cross_exp, 2)
                    nc.scalar.activation(lb_, lb_, ACT.Exp).then_inc(cross_exp, 1)
                split_hi(n + 2, n % 2, groups_done, g0 + read)
                if n == 1:
                    a.wait_ge(evacuated, g0 + 4)
                    nc.scalar.activation(lb_, fk, ACT.Abs).then_inc(decay_act, 1)
                    a.wait_ge(decay_act, 1)
                    nc.scalar.activation(lb_, lb_, ACT.Exp, scale=-1.0).then_inc(decay_act, 1)
                    a.wait_ge(decay_act, 2)
                    nc.scalar.activation(lb_, lb_, ACT.Ln, bias=1.0).then_inc(decay_act, 1)
                if n == 2:
                    a.wait_ge(decay_vec, 2)
                    nc.scalar.activation(fk, fk, ACT.Exp).then_inc(decay_act, 1)
                if n == 3:
                    a.wait_ge(evacuated, g0 + 8)
                    nc.scalar.activation(Q[:, :], Q[:, :], ACT.Silu).then_inc(q_silu, 1)
                if 4 <= n <= 10:
                    a.wait_ge(level_arg, 2 * (n - 3))
                    nc.scalar.activation(EX, EX, ACT.Exp).then_inc(level_exp, 1)
                if n == 11:
                    a.wait_ge(evacuated, g0 + 52)
                    nc.scalar.activation(G[:, :], G[:, :], ACT.Silu).then_inc(q_silu, 1)
            for k in range(4):
                a.wait_ge(mixb_ready, k + 1)
                nc.scalar.activation(tile(xghi, 4 + k), tile(GBt, k), ACT.Copy).then_inc(xghi_ready, 1)
            nc.scalar.preload_act_table_set(LOG_EXP)
            for h in range(HH + 1):
                if h < HH:
                    root_of(tile(GC, h), banks[4 + h][:, :], P, head_sums, h + 1)
                if h:
                    a.wait_ge(mixa_ready, h)
                    nc.scalar.activation(tile(xghi, h - 1), tile(CH, h - 1), ACT.Copy).then_inc(xghi_ready, 1)
            def project(name, ksplit, norm, gain=None, goff=0, unroll=False, t=xT):
                nk = len(ksplit)
                nc.scalar.preload_act_table_set(LOG_EXP)
                for i in steps(a, 2, unroll):
                    for b in range(2):
                        def ahead(j):
                            n = i * (2 * nk) + (UB[name] + b * nk + j + 2)
                            if unroll and n >= UNITS:
                                return
                            s = (b * nk + j) % 2
                            if j < nk - 1:
                                split_hi(n, s, parts_used, i * (2 * nk - 2) + (MB[name] + b * (nk - 1) + j + 1))
                            else:
                                split_hi(n, s, groups_done, i * 4 + (GB[name] + 2 * b + 2))
                        for j in range(nk - 1):
                            ahead(j)
                        for f in range(2):
                            gr = 2 * b + f
                            k = i * 4 + gr
                            if norm:
                                base = ADDED[norm]
                                if gr == 1:
                                    last_square_read(norm)
                                a.wait_ge(acc_added,
                                          (i * 2 + base, i * 3 + base, i * 3 + (base + 1), i * 4 + (base + 1))[gr])
                            if gain:
                                xg_hi(evacuated, k + (GB[name] + 1), xT, gain, k, k + goff)
                            else:
                                a.wait_ge(evacuated, k + (GB[name] + 1))
                            if norm:
                                nc.scalar.activation(tile(sq, f), tile(t, k), ACT.Square).then_inc(square_ready, 1)
                        ahead(nk - 1)

            project("w_out", [8], "post_mix", t=Y0)
            root("post_mix")
            for k in range(DT):
                xg_hi(resid_ready, k + 1, xT, "pre_ffn_g", k)
                square("pre_ffn", k, xT)

            def up(m, norm=None, conv=False):
                name = f"up{m}"
                gb, hb = GB[name], FT * m

                def step(i, first):
                    if first:
                        split_hi(UB[name] + 2, 0, groups_done, gb + 2)
                        if norm:
                            root(norm)
                        nc.scalar.preload_act_table(ACT.Silu)
                    for f in range(2):
                        if conv:
                            a.wait_ge(evacuated, i * 4 + (gb + f + 1))
                            nc.scalar.activation(tile(Tt, f), tile(Ut, f), ACT.Copy,
                                                 scale=tap_col(i, 2, 0, f)).then_inc(tap_ready, 1)
                    for f in range(2):
                        if conv:
                            a.wait_ge(conv_ready, i * 4 + (f + 1))
                        else:
                            a.wait_ge(evacuated, i * 4 + (gb + f + 1))
                        nc.scalar.activation(tile(Tt, f), tile(Tt, f), ACT.Silu).then_inc(silu_ready, 1)
                    if not first:
                        split_hi(i * 2 + (UB[name] + 2), 0, groups_done, i * 4 + (gb + 2))
                    for f in range(2):
                        if conv:
                            a.wait_ge(evacuated, i * 4 + (gb + f + 3))
                            nc.scalar.activation(tile(At, f), tile(Ut, f), ACT.Copy,
                                                 scale=tap_col(i, 2, 1, f)).then_inc(tap_ready, 1)
                    if conv:
                        split_hi(i * 2 + (UB[name] + 3), 1, groups_done, i * 4 + (gb + 4))
                    for f in range(2):
                        a.wait_ge(gated_ready, i * 2 + (hb + f + 1))
                        nc.scalar.activation(tile(ahi, i * 2 + f), tile(At, f), ACT.Copy).then_inc(ahi_ready, 1)
                    if not conv:
                        split_hi(i * 2 + (UB[name] + 3), 1, groups_done, i * 4 + (gb + 4))

                step(0, True)
                with a.Fori(1, FT // 2) as i:
                    step(i, False)

            up(0, "pre_ffn", conv=True)
            project("down0", DOWN, "post_ffn", t=Y1)
            root("post_ffn")
            for k in range(DT):
                xg_hi(resid_ready, DT + k + 1, xT, "ffn_pre_norm_2", k)
                square("pre0", k, xT)
            up(1, "pre0")
            project("down1", DOWN, "mix0", "mix_norm_2")
            root("mix0")
            for u in range(2):
                split_hi(UB["pool"] + u + 2, u, groups_done, GB["pool"] + 4 * (u + 1))

            def mixed_hi(pos):
                k = MIXED_ORDER[pos]
                xg_hi(mixed_ready, pos + 1, xT, "ffn_post_norm_2", k)

            for pos in range(4):
                mixed_hi(pos)
            square("post0", 0, xT, MIXED_ORDER[0])
            square("post0", 1, xT, MIXED_ORDER[1])
            mixed_hi(4)
            mixed_hi(5)
            for pos in range(2, 6):
                square("post0", pos, xT, MIXED_ORDER[pos])
            mixed_hi(6)
            square("post0", 6, xT, MIXED_ORDER[6])
            mixed_hi(7)
            square("post0", 7, xT, MIXED_ORDER[7])
            up(2, "post0")
            project("down2", DOWN, "kv_pre1", "kv_in_norm_2")
            root("kv_pre1")
            split_hi(UB["kv"] + 2, 0, groups_done, GB["kv"] + 2)
            a.wait_ge(groups_done, GB["kv"] + 4)
            for k in range(DT):
                xg_hi(evacuated, GB["down2"] + k + 1, xT, "ffn_pre_norm_2", k, 8 + k)
            split_hi(UB["kv"] + 3, 1, groups_done, GB["kv"] + 4)
            root_of(kvt[:, T:2 * T], banks[6][:, :], P, key_sums, 1)
            up(3)
            project("down3", DOWN, "mix1", "mix_norm_2", 8)
            root("mix1")
            a.wait_ge(latent_ready, 1)
            nc.scalar.activation(ckhi[:, :], Ut[:, 0:T], ACT.Copy).then_inc(latent_hi, 1)
            for u in range(2):
                split_hi(UB["dq"] + u + 2, u, groups_done, GB["dq"] + (1, 4)[u])
            for j in range(1, 1 + QR):
                if j == 1:
                    root_of(PT[:, 0:T], misc[:, :], QR * P, query_sums, 1)
                a.wait_ge(latent_ready, j + 1)
                nc.scalar.activation(tile(cqhi, j - 1), tile(At, j - 1), ACT.Copy).then_inc(latent_hi, 1)
            with a.Fori(0, QUARTERS) as q:
                split_hi(q * 2 + (UB["attn"] + 3), 1, groups_done, q * 16 + (GB["attn"] + 10))
                split_hi(q * 2 + (UB["attn"] + 2), 0, groups_done, q * 16 + (GB["attn"] + 16))

                def exps(h):
                    for i in range(TC):
                        e = 4 * h + i
                        a.wait_ge(negmax_ready, q * 16 + (e + 1))
                        c = 4 * (h % 2) + i
                        off = i * (i + 1) // 2 * P
                        nc.scalar.activation(probs(h)[:, off:off + (i + 1) * P], ring[i][:, 0:(i + 1) * P],
                                             ACT.Exp, bias=negmax[:, c:c + 1], scale=float((NOPE + ROPE) ** -0.5),
                                             accum_out=rowsum[:, c:c + 1]).then_inc(exp_ready, 1)

                exps(0)
                for h in range(4):
                    if h < 3:
                        exps(h + 1)
                    if h < 3:
                        a.wait_ge(turned_ready, q * 12 + (3 * h + 2))
                        nc.scalar.activation(PT[:, 4 * P:7 * P], banks[5][:, 0:3 * P], ACT.Copy
                                             ).then_inc(turned_act, 1)
                    else:
                        a.wait_ge(turned_ready, q * 12 + (3 * h + 1))
                        nc.scalar.activation(PT[:, 0:4 * P], banks[4][:, 0:4 * P], ACT.Copy).then_inc(turned_act, 1)
                    a.wait_ge(turned_ready, q * 12 + (3 * h + 3))
                    nc.scalar.activation(PT[:, 7 * P:10 * P], banks[6][:, 0:3 * P], ACT.Copy).then_inc(turned_act, 1)
                    a.wait_ge(out_ready, q * 4 + (h + 1))
                    nc.scalar.activation(tile(oThi, q * 4 + h), banks[7][:, :], ACT.Copy).then_inc(outhi_ready, 1)
            project("w_o", [8, 8], "post1", "ffn_post_norm_2", 8)
            up(4, "post1")
            project("down4", DOWN, "final", unroll=True)
            root("final")


        @block.tensor
        def _(pe):
            def unit_ready(n, s):
                pe.wait_ge(wlo_ready[s], split_count(n, s))

            def three(bank, whi_, wlo_, xhi, xlo, first, last):
                nc.tensor.matmul(bank, wlo_, xhi, start=first, stop=False)
                nc.tensor.matmul(bank, whi_, xlo, start=False, stop=False)
                return nc.tensor.matmul(bank, whi_, xhi, start=False, stop=last)

            def bank_free(g):
                pe.wait_ge(evacuated, g - RING + 1)

            def sum_norm(name):
                j = NORM[name]
                pe.wait_ge(acc_added, ADDED[name] + ADDS[name])
                if j:
                    pe.wait_ge(rstd_log, j)
                parts = [acc[:, :]] + ([sq[:, T:2 * T]] if ADDS[name] < DT - 1 else [])
                for n, part in enumerate(parts):
                    if n:
                        pe.wait_ge(square_ready, DT * (j + 1))
                    m = nc.tensor.matmul(stat[:, :], ones[:, :], part, start=(n == 0), stop=(n == len(parts) - 1))
                m.then_inc(sums_ready, 1)
                if j == 0:
                    for c in range(TC):
                        nc.tensor.matmul(misc[:, c:c + 1], acc[:, c * P:(c + 1) * P], ones[:, 0:1],
                                         start=True, stop=False)
                        m = nc.tensor.matmul(misc[:, c:c + 1], sq[:, T + c * P:T + (c + 1) * P], ones[:, 0:1],
                                             start=False, stop=True)
                    m.then_inc(rcol_sums, 1)

            pe.wait_ge(ident_loaded, 16)
            pe.wait_ge(first_row_loaded, 16)
            nc.tensor.transpose(banks[7][:, 0:DT], rows[0:DT, 0:P], ident[0:DT, 0:DT]).then_inc(first_turned, 1)
            for c in range(TC):
                pe.wait_ge(x_loaded[c], 16)
                for k in range(DT):
                    if c == 0 and k == 7:
                        pe.wait_ge(first_gain, 1)
                    m = nc.tensor.transpose(banks[k][:, c * P:(c + 1) * P],
                                            fkb[:, c * D + k * P:c * D + (k + 1) * P], ident[:, :])
                    if c == TC - 1:
                        m.then_inc(groups_done, 1)

            def turn_vectors():
                pe.wait_ge(rows_loaded, 16 * (len(VECTORS) + 1))
                nc.tensor.transpose(banks[6][:, 0:NVEC], rows[0:NVEC, 0:P], ident[0:NVEC, 0:NVEC])
                nc.tensor.transpose(banks[6][:, P:P + 88], rows[0:88, P:2 * P], ident[0:88, 0:88])
                nc.tensor.transpose(banks[6][:, P + 88:P + 132], rows[0:44, 2 * P:3 * P], ident[0:44, 0:44]
                                    ).then_inc(cols_turned, 1)

            def up_unit(n, s, g, xg, order=range(DT)):
                unit_ready(n, s)
                w, wl = slot(whi, s), slot(wlo, s)
                for f in range(2):
                    bank_free(g + f)
                    bank = ring[(2 * s + f) % RING][:, :]
                    for pos, k in enumerate(order):
                        if f == 0 and s == 0:
                            pe.wait_ge(xg_ready, XG[xg] + pos + 1)
                        m = three(bank, w[:, k, f * P:(f + 1) * P], wl[:, k, f * P:(f + 1) * P],
                                  tile(xghi, k), tile(xglo, k), pos == 0, pos == DT - 1)
                    m.then_inc(groups_done, 1)

            def first_units(n, g, xg, between, order=tuple(range(DT))):
                for tiles, slots in ([((k,), (0, 1)) for k in range(4)]
                                     + [(range(4, DT), (0,)), (range(4, DT), (1,))]):
                    for pos in tiles:
                        k = order[pos]
                        pe.wait_ge(xg_ready, XG[xg] + pos + 1)
                        for s in slots:
                            if pos == 0:
                                unit_ready(n + s, s)
                            for f in range(2):
                                if pos == 0:
                                    bank_free(g + 2 * s + f)
                                m = three(ring[2 * s + f][:, :], slot(whi, s)[:, k, f * P:(f + 1) * P],
                                          slot(wlo, s)[:, k, f * P:(f + 1) * P], tile(xghi, k), tile(xglo, k),
                                          pos == 0, pos == DT - 1)
                                if pos == DT - 1:
                                    m.then_inc(groups_done, 1)
                    if slots == (0,) and between:
                        between()

            def level(l, g):
                if l == 0:
                    pe.wait_ge(q_silu, 1)
                    pe.wait_ge(decay_act, 4)
                else:
                    pe.wait_ge(level_ready, 2 * l)
                for h in range(HH):
                    bank_free(g + h)
                    for c in range(TC):
                        at_ = slice((TC * h + c) * P, (TC * h + c + 1) * P)
                        left, right = (fk[:, at_], Q[:, at_]) if l == 0 else (LG[:, at_], LG[:, at_])
                        m = nc.tensor.matmul(ring[(g + h) % RING][:, c * P:(c + 1) * P], left, right,
                                             start=True, stop=True)
                    m.then_inc(groups_done, 1)

            g = GB["w_in"]
            pe.wait_ge(ones_ready, 2)
            up_unit(0, 0, g, "w_in")
            sum_norm("pre_mix")
            turn_vectors()
            up_unit(1, 1, g + 2, "w_in")
            g += 4
            for n in range(2, 12):
                up_unit(n, n % 2, g, "w_in")
                g += 2
                if n >= 4:
                    level(n - 4, g)
                    g += 4
            for s in range(2):
                unit_ready(12 + s, s)
                for c in range(TC):
                    bank_free(g)
                    for k in range(DT):
                        xh = xghi[:, k * T + c * P:k * T + (c + 1) * P]
                        xl = xglo[:, k * T + c * P:k * T + (c + 1) * P]
                        w, wl = slot(whi, s)[:, k, :], slot(wlo, s)[:, k, :]
                        m = three(ring[g % RING][:, 0:UC], xh, xl, w, wl, k == 0, k == DT - 1)
                    m.then_inc(groups_done, 1)
                    g += 1
            pe.wait_ge(cross_ready, 5)
            for h in range(HH):
                def c_(t, c):
                    return t[:, (TC * h + c) * P:(TC * h + c + 1) * P]
                for pairs in (((GC, 0, 1), (fkb, 0, 2), (fkb, 2, 3)), ((GC, 1, 2), (fkb, 1, 3), (GC, 2, 3))):
                    bank_free(g)
                    for n, (t, i, j) in enumerate(pairs):
                        m = nc.tensor.matmul(ring[g % RING][:, n * P:(n + 1) * P], c_(t, i), c_(lb_, j),
                                             start=True, stop=True)
                    m.then_inc(groups_done, 1)
                    g += 1
            for h in range(HH):
                bank_free(g)
                pe.wait_ge(evacuated, GB["cross"] + 2 * h + 2)
                off = 0
                for i in range(TC):
                    v = V[:, i * 512 + h * P:i * 512 + (h + 1) * P]
                    m = nc.tensor.matmul(ring[h][:, i * P:(i + 1) * P], v,
                                         SD[:, (TC * h + i) * P:(TC * h + i + 1) * P],
                                         start=(i == 0), stop=(i == TC - 1))
                    if i < TC - 1:
                        n = TC - 1 - i
                        nc.tensor.matmul(ring[h][:, (i + 1) * P:T], v,
                                         SC[:, (6 * h + off) * P:(6 * h + off + n) * P], start=False, stop=False)
                        off += n
                m.then_inc(groups_done, 1)
                g += 1
            order = [4, 5, 6, 7, 0, 1, 2, 3]
            for part in range(2):
                for b in range(2):
                    unit_ready(UB["w_out"] + b, b)
                    w, wl = slot(whi, b), slot(wlo, b)
                    for f in range(2):
                        if part == 0:
                            bank_free(g + 2 * b + f)
                        for pos in range(4 * part, 4 * part + 4):
                            k = order[pos]
                            if b == 0 and f == 0:
                                pe.wait_ge(xg_ready, XG["w_out"] + pos + 1)
                            m = three(ring[2 * b + f][:, :], w[:, k, f * P:(f + 1) * P], wl[:, k, f * P:(f + 1) * P],
                                      tile(xghi, k), tile(xglo, k), pos == 0, pos == DT - 1)
                        if part == 1:
                            m.then_inc(groups_done, 1)
                    if part == 0 and b == 0:
                        for h in range(HH):
                            pe.wait_ge(osq_ready, h + 1)
                            nc.tensor.matmul(banks[4 + h][:, :], ones[:, :], tile(GC, h), start=True, stop=True
                                             ).then_inc(head_sums, 1)

            def project(name, ksplit, hi, lo, ready, base, iterations=None):
                nk, total = len(ksplit), sum(ksplit)
                for i in (steps(pe, 2) if iterations is None else iterations):
                    for b in range(2):
                        pos0 = 0
                        for j, kt in enumerate(ksplit):
                            s = (b * nk + j) % 2
                            unit_ready(i * (2 * nk) + (UB[name] + b * nk + j), s)
                            w, wl = slot(whi, s, kt), slot(wlo, s, kt)
                            for f in range(2):
                                if j == 0:
                                    bank_free(i * 4 + (GB[name] + 2 * b + f))
                                for pos in range(pos0, pos0 + kt):
                                    k = pos
                                    if b == 0 and f == 0:
                                        pe.wait_ge(ready, base + pos + 1)
                                    m = three(ring[2 * b + f][:, :], w[:, k - pos0, f * P:(f + 1) * P],
                                              wl[:, k - pos0, f * P:(f + 1) * P], tile(hi, k), tile(lo, k),
                                              pos == 0, pos == total - 1)
                                if j == nk - 1:
                                    m.then_inc(groups_done, 1)
                            if j < nk - 1:
                                m.then_inc(parts_used, 1)
                            pos0 += kt

            project("w_out", [8], xghi, xglo, xg_ready, XG["w_out"], (1,))
            sum_norm("post_mix")

            def ffn(m, norm=None, between=None, one_by_one=False, order=tuple(range(DT))):
                name = f"up{m}"
                between = (lambda: sum_norm(norm)) if norm else between
                if one_by_one:
                    first_units(UB[name], GB[name], name, between, order)
                else:
                    up_unit(UB[name], 0, GB[name], name)
                    between()
                    up_unit(UB[name] + 1, 1, GB[name] + 2, name)
                with pe.Fori(1, FT // 2) as i:
                    for s in range(2):
                        up_unit(i * 2 + (UB[name] + s), s, i * 4 + (GB[name] + 2 * s), name)
                project(f"down{m}", DOWN, ahi, alo, act_ready, FT * m)

            ffn(0, "pre_ffn", one_by_one=True)
            sum_norm("post_ffn")
            ffn(1, "pre0", one_by_one=True)
            for n, w in enumerate(POOL_ORDER):
                u = n // 2
                unit_ready(UB["pool"] + u, u)
                wh, wl = slot(whi, u, 4), slot(wlo, u, 4)
                for f in range(2):
                    g = GB["pool"] + 2 * n + f
                    bank_free(g)
                    for kt in range(2):
                        k = 2 * w + kt
                        pe.wait_ge(xg_ready, XG["pool"] + k + 1)
                        c = slice(f * P, (f + 1) * P)
                        m = three(ring[g % RING][:, :], wh[:, 2 * (n % 2) + kt, c], wl[:, 2 * (n % 2) + kt, c],
                                  tile(xghi, k), tile(xglo, k), kt == 0, kt == 1)
                    m.then_inc(groups_done, 1)
                    if g == GB["pool"] + 1:
                        sum_norm("mix0")
            ffn(2, "post0", one_by_one=True, order=MIXED_ORDER)

            def narrow(name, norm, counts):
                for u in range(2):
                    unit_ready(UB[name] + u, u)
                    bank_free(GB[name] + u)
                    w, wl = slot(whi, u, DT, P), slot(wlo, u, DT, P)
                    for k in range(DT):
                        pe.wait_ge(xg_ready, XG[name] + k + 1)
                        m = three(ring[u][:, :], w[:, k, :], wl[:, k, :], tile(xghi, k), tile(xglo, k),
                                  k == 0, k == DT - 1)
                    m.then_inc(groups_done, counts[u])
                    if u == 0:
                        sum_norm(norm)

            narrow("kv", "kv_pre1", (2, 2))
            pe.wait_ge(evacuated, GB["kv"] + 4)

            def key_extras():
                pe.wait_ge(small_step, 1)
                pe.wait_ge(consts_loaded, 16 * 3)
                nc.tensor.matmul(banks[6][:, :], ones[:, :], kvt[:, 0:T], start=True, stop=True).then_inc(key_sums, 1)
                nc.tensor.matmul(banks[7][:, :], perm[:, :], Ut[:, T:2 * T], start=True, stop=True
                                 ).then_inc(key_turned, 1)

            ffn(3, between=key_extras)
            narrow("dq", "mix1", (1, 3))
            pe.wait_ge(small_step, 3)
            nc.tensor.matmul(misc[:, :], ones[:, :], PT[:, 0:T], start=True, stop=False)
            nc.tensor.matmul(misc[:, :], ones[:, :], PT[:, T:2 * T], start=False, stop=True
                             ).then_inc(query_sums, 1)
            w0 = whi[:, 0:UNIT], wlo[:, 0:UNIT]
            w1 = whi[:, UNIT:2 * UNIT], wlo[:, UNIT:2 * UNIT]
            with pe.Fori(0, QUARTERS) as q:
                gb = GB["attn"]
                unit_ready(q * 2 + UB["attn"], 0)
                pe.wait_ge(latent_split, 1)

                def group(n):
                    bank_free(q * 16 + (gb + n))
                    return ring[n % RING][:, :]

                def queries(x, n):
                    bank = group(n)
                    for kt in range(QR):
                        o = 1024 + kt * 512 + x * P
                        m = three(bank, w0[0][:, o:o + P], w0[1][:, o:o + P],
                                  tile(cqhi, kt), tile(cqlo, kt), kt == 0, kt == QR - 1)
                    m.then_inc(groups_done, 1)

                for x in range(4):
                    c = slice(x * P, (x + 1) * P)
                    three(group(x), w0[0][:, c], w0[1][:, c], ckhi[:, :], cklo[:, :], True, True
                          ).then_inc(groups_done, 1)
                for x in range(4):
                    c = slice(x * P, (x + 1) * P)
                    three(group(4 + x), ckhi[:, c], cklo[:, c], w0[0][:, 512:1024], w0[1][:, 512:1024],
                          True, True).then_inc(groups_done, 1)
                unit_ready(q * 2 + (UB["attn"] + 1), 1)
                pe.wait_ge(latent_split, 1 + QR)
                for j in range(2):
                    bank = group(8 + j)
                    for kt in range(QR):
                        o = kt * 256 + j * P
                        m = three(bank, w1[0][:, o:o + P], w1[1][:, o:o + P],
                                  tile(cqhi, kt), tile(cqlo, kt), kt == 0, kt == QR - 1)
                    m.then_inc(groups_done, 1)
                queries(0, 10)
                queries(1, 11)
                for j in range(2):
                    bank = group(12 + j)
                    pe.wait_ge(evacuated, q * 16 + (gb + 9 + j))
                    nc.tensor.matmul(bank, perm[:, :], tile(QRr, j), start=True, stop=True
                                     ).then_inc(groups_done, 1)
                queries(2, 14)
                queries(3, 15)

                def scores(h):
                    if h % 2 == 0:
                        pe.wait_ge(qrope_ready, q * 2 + (h // 2 + 1))
                    for i in range(TC):
                        if h == 0:
                            pe.wait_ge(evacuated, q * 16 + (gb + 13 + i))
                        else:
                            pe.wait_ge(exp_ready, q * 16 + (4 * (h - 1) + i + 1))
                        n = (i + 1) * P
                        nc.tensor.matmul(ring[i][:, 0:n], QN[:, h * T + i * P:h * T + (i + 1) * P],
                                         KN[:, h * T:h * T + n], start=True, stop=False)
                        r = (h // 2) * T + i * P
                        nc.tensor.matmul(ring[i][:, 0:n], QRt[:, r:r + P], Tt[:, (h % 2) * T:(h % 2) * T + n],
                                         start=False, stop=False)
                        nc.tensor.matmul(ring[i][:, i * P:n], identb[:, :], causal[:, :],
                                         start=False, stop=True).then_inc(scores_ready, 1)

                scores(0)
                for h in range(4):
                    if h < 3:
                        scores(h + 1)
                    for i in range(TC):
                        pe.wait_ge(probs_ready, q * 16 + (4 * h + i + 1))
                        off = i * (i + 1) // 2
                        for j in range(i + 1):
                            bank, at_ = [(banks[4], i), (banks[5], i - 1), (banks[6], i - 2), (banks[6], 2)][j]
                            m = nc.tensor.transpose(bank[:, at_ * P:(at_ + 1) * P],
                                                    probs(h)[:, (off + j) * P:(off + j + 1) * P], ident[:, :])
                            if i == TC - 1 and j != 2:
                                m.then_inc(turned_ready, 1)
                    pe.wait_ge(outlo_ready, q * 4 + (h + 1))
                    seg = 0
                    for j in range(TC):
                        if j == (1 if h == 3 else 0):
                            pe.wait_ge(turned_vec, q * 4 + (h + 1))
                        elif j < 3:
                            pe.wait_ge(turned_act, q * 8 + (2 * h + (2 if j == 2 else 1)))
                        n = (TC - j) * P
                        m = nc.tensor.matmul(banks[7][:, j * P:T], VV[:, j * 512 + h * P:j * 512 + (h + 1) * P],
                                             PT[:, seg:seg + n], start=(j == 0), stop=(j == TC - 1))
                        seg += n
                    m.then_inc(out_ready, 1)
            project("w_o", [8, 8], oThi, oTlo, outlo_ready, 1)
            ffn(4, "post1")
            sum_norm("final")
            g = GB["x_out"]
            for c in range(TC):
                for half in range(2):
                    bank_free(g)
                    for kk in range(4):
                        k = 4 * half + kk
                        if c == 0:
                            pe.wait_ge(normed_out, k + 1)
                        m = nc.tensor.transpose(ring[g % RING][:, kk * P:(kk + 1) * P],
                                                Z[:, k * T + c * P:k * T + (c + 1) * P], ident[:, :])
                    m.then_inc(groups_done, 1)
                    g += 1

        @block.vector
        def _(v):
            def split_lo(n, s):
                v.wait_ge(whi_ready[s], split_count(n, s))
                c = slice(s * UNIT, (s + 1) * UNIT)
                nc.vector.tensor_tensor(wlo[:, c], raw[:, c], whi[:, c].bitcast(F32), ALU.subtract
                                        ).then_inc(wlo_ready[s], 2)

            def xg_lo(xg, pos, k, t, gain, w=None):
                v.wait_ge(xghi_ready, XG[xg] + pos + 1)
                hi = tile(xghi, k).bitcast(F32)
                if gain is None:
                    ins = nc.vector.tensor_tensor(tile(xglo, k), t, hi, ALU.subtract)
                else:
                    ins = nc.vector.scalar_tensor_tensor(tile(xglo, k), t, col(gain, k if w is None else w), hi,
                                                         ALU.mult, ALU.subtract)
                ins.then_inc(xg_ready, 1)

            def rstd(name):
                v.wait_ge(rstd_ready, NORM[name] + 1)

            v.wait_ge(first_turned, 1)
            nc.vector.tensor_copy(cols[:, 0:DT], banks[7][:, 0:DT]).then_inc(first_gain, 1)
            for k in range(DT):
                v.wait_ge(groups_done, k + 1)
                nc.vector.tensor_copy(tile(xT, k), banks[k][:, :]).then_inc(evacuated, 1)
            split_lo(0, 0)
            v.wait_ge(first_gain, 1)
            for k in range(DT):
                xg_lo("w_in", k, k, tile(xT, k), "pre_mix_g")
            split_lo(1, 1)
            v.wait_ge(ident_loaded, 16)
            v.wait_ge(consts_loaded, 16 * 3)
            nc.vector.tensor_copy(identb[:, :], ident[:, :])
            nc.vector.tensor_copy(causal[:, :], wide_causal[:, :])
            nc.vector.tensor_copy(masks[:, :], wide_masks[:, :]).then_inc(masks_ready, 1)
            v.wait_ge(cols_turned, 1)
            nc.vector.tensor_copy(cols[:, DT:NVEC], banks[6][:, DT:NVEC]).then_inc(cols_ready, 1)
            nc.vector.tensor_copy(cw[:, 0:88], banks[6][:, P:P + 88]).then_inc(cols_ready, 1)
            nc.vector.tensor_copy(cw[:, 88:132], banks[6][:, P + 88:P + 132]).then_inc(cols_ready, 1)
            v.wait_ge(cols_ready, 3)
            rstd("pre_mix")

            g = GB["w_in"]
            dests = [fk, Q[:, :], GC[:, :], CH[:, :], GBt[:, :], G[:, :]]
            mask = masks[:, :].rearrange("p (l t) -> p l t", l=8)

            def take(l, g):
                v.wait_ge(evacuated, g)
                for h in range(HH):
                    v.wait_ge(groups_done, g + 1)
                    nc.vector.copy_predicated(
                        SD[:, h * TC * P:(h + 1) * TC * P].rearrange("p (c t) -> p c t", c=TC),
                        mask[:, l:l + 1, :].to_broadcast([P, TC, P]),
                        ring[g % RING][:, :].rearrange("p (c t) -> p c t", c=TC)).then_inc(evacuated, 1)
                    g += 1
                return g

            def level_operand(l):
                hs = LEVELS[l - 1]
                e, k_, q_, o = (t.rearrange("p (n two h) -> p n two h", two=2, h=hs) for t in (EX, fk, Q[:, :], LG))
                v.wait_ge(level_exp, l)
                nc.vector.tensor_tensor(o[:, :, 0, :], e[:, :, 0, :], k_[:, :, 0, :], ALU.mult).then_inc(level_ready, 1)
                nc.vector.tensor_tensor(o[:, :, 1, :], e[:, :, 1, :], q_[:, :, 1, :], ALU.mult).then_inc(level_ready, 1)

            mixb_steps = [0]

            def after_mixb():
                v.wait_ge(mixb_part, mixb_steps[0])

            def mixb_step(ins):
                ins.then_inc(mixb_part, 1)
                mixb_steps[0] += 1

            def conv_tile(k):
                m, c, b = tile(GC, k), tile(CH, k), tile(GBt, k)
                mixb_step(nc.vector.tensor_tensor(m, m, c, ALU.mult))
                after_mixb()
                mixb_step(nc.vector.tensor_scalar(c, m, col("conv_w", 8 + k), None, ALU.mult))
                after_mixb()
                mixb_step(nc.vector.scalar_tensor_tensor(c[:, 1:T], m[:, 0:T - 1], col("conv_w", 4 + k), c[:, 1:T],
                                                         ALU.mult, ALU.add))
                after_mixb()
                mixb_step(nc.vector.scalar_tensor_tensor(c[:, 2:T], m[:, 0:T - 2], col("conv_w", k), c[:, 2:T],
                                                         ALU.mult, ALU.add))
                after_mixb()
                nc.vector.tensor_tensor(b, b, c, ALU.mult).then_inc(mixb_ready, 1)

            def cross_ends(scale_chunks):
                if not scale_chunks:
                    v.wait_ge(cross_exp, 1)
                    v.wait_ge(mixb_ready, 4)
                    nc.vector.tensor_tensor(GC[:, :], LG, fk, ALU.mult).then_inc(cross_ready, 1)
                    return
                v.wait_ge(cross_exp, 3)
                nc.vector.tensor_tensor(lb_, lb_, Q[:, :], ALU.mult).then_inc(cross_ready, 1)
                ge = GC[:, :].rearrange("p (h c t) -> p h c t", h=HH, c=TC)
                fe = fk.rearrange("p (h c t) -> p h c t", h=HH, c=TC)
                en = ends[:, :].rearrange("p (h c) -> p h c", h=HH)
                for dst, src, c, e, after in ((0, ge, 0, 1, 1), (1, ge, 1, 2, 1), (2, fe, 0, 2, 3)):
                    v.wait_ge(cross_ready, after)
                    nc.vector.tensor_tensor(fe[:, :, dst, :], src[:, :, c, :],
                                            en[:, :, e:e + 1].to_broadcast([P, HH, P]), ALU.mult
                                            ).then_inc(cross_ready, 1)

            for n in range(14):
                s = n % 2
                if n in (12, 13):
                    if n == 12:
                        v.wait_ge(small_root, 1)
                        v.wait_ge(level_ready, 2 * len(LEVELS))
                    for c in range(TC):
                        v.wait_ge(groups_done, g + 1)
                        nc.vector.tensor_scalar(V[:, c * 512 + s * UC:c * 512 + (s + 1) * UC],
                                                ring[g % RING][:, 0:UC], rcol[:, c:c + 1], float(P) ** -0.5,
                                                ALU.mult, ALU.mult).then_inc(evacuated, 1)
                        g += 1
                        if n == 12 and c in (1, 3):
                            cross_ends(c == 3)
                else:
                    for f in range(2):
                        v.wait_ge(groups_done, g + 1)
                        nc.vector.tensor_tensor(tile(dests[n // 2], 2 * s + f), ring[g % RING][:, :], R[:, :],
                                                ALU.mult).then_inc(evacuated, 1)
                        g += 1
                if n < 4 or n == 12:
                    split_lo(n + 2, s)
                if n == 1:
                    nc.vector.memset(SD[:, :], 0.0).then_inc(scores_cleared, 1)
                if n == 2:
                    v.wait_ge(decay_act, 3)
                    nc.vector.scalar_tensor_tensor(lb_, fk, 0.0, lb_, ALU.min, ALU.subtract).then_inc(decay_vec, 1)
                    v.wait_ge(decay_vec, 1)
                    nc.vector.tensor_tensor(fk, lb_, fk, ALU.subtract).then_inc(decay_vec, 1)
                    v.wait_ge(decay_vec, 2)
                    v.wait_ge(ones_ready, 2)
                    for c in range(HH * TC):
                        b = lb_[:, c * P:(c + 1) * P]
                        nc.vector.tensor_tensor_scan(b, ones[:, :], b, 0.0, ALU.mult, ALU.add
                                                     ).then_inc(decay_vec, 1)
                if 4 <= n <= 11:
                    if n == 4:
                        v.wait_ge(scores_cleared, 1)
                        v.wait_ge(masks_ready, 1)
                    g = take(n - 4, g)
                    split_lo(n + 2, s)
                    if n < 11:
                        level_operand(n - 3)
                if 8 <= n <= 11:
                    v.wait_ge(evacuated, GB["w_in"] + 8 + 6 * (min(n, 9) - 4) + 2)
                    conv_tile(n - 8)

            for h in range(HH):
                for part in range(2):
                    v.wait_ge(groups_done, g + 1)
                    o = (6 * h + 3 * part) * P
                    nc.vector.tensor_copy(SC[:, o:o + 3 * P], ring[g % RING][:, 0:3 * P]).then_inc(evacuated, 1)
                    g += 1
            split_lo(15, 1)
            for k in range(4):
                xg_lo("w_out", k, 4 + k, tile(GBt, k), None)
            v.wait_ge(q_silu, 2)
            for h in range(HH):
                o = tile(CH, h)
                v.wait_ge(groups_done, g + 1)
                nc.vector.tensor_copy(o, ring[h][:, :]).then_inc(evacuated, 1)
                g += 1
                v.wait_ge(evacuated, g)
                nc.vector.tensor_tensor(tile(GC, h), o, o, ALU.mult).then_inc(osq_ready, 1)
                v.wait_ge(osq_ready, h + 1)
                nc.vector.scalar_tensor_tensor(o, o, col("hgrn_norm_g", h), tile(G, h), ALU.mult, ALU.mult
                                               ).then_inc(head_part, 1)
            v.wait_ge(head_part, HH)
            for h in range(HH + 1):
                if h < HH:
                    v.wait_ge(small_root, 2 + h)
                    nc.vector.tensor_tensor(tile(CH, h), tile(CH, h), tile(GC, h), ALU.mult).then_inc(mixa_ready, 1)
                if h:
                    xg_lo("w_out", 3 + h, h - 1, tile(CH, h - 1), None)

            def project(name, ksplit, dst, factor=None, xg=None, gain=None, goff=0, unroll=False):
                nk = len(ksplit)
                for i in steps(v, 2, unroll):
                    for b in range(2):
                        def ahead(j):
                            n = i * (2 * nk) + (UB[name] + b * nk + j + 2)
                            if not (unroll and n >= UNITS):
                                split_lo(n, (b * nk + j) % 2)
                        for j in range(nk - 1):
                            ahead(j)
                        for f in range(2):
                            gr = 2 * b + f
                            t = tile(dst, i * 4 + gr)
                            v.wait_ge(groups_done, i * 4 + (GB[name] + gr + 1))
                            if factor is None:
                                ins = nc.vector.tensor_copy(t, ring[gr][:, :])
                            else:
                                ins = nc.vector.scalar_tensor_tensor(t, ring[gr][:, :], factor, t,
                                                                     ALU.mult, ALU.add)
                            ins.then_inc(evacuated, 1)
                        if xg:
                            for f in range(2):
                                k = i * 4 + (2 * b + f)
                                xg_lo(xg, k, k, tile(dst, k), gain, k + goff)
                        if xg or factor or b == 0:
                            ahead(nk - 1)

            def add_normed(y, gain, first, xg, next_gain):
                def scale_y(k):
                    nc.vector.scalar_tensor_tensor(tile(y, k), tile(y, k), col(gain, k), R[:, :],
                                                   ALU.mult, ALU.mult).then_inc(resid_part, 1)

                scale_y(0)
                for k in range(DT):
                    v.wait_ge(resid_part, first + k + 1)
                    nc.vector.tensor_tensor(tile(xT, k), tile(xT, k), tile(y, k), ALU.add).then_inc(resid_ready, 1)
                    if k + 1 < DT:
                        scale_y(k + 1)
                    xg_lo(xg, k, k, tile(xT, k), next_gain)

            project("w_out", [8], Y0)
            rstd("post_mix")
            add_normed(Y0, "post_mix_g", 0, "up0", "pre_ffn_g")

            def up(m, norm=None, conv=False):
                name = f"up{m}"
                gb, hb = GB[name], FT * m
                def step(i, first):
                    def conv_rest(f, half, dst):
                        n = 2 * half + f
                        u = tile(Ut, f)
                        v.wait_ge(tap_ready, i * 4 + (n + 1))
                        for tap, sh, signal in ((1, 1, conv_part), (0, 2, conv_ready)):
                            if sh == 2:
                                v.wait_ge(conv_part, i * 4 + (n + 1))
                            nc.vector.scalar_tensor_tensor(dst[:, sh:T], u[:, 0:T - sh], tap_col(i, tap, half, f),
                                                           dst[:, sh:T], ALU.mult, ALU.add).then_inc(signal, 1)
                    if first:
                        split_lo(UB[name] + 2, 0)
                        if norm:
                            rstd(norm)
                    for f in range(2):
                        v.wait_ge(groups_done, i * 4 + (gb + f + 1))
                        nc.vector.tensor_tensor(tile(Ut if conv else Tt, f), ring[f][:, :], R[:, :], ALU.mult
                                                ).then_inc(evacuated, 1)
                    if conv:
                        for f in range(2):
                            conv_rest(f, 0, tile(Tt, f))
                    if not first:
                        split_lo(i * 2 + (UB[name] + 2), 0)
                    if conv:
                        v.wait_ge(conv_ready, i * 4 + 2)
                    for f in range(2):
                        v.wait_ge(groups_done, i * 4 + (gb + f + 3))
                        nc.vector.tensor_tensor(tile(Ut if conv else At, f), ring[2 + f][:, :], R[:, :], ALU.mult
                                                ).then_inc(evacuated, 1)
                    for f in range(2):
                        if conv:
                            conv_rest(f, 1, tile(At, f))
                            v.wait_ge(conv_ready, i * 4 + (f + 3))
                        else:
                            v.wait_ge(evacuated, i * 4 + (gb + f + 3))
                        v.wait_ge(silu_ready, i * 2 + (hb + f + 1))
                        nc.vector.tensor_tensor(tile(At, f), tile(At, f), tile(Tt, f), ALU.mult
                                                ).then_inc(gated_ready, 1)
                    for f in range(2):
                        v.wait_ge(ahi_ready, i * 2 + (hb + f + 1))
                        nc.vector.tensor_tensor(tile(alo, i * 2 + f), tile(At, f),
                                                tile(ahi, i * 2 + f).bitcast(F32), ALU.subtract
                                                ).then_inc(act_ready, 1)
                    v.wait_ge(act_ready, i * 2 + (hb + 2))
                    if not conv:
                        split_lo(i * 2 + (UB[name] + 3), 1)

                step(0, True)
                with v.Fori(1, FT // 2) as i:
                    step(i, False)

            up(0, "pre_ffn", conv=True)
            project("down0", DOWN, Y1)
            rstd("post_ffn")
            add_normed(Y1, "post_ffn_g", DT, "up1", "ffn_pre_norm_2")
            up(1, "pre0")
            project("down1", DOWN, xT, 0.5, "pool", "mix_norm_2")
            pool_steps = [0]

            def pool_do(ins):
                ins.then_inc(pool_step, 1)
                pool_steps[0] += 1

            def take(n):
                k = 2 * POOL_ORDER[n // 2] + n % 2
                v.wait_ge(groups_done, GB["pool"] + n + 1)
                nc.vector.tensor_tensor(PU[:, k * PW + 16:(k + 1) * PW], ring[n % RING][:, :], R[:, :], ALU.mult
                                        ).then_inc(evacuated, 1)

            def windows(w):
                for step in range(w + 1):
                    if pool_steps[0]:
                        v.wait_ge(pool_step, pool_steps[0])
                    pool_do(window_step(nc.vector, w, step))

            def add_mixed(w, pos):
                u, cur = window(w, -1), window(w, w)
                edge = edges[:, w * 32:(w + 1) * 32].rearrange("p (k t) -> p k t", k=2)
                count = inv[:, w * 16:(w + 1) * 16].rearrange("p (k t) -> p k t", k=1).to_broadcast([P, 2, 16])
                if w < 2:
                    v.wait_ge(pool_step, pool_steps[0])
                pool_do(nc.vector.tensor_tensor(edge, cur[:, :, 16:32], count, ALU.mult))
                v.wait_ge(pool_step, pool_steps[0])
                pool_do(nc.vector.scalar_tensor_tensor(cur[:, :, 16:PW], cur[:, :, 16:PW], 0.5 ** (w + 1),
                                                       u[:, :, 16:PW], ALU.mult, ALU.subtract))
                v.wait_ge(pool_step, pool_steps[0])
                pool_do(nc.vector.tensor_tensor(cur[:, :, 16:32], edge, u[:, :, 16:32], ALU.subtract))
                v.wait_ge(pool_step, pool_steps[0])
                for kt in range(2):
                    k = 2 * w + kt
                    nc.vector.scalar_tensor_tensor(tile(xT, k), cur[:, kt, 16:PW], col("pool_scale_2", k), tile(xT, k),
                                                   ALU.mult, ALU.add).then_inc(mixed_ready, 1)

            def mixed_lo(pos):
                for p_ in (pos, pos + 1):
                    k = MIXED_ORDER[p_]
                    v.wait_ge(mixed_ready, p_ + 1)
                    xg_lo("up2", p_, k, tile(xT, k), "ffn_post_norm_2")

            v.wait_ge(pads_ready, 2)
            v.wait_ge(inv_loaded, 16)
            rstd("mix0")
            for n in range(4):
                take(n)
            v.wait_ge(evacuated, GB["pool"] + 4)
            windows(0)
            add_mixed(0, 0)
            for n in range(4, 8):
                take(n)
            split_lo(UB["pool"] + 2, 0)
            mixed_lo(0)
            v.wait_ge(evacuated, GB["pool"] + 8)
            windows(1)
            add_mixed(1, 2)
            mixed_lo(2)
            v.wait_ge(far_step, 4)
            add_mixed(3, 4)
            mixed_lo(4)
            v.wait_ge(far_step, 7)
            add_mixed(2, 6)
            mixed_lo(6)
            up(2, "post0")
            project("down2", DOWN, xT, 0.5, "kv", "kv_in_norm_2")
            rstd("kv_pre1")
            g = GB["kv"]
            ck, krope = Ut[:, 0:T], Ut[:, T:2 * T]
            k0, k1 = kvt[:, 0:T], kvt[:, T:2 * T]
            v.wait_ge(groups_done, g + 2)
            nc.vector.tensor_tensor(ck, ring[0][:, :], R[:, :], ALU.mult).then_inc(evacuated, 2)
            split_lo(UB["kv"] + 2, 0)
            v.wait_ge(evacuated, g + 2)
            v.wait_ge(groups_done, g + 4)
            nc.vector.tensor_tensor(krope, ring[1][:, :], R[:, :], ALU.mult).then_inc(evacuated, 2)
            nc.vector.tensor_tensor(k0, ck, ck, ALU.mult).then_inc(small_step, 1)
            for k in range(DT):
                xg_lo("up3", k, k, tile(xT, k), "ffn_pre_norm_2", 8 + k)
            split_lo(UB["kv"] + 3, 1)
            v.wait_ge(rope_kv_loaded, 16)
            v.wait_ge(key_turned, 1)
            nc.vector.tensor_tensor(k0, banks[7][:, :], rope_kv[:, T:2 * T], ALU.mult).then_inc(ck_ready, 1)
            nc.vector.tensor_tensor(krope, krope, rope_kv[:, 0:T], ALU.mult).then_inc(ck_ready, 1)
            v.wait_ge(ck_ready, 2)
            nc.vector.tensor_tensor(krope, krope, k0, ALU.add).then_inc(ck_ready, 1)
            v.wait_ge(small_root, 6)
            nc.vector.scalar_tensor_tensor(ck, ck, col("ckv_norm_2", 0), k1, ALU.mult, ALU.mult).then_inc(ck_ready, 1)
            up(3)
            project("down3", DOWN, xT, 0.5, "dq", "mix_norm_2", 8)
            v.wait_ge(groups_done, GB["dq"])
            nc.vector.memset(Tt[64:128, 0:T], 0.0)
            nc.vector.memset(Tt[0:64, T:2 * T], 0.0).then_inc(outlo_ready, 1)
            v.wait_ge(ck_ready, 4)
            nc.vector.tensor_copy(Tt[0:64, 0:T], Ut[0:64, T:2 * T])
            nc.vector.tensor_copy(Tt[64:128, T:2 * T], Ut[64:128, T:2 * T]).then_inc(latent_ready, 1)

            def latent_lo(j):
                v.wait_ge(latent_hi, j + 1)
                hi = ckhi[:, :] if j == 0 else tile(cqhi, j - 1)
                lo = cklo[:, :] if j == 0 else tile(cqlo, j - 1)
                src = Ut[:, 0:T] if j == 0 else tile(At, j - 1)
                nc.vector.tensor_tensor(lo, src, hi.bitcast(F32), ALU.subtract).then_inc(latent_split, 1)

            rstd("mix1")
            g = GB["dq"]
            for u in range(2):
                v.wait_ge(groups_done, g + (1, 4)[u])
                nc.vector.tensor_tensor(tile(At, u), ring[u][:, :], R[:, :], ALU.mult).then_inc(evacuated, (1, 3)[u])
                v.wait_ge(evacuated, g + (1, 4)[u])
                nc.vector.tensor_tensor(tile(PT, u), tile(At, u), tile(At, u), ALU.mult).then_inc(small_step, 1)
                if u == 0:
                    latent_lo(0)
            split_lo(UB["dq"] + 2, 0)
            r = tile(PT, 0)
            v.wait_ge(small_root, 7)
            for u in range(2):
                nc.vector.scalar_tensor_tensor(tile(At, u), tile(At, u), col("q_lora_norm_2", u), r,
                                               ALU.mult, ALU.mult).then_inc(latent_ready, 1)
            for j in range(1, 1 + QR):
                latent_lo(j)

            scale = float((NOPE + ROPE) ** -0.5)
            v.wait_ge(rope_q_loaded, 16)
            gb = GB["attn"]
            with v.Fori(0, QUARTERS) as q:
                def take(n, dst):
                    v.wait_ge(groups_done, q * 16 + (gb + n + 1))
                    nc.vector.tensor_copy(dst, ring[n % RING][:, :]).then_inc(evacuated, 1)

                for n in range(8):
                    take(n, tile((KN, VV)[n // 4], n % 4))
                for j in range(2):
                    take(8 + j, tile(QRr, j))
                for j in range(2):
                    v.wait_ge(evacuated, q * 16 + (gb + 9 + j))
                    nc.vector.tensor_tensor(tile(QRt, j), tile(QRr, j), rope_q[:, 0:T], ALU.mult
                                            ).then_inc(qrope_part, 1)
                for j in range(2):
                    take(10 + j, tile(QN, j))
                for j in range(2):
                    v.wait_ge(groups_done, q * 16 + (gb + 13 + j))
                    v.wait_ge(qrope_part, q * 2 + (j + 1))
                    nc.vector.tensor_tensor(tile(QRr, j), ring[j][:, :], rope_q[:, T:2 * T], ALU.mult
                                            ).then_inc(evacuated, 1)
                    v.wait_ge(evacuated, q * 16 + (gb + 13 + j))
                    nc.vector.tensor_tensor(tile(QRt, j), tile(QRt, j), tile(QRr, j), ALU.add
                                            ).then_inc(qrope_ready, 1)
                for j in range(2):
                    take(14 + j, tile(QN, 2 + j))

                def maxes(h):
                    for i in range(TC):
                        e, c = 4 * h + i, 4 * (h % 2) + i
                        v.wait_ge(scores_ready, q * 16 + (e + 1))
                        nc.vector.tensor_reduce(rowmax[:, c:c + 1], ring[i][:, 0:(i + 1) * P], AX_X, ALU.max
                                                ).then_inc(max_part, 1)
                        v.wait_ge(max_part, q * 16 + (e + 1))
                        nc.vector.tensor_scalar(negmax[:, c:c + 1], rowmax[:, c:c + 1], -scale, None, ALU.mult
                                                ).then_inc(negmax_ready, 1)

                def normalise(h):
                    c0 = 4 * (h % 2)
                    v.wait_ge(exp_ready, q * 16 + (4 * h + 4))
                    nc.vector.reciprocal(rowinv[:, c0:c0 + 4], rowsum[:, c0:c0 + 4]).then_inc(recip_ready, 1)
                    v.wait_ge(recip_ready, q * 4 + (h + 1))
                    for i in range(TC):
                        off = i * (i + 1) // 2 * P
                        pr = probs(h)[:, off:off + (i + 1) * P]
                        nc.vector.tensor_scalar(pr, pr, rowinv[:, c0 + i:c0 + i + 1], None, ALU.mult
                                                ).then_inc(probs_ready, 1)

                maxes(0)
                normalise(0)
                for h in range(4):
                    if h < 3:
                        maxes(h + 1)
                    if h < 3:
                        v.wait_ge(turned_ready, q * 12 + (3 * h + 1))
                        nc.vector.tensor_copy(PT[:, 0:4 * P], banks[4][:, 0:4 * P]).then_inc(turned_vec, 1)
                    else:
                        v.wait_ge(turned_ready, q * 12 + (3 * h + 2))
                        nc.vector.tensor_copy(PT[:, 4 * P:7 * P], banks[5][:, 0:3 * P]).then_inc(turned_vec, 1)
                    if h < 3:
                        normalise(h + 1)
                    v.wait_ge(outhi_ready, q * 4 + (h + 1))
                    nc.vector.tensor_tensor(tile(oTlo, q * 4 + h), banks[7][:, :],
                                            tile(oThi, q * 4 + h).bitcast(F32), ALU.subtract
                                            ).then_inc(outlo_ready, 1)
            project("w_o", [8, 8], xT, 1.0, "up4", "ffn_post_norm_2", 8)
            up(4, "post1")
            project("down4", DOWN, xT, 0.5, unroll=True)
            rstd("final")
            for k in range(DT):
                nc.vector.scalar_tensor_tensor(tile(Z, k), tile(xT, k), col("final_norm_2", k), R[:, :],
                                               ALU.mult, ALU.mult).then_inc(normed_out, 1)
            g = GB["x_out"]
            for n in range(2 * TC):
                v.wait_ge(groups_done, g + n + 1)
                nc.vector.tensor_copy(ob[:, n * T:(n + 1) * T], ring[n % RING][:, :]).then_inc(evacuated, 1)


def constants():
    import numpy as np

    s, t = np.arange(P)[:, None], np.arange(P)[None, :]
    masks = [s == t]
    for h in LEVELS:
        masks.append((s // (2 * h) == t // (2 * h)) & (s % (2 * h) < h) & (t % (2 * h) >= h))
    perm = np.zeros((P, P), np.float32)
    for m in range(P):
        if m % ROPE < ROPE // 2:
            perm[m + ROPE // 2, m] = -1.0
        else:
            perm[m - ROPE // 2, m] = 1.0
    freq = np.float32(10000.0) ** (-np.arange(0, ROPE, 2, dtype=np.float32) / np.float32(ROPE))
    ang = (np.arange(T, dtype=np.float32)[None, :] * freq[:, None]).astype(np.float32)
    rope = np.concatenate([np.tile(np.cos(ang), (4, 1)), np.tile(np.sin(ang), (4, 1))], 1).astype(np.float32)
    count = np.stack([1.0 / np.minimum(np.arange(1, 17), w) for w in (2, 4, 8, 16)])
    return {
        "ident": np.eye(P, dtype=np.float32), "perm": perm,
        "causal": np.where(t <= s, 0.0, -1e30).astype(np.float32),
        "masks": np.concatenate([m.astype(np.int32) for m in masks], 1),
        "rope": rope, "inv_count": count.astype(np.float32).reshape(1, 4 * 16),
    }


_INS = ["x", "lb_param", "w_in", "w_out", "conv_w", "ffn_w_up", "ffn_conv_w", "ffn_w_down", "hgrn_norm_g",
        "pre_mix_g", "post_mix_g", "pre_ffn_g", "post_ffn_g", "ffn_pre_norm_2", "ffn_pre_wg_2", "ffn_pre_wu_2",
        "ffn_pre_wd_2", "mix_norm_2", "ffn_post_norm_2", "ffn_post_wg_2", "ffn_post_wu_2", "ffn_post_wd_2",
        "pool_w_2", "pool_scale_2", "kv_in_norm_2", "w_dkv_2", "ckv_norm_2", "w_uk_2", "w_uv_2",
        "q_lora_norm_2", "w_dq_2", "w_uq_2", "w_o_2", "final_norm_2"]


def kernel(**inputs):
    import numpy as _np
    import concourse.bacc as _bacc
    from concourse import mybir as _mybir
    from concourse.bass_utils import run_bass_kernel_spmd as _run

    nc = _bacc.Bacc("TRN2", target_bir_lowering=False, num_devices=1)
    arrays, args = {}, {}
    given = {name: inputs[name] for name in _INS}
    given.update(constants())
    for name, value in given.items():
        a = _np.ascontiguousarray(value)
        arrays[f"in_{name}_dram"] = a
        args[name] = nc.dram_tensor(f"in_{name}_dram", a.shape, _mybir.dt.from_np(a.dtype),
                                    kind="ExternalInput").ap()
    out = nc.dram_tensor("out_0_dram", (1, T, D), _mybir.dt.float32, kind="ExternalOutput").ap()
    build(nc, args, out)
    r = _run(nc, [arrays], core_ids=[0])
    return r.results[0]["out_0_dram"]
```
